# Optimizing a Trainium2 kernel written in Bass

```python
import jax, jax.numpy as jnp
from jax import lax
import numpy as np

D_MODEL = 1024
BATCH = 1
SEQ = 512
DEPTH = 1

HEAD_DIM = D_MODEL // 16
N_FOX_HEADS = 4
N_DIL_HEADS = 4
N_CONV_GROUPS = 4
N_POOL_GROUPS = 4
D_FOX = N_FOX_HEADS * HEAD_DIM
D_DIL = N_DIL_HEADS * HEAD_DIM
D_CONV = N_CONV_GROUPS * HEAD_DIM
D_POOL = N_POOL_GROUPS * HEAD_DIM
D_MIX = D_FOX + D_DIL + D_CONV + D_POOL
POOL_GROUP = D_POOL // N_POOL_GROUPS
IN_SIZES = (D_FOX, D_FOX, D_FOX, D_DIL, D_DIL, D_DIL, D_CONV, D_CONV, D_CONV, D_POOL, N_FOX_HEADS)
D_IN = sum(IN_SIZES)
Q_BLOCK = 128
DILATION_PATTERNS = ((128, 1), (512, 4), (2048, 16))
CONV_WIDTH = 3
POOL_WINDOWS = (2, 4, 8, 16)
N_EXPERTS = 16
N_EXPERT_GROUPS = 4
EXPERTS_PER_GROUP = N_EXPERTS // N_EXPERT_GROUPS
TOP_K = 2
D_EXPERT = D_MODEL // 2
ALPHA = (2 * DEPTH) ** 0.25
BETA = (8 * DEPTH) ** -0.25
LN_EPS = 1e-5

kernel_name = 'hybrid_fox_dilated_conv_pool_grouped_moe'

def layer_norm(x, g, b):
    xf = x.astype(jnp.float32)
    mu = jnp.mean(xf, axis=-1, keepdims=True)
    var = jnp.mean(jnp.square(xf - mu), axis=-1, keepdims=True)
    y = (xf - mu) * lax.rsqrt(var + LN_EPS) * g.astype(jnp.float32) + b.astype(jnp.float32)
    return y.astype(x.dtype)

def to_heads(t, n_heads):
    b, s, _ = t.shape
    return t.reshape(b, s, n_heads, HEAD_DIM).transpose(0, 2, 1, 3)

def from_heads(t):
    b, h, s, d = t.shape
    return t.transpose(0, 2, 1, 3).reshape(b, s, h * d)

def forgetting_attention(q, k, v, log_f):
    B, H, S, D = q.shape
    nb = S // Q_BLOCK
    c = jnp.cumsum(log_f, axis=-1)
    qb = q.reshape(B, H, nb, Q_BLOCK, D).transpose(2, 0, 1, 3, 4)
    cqb = c.reshape(B, H, nb, Q_BLOCK).transpose(2, 0, 1, 3)
    kpos = jnp.arange(S)
    scale = D ** -0.5

    def block(args):
        qi, ci, bi = args
        s = jnp.einsum('bhqd,bhkd->bhqk', qi, k).astype(jnp.float32) * scale
        s = s + (ci[..., :, None] - c[..., None, :])
        qpos = bi * Q_BLOCK + jnp.arange(Q_BLOCK)
        s = jnp.where(kpos[None, :] <= qpos[:, None], s, -jnp.inf)
        p = jax.nn.softmax(s, axis=-1)
        return jnp.einsum('bhqk,bhkd->bhqd', p.astype(v.dtype), v)

    out = lax.map(block, (qb, cqb, jnp.arange(nb)))
    return out.transpose(1, 2, 0, 3, 4).reshape(B, H, S, D)

def banded_window_attention(q, k, v, window):
    B, G, L, D = q.shape
    nb = -(-L // Q_BLOCK)
    Lp = nb * Q_BLOCK
    pad_end = ((0, 0), (0, 0), (0, Lp - L), (0, 0))
    pad_front = ((0, 0), (0, 0), (Q_BLOCK, 0), (0, 0))
    q = jnp.pad(q, pad_end)
    kp = jnp.pad(jnp.pad(k, pad_end), pad_front)
    vp = jnp.pad(jnp.pad(v, pad_end), pad_front)

    def banded(t):
        prev = t[:, :, :Lp].reshape(B, G, nb, Q_BLOCK, D)
        cur = t[:, :, Q_BLOCK:].reshape(B, G, nb, Q_BLOCK, D)
        return jnp.concatenate([prev, cur], axis=3)

    kb, vb = banded(kp), banded(vp)
    qb = q.reshape(B, G, nb, Q_BLOCK, D)
    s = jnp.einsum('bgnqd,bgnkd->bgnqk', qb, kb).astype(jnp.float32) * (D ** -0.5)
    qpos = jnp.arange(nb)[:, None] * Q_BLOCK + jnp.arange(Q_BLOCK)[None, :]
    kpos = jnp.arange(nb)[:, None] * Q_BLOCK - Q_BLOCK + jnp.arange(2 * Q_BLOCK)[None, :]
    dist = qpos[:, :, None] - kpos[:, None, :]
    valid = (dist >= 0) & (dist <= window) & (kpos[:, None, :] >= 0)
    s = jnp.where(valid, s, -jnp.inf)
    lse = jax.nn.logsumexp(s, axis=-1, keepdims=True)
    p = jnp.exp(s - lse)
    o = jnp.einsum('bgnqk,bgnkd->bgnqd', p.astype(v.dtype), vb)
    return o.reshape(B, G, Lp, D)[:, :, :L], lse[..., 0].reshape(B, G, Lp)[:, :, :L]

def dilated_attention(q, k, v):
    B, H, S, D = q.shape
    outs, lses = [], []
    for w, r in DILATION_PATTERNS:
        L = S // r

        def split(t):
            return t.reshape(B, H, L, r, D).transpose(0, 1, 3, 2, 4).reshape(B, H * r, L, D)

        o, lse = banded_window_attention(split(q), split(k), split(v), w // r)
        outs.append(o.reshape(B, H, r, L, D).transpose(0, 1, 3, 2, 4).reshape(B, H, S, D))
        lses.append(lse.reshape(B, H, r, L).transpose(0, 1, 3, 2).reshape(B, H, S))
    wts = jax.nn.softmax(jnp.stack(lses), axis=0)
    return jnp.einsum('pbhs,pbhsd->bhsd', wts.astype(q.dtype), jnp.stack(outs))

def short_conv_mixer(b_gate, c_gate, h, conv_w):
    u = c_gate * h
    y = lax.conv_general_dilated(u, conv_w[:, None, :], window_strides=(1,),
                                 padding=((CONV_WIDTH - 1, 0),),
                                 dimension_numbers=('NWC', 'WIO', 'NWC'),
                                 feature_group_count=u.shape[-1])
    return b_gate * y

def multiscale_pool_mixer(u, pool_w, pool_scale):
    B, S, C = u.shape
    uf = u.astype(jnp.float32)
    cs0 = jnp.pad(jnp.cumsum(uf, axis=1), ((0, 0), (1, 0), (0, 0)))
    t = jnp.arange(S)
    groups = []
    for gi, w in enumerate(POOL_WINDOWS):
        sl = slice(gi * POOL_GROUP, (gi + 1) * POOL_GROUP)
        c = cs0[:, :, sl]
        lagged = jnp.pad(c, ((0, 0), (w - 1, 0), (0, 0)))[:, :S]
        count = jnp.minimum(t + 1, w).astype(jnp.float32)[None, :, None]
        groups.append((c[:, 1:] - lagged) / count - uf[:, :, sl])
    p = jnp.stack(groups, axis=2).astype(u.dtype)
    y = jnp.einsum('bsgc,gcd->bsgd', p, pool_w).reshape(B, S, C)
    return y * pool_scale

def route(x2, w_router, router_bias):
    T = x2.shape[0]
    s = jax.nn.sigmoid((x2 @ w_router).astype(jnp.float32))
    sel = s + router_bias.astype(jnp.float32)
    grp = sel.reshape(T, N_EXPERT_GROUPS, EXPERTS_PER_GROUP)
    grp_score = jnp.sum(lax.top_k(grp, TOP_K)[0], axis=-1)
    best = jnp.argmax(grp_score, axis=-1)
    in_group = (jnp.arange(N_EXPERTS) // EXPERTS_PER_GROUP)[None, :] == best[:, None]
    _, idx = lax.top_k(jnp.where(in_group, sel, -jnp.inf), TOP_K)
    gate = jnp.take_along_axis(s, idx, axis=-1)
    gate = gate / jnp.sum(gate, axis=-1, keepdims=True)
    return jnp.sum(jax.nn.one_hot(idx, N_EXPERTS, dtype=jnp.float32) * gate[..., None], axis=1)

def moe_ffn(x, comb, w_gate, w_up, w_down):
    B, S, D = x.shape
    x2 = x.reshape(-1, D)
    out = jnp.zeros(x2.shape, jnp.float32)
    for e in range(N_EXPERTS):
        h = jax.nn.silu(x2 @ w_gate[e]) * (x2 @ w_up[e])
        out = out + comb[:, e:e + 1] * (h @ w_down[e]).astype(jnp.float32)
    return out.astype(x.dtype).reshape(B, S, D)

def setup_inputs(seed: int = 0) -> dict:
    key = jax.random.key(seed)
    ks = jax.random.split(key, 17)
    f32 = jnp.float32
    nrm = lambda k, shape: jax.random.normal(k, shape, f32)
    return {
        'x': nrm(ks[0], (BATCH, SEQ, D_MODEL)),
        'w_in': nrm(ks[1], (DEPTH, D_MODEL, D_IN)) * D_MODEL ** -0.5,
        'b_f': 2.0 + 0.1 * nrm(ks[2], (DEPTH, N_FOX_HEADS)),
        'conv_w': nrm(ks[3], (DEPTH, CONV_WIDTH, D_CONV)) * CONV_WIDTH ** -0.5,
        'pool_w': nrm(ks[4], (DEPTH, N_POOL_GROUPS, POOL_GROUP, POOL_GROUP)) * POOL_GROUP ** -0.5,
        'pool_scale': 1.0 + 0.02 * nrm(ks[5], (DEPTH, D_POOL)),
        'w_o': nrm(ks[6], (DEPTH, D_MIX, D_MODEL)) * (D_MIX ** -0.5 * BETA),
        'ln1_g': 1.0 + 0.02 * nrm(ks[7], (DEPTH, D_MODEL)),
        'ln1_b': 0.02 * nrm(ks[8], (DEPTH, D_MODEL)),
        'w_router': nrm(ks[9], (D_MODEL, N_EXPERTS)) * D_MODEL ** -0.5,
        'router_bias': 0.01 * nrm(ks[10], (N_EXPERTS,)),
        'w_gate': nrm(ks[11], (DEPTH, N_EXPERTS, D_MODEL, D_EXPERT)) * D_MODEL ** -0.5,
        'w_up': nrm(ks[12], (DEPTH, N_EXPERTS, D_MODEL, D_EXPERT)) * D_MODEL ** -0.5,
        'w_down': nrm(ks[13], (DEPTH, N_EXPERTS, D_EXPERT, D_MODEL)) * (D_EXPERT ** -0.5 * BETA),
        'ln2_g': 1.0 + 0.02 * nrm(ks[14], (DEPTH, D_MODEL)),
        'ln2_b': 0.02 * nrm(ks[15], (DEPTH, D_MODEL)),
    }

def reference(x, w_in, b_f, conv_w, pool_w, pool_scale, w_o, ln1_g, ln1_b,
              w_router, router_bias, w_gate, w_up, w_down, ln2_g, ln2_b):
    B, S, D = x.shape
    offsets = [int(o) for o in np.cumsum(IN_SIZES)[:-1]]
    for l in range(DEPTH):
        proj = x @ w_in[l]
        fq, fk, fv, dq, dk, dv, cb, cc, ch, pu, fl = jnp.split(proj, offsets, axis=-1)
        log_f = jax.nn.log_sigmoid((fl + b_f[l]).astype(jnp.float32)).transpose(0, 2, 1)
        ya = from_heads(forgetting_attention(to_heads(fq, N_FOX_HEADS), to_heads(fk, N_FOX_HEADS),
                                             to_heads(fv, N_FOX_HEADS), log_f))
        yb = from_heads(dilated_attention(to_heads(dq, N_DIL_HEADS), to_heads(dk, N_DIL_HEADS),
                                          to_heads(dv, N_DIL_HEADS)))
        yc = short_conv_mixer(cb, cc, ch, conv_w[l])
        yd = multiscale_pool_mixer(pu, pool_w[l], pool_scale[l])
        mix = jnp.concatenate([ya, yb, yc, yd], axis=-1) @ w_o[l]
        x = layer_norm(ALPHA * x + mix, ln1_g[l], ln1_b[l])
        comb = route(x.reshape(-1, D), w_router, router_bias)
        x = layer_norm(ALPHA * x + moe_ffn(x, comb, w_gate[l], w_up[l], w_down[l]), ln2_g[l], ln2_b[l])
    return x


_drawn_inputs = setup_inputs


def setup_inputs(seed=0):
    import zlib

    import numpy as np

    out = dict(_drawn_inputs(seed))
    spreads = {}
    factors = {'b_f': 26.32, 'pool_scale': 4.196, 'ln2_g': 8.275, 'ln2_b': 8.237}
    for name, (base, spread) in spreads.items():
        noise = np.random.default_rng([zlib.crc32(name.encode()), seed]).standard_normal(out[name].shape)
        drawn = base * np.exp(spread * noise) if base else spread * noise
        out[name] = __import__('jax').numpy.asarray(drawn.astype(out[name].dtype))
    for name, factor in factors.items():
        out[name] = (out[name] * factor).astype(out[name].dtype)
    return out
```

```python
from contextlib import ExitStack

import numpy as np
import concourse.bass as bass
from concourse import mybir

F32 = mybir.dt.float32
BF16 = mybir.dt.bfloat16
I32 = mybir.dt.int32
U32 = mybir.dt.uint32
ALU = mybir.AluOpType
ACT = mybir.ActivationFunctionType
AX = mybir.AxisListType

P = 128
S = 512
D = 1024
NT = S // P
NC = D // P
HD = D // 16
GW = 4 * HD
NH = 8
E = 16
EG = 4
F = D // 2
NF = F // P
CAP = 96
CHUNKS = -(-S // CAP)
EROWS = CHUNKS * CAP
MAIN = E * CAP
MORE = EROWS - CAP
PATTERNS = ((128, 1), (512, 4), (2048, 16))
WINDOWS = (2, 4, 8, 16)
ALPHA = 2.0 ** 0.25
EPS = 1e-5
NEG = -1e30
SPLIT = 640
OFF = [P * (i * (i + 1) // 2) for i in range(NT)]
PROBS = P * (NT * (NT + 1) // 2)

BLOCKS = ["fq", "fk", "fv", "dq", "dk", "dv", "pu", "cc", "ch", "cb"]
BLOCK_COL = dict(fq=0, fk=1, fv=2, dq=3, dk=4, dv=5, cb=6, cc=7, ch=8, pu=9)
NSLOT = 6
UNITS0 = [("fq", 0), ("fq", 1), ("fk", 0), ("fk", 1), ("fv", 0), ("fv", 1)]
FILL = [[("dq", 0), ("dq", 1)], [("dk", 0), ("dk", 1)], [("dv", 0), ("dv", 1)], [("pu", 0), ("pu", 1)],
        [("cc", 0), ("ch", 0)], [("cb", 0), ("cc", 1)], [("ch", 1), ("cb", 1)], []]
UNITS = UNITS0 + [u for f in FILL for u in f] + [("pool", 0), ("pool", 1)]
NX = 2 * NT
ON_DVE = ("fv", "dv", "ch", "cb")


def unit_engine(n):
    if n < NX:
        return "dve" if n % 2 else "act"
    return "dve" if UNITS[n - NX][0] in ON_DVE else "act"


def unit_count(n):
    return sum(unit_engine(m) == unit_engine(n) for m in range(n + 1))


def unit_no(u):
    return NX + UNITS.index(u)


C_IDENT = 0
C_TRI = C_IDENT + P
C_DIL = C_TRI + P
C_UP = C_DIL + S
C_POOL = C_UP + S
C_LOW = C_POOL + 34
C_ROW = C_LOW + 16
C_TOK = C_ROW + 2 * E
NCONST = C_TOK + 1 + NT


def constants():
    c = np.zeros((P, NCONST), np.float32)
    q, k = np.arange(P)[:, None], np.arange(P)[None, :]
    c[:, C_IDENT:C_IDENT + P] = q == k
    c[:, C_TRI:C_TRI + P] = np.where(k <= q, 0.0, NEG)
    for b in range(NT):
        dist = q + P * (NT - 1 - b) - k
        n = sum(((dist >= 0) & (dist % r == 0) & (dist // r <= w // r)).astype(np.int64) for w, r in PATTERNS)
        c[:, C_DIL + P * b:C_DIL + P * (b + 1)] = np.where(n > 0, np.log(np.maximum(n, 1)), NEG)
    c[:, C_UP:C_UP + S] = np.arange(S)[None, :] >= q
    for t in range(2):
        for half in range(2):
            w = WINDOWS[2 * t + half]
            rows = slice(64 * half, 64 * half + 64)
            c[rows, C_POOL + 16 * t:C_POOL + 16 * t + 16] = 1.0 / np.minimum(np.arange(16) + 1, w)
            c[rows, C_POOL + 32 + t] = 1.0 / w
    c[:, C_LOW:C_LOW + 16] = (np.arange(4)[None, :] < np.arange(4)[:, None]).reshape(1, 16)
    c[:, C_ROW:C_ROW + E] = CAP * np.arange(E)
    c[:, C_ROW + E:C_ROW + 2 * E] = MAIN - CAP + (MORE - CAP) * np.arange(E)
    c[:, C_TOK] = np.arange(P)
    c[:, C_TOK + 1:C_TOK + 1 + NT] = P * np.arange(NT)
    selectors = np.repeat(np.eye(4, dtype=np.float32), P, axis=1)
    return c, selectors, np.broadcast_to(np.arange(EROWS, dtype=np.float32), (P, EROWS)).copy()


def build(nc, x, w_in, b_f, conv_w, pool_w, pool_scale, w_o, ln1_g, ln1_b, w_router, router_bias,
          w_gate, w_up, w_down, ln2_g, ln2_b, consts, selectors, slot_numbers, out):
    x1_rows = nc.dram_tensor("x1_rows", [S, D], F32, kind="Internal").ap()
    y_rows = nc.dram_tensor("y_rows", [E * EROWS, D], F32, kind="Internal").ap()

    x_v = x.rearrange("a (t p) d -> (a t) p d", p=P)
    out_v = out.rearrange("a (t p) d -> (a t) p d", p=P)
    w_in_v = w_in.rearrange("l (c p) n -> p (l c) n", p=P)
    w_o_v = w_o.rearrange("l (c p) n -> p (l c) n", p=P)
    w_gate_v = w_gate.rearrange("l e (p c) n -> (l e) p (c n)", c=NC)
    w_up_v = w_up.rearrange("l e (p c) n -> (l e) p (c n)", c=NC)
    w_down_v = w_down.rearrange("l e (c p) n -> (l e) p c n", p=P)
    w_router_v = w_router.rearrange("(p c) n -> p c n", c=NC)
    x1_rows_v = x1_rows.rearrange("(t p) d -> t p d", p=P)

    with ExitStack() as ctx:
        def sb(name, shape, dt=F32):
            return ctx.enter_context(nc.sbuf_tensor(name, shape, dt))

        def sem(name):
            return ctx.enter_context(nc.semaphore(name))

        WREG = NC * F
        wbuf = sb("wbuf", [P, 6 * WREG])
        x_sb = sb("x_sb", [P, NT, D])
        ln_gb = sb("ln_gb", [P, 2, D])
        heads_region = sb("heads_region", [P, NH * S])
        v_region = sb("v_region", [P, 2 * NT * GW])
        probs_region = sb("probs_region", [P, 4 * PROBS])
        cbc_region = sb("cbc_region", [P, 2 * S])
        mix_region = sb("mix_region", [P, NC * S])
        local_region = sb("local_region", [P, 2082])
        osb_region = sb("osb_region", [P, 2 * NT * P])
        cst = sb("cst", [P, NCONST])
        small = sb("small", [P, 1428])

        gate_w = [wbuf[:, 3 * b * WREG:(3 * b + 1) * WREG].rearrange("p (c n) -> p c n", c=NC) for b in range(2)]
        up_w = [wbuf[:, (3 * b + 1) * WREG:(3 * b + 2) * WREG].rearrange("p (c n) -> p c n", c=NC) for b in range(2)]
        down_w = [wbuf[:, (3 * b + 2) * WREG:(3 * b + 3) * WREG].rearrange("p (c n) -> p c n", c=NF)
                  for b in range(2)]
        in_w = [wbuf[:, s * NC * GW:(s + 1) * NC * GW].rearrange("p (c n) -> p c n", c=NC) for s in range(NSLOT)]
        o_w = wbuf[:, 3 * WREG:5 * WREG].rearrange("p (c n) -> p c n", c=NC)
        xT = wbuf[:, 5 * WREG:6 * WREG].rearrange("p (c s) -> p c s", c=NC)

        qkT = heads_region[:, :].rearrange("p (m s) -> p m s", m=NH)
        v_sb = v_region[:, :].rearrange("p (g t n) -> p g t n", g=2, t=NT)
        probs = [probs_region[:, b * PROBS:(b + 1) * PROBS] for b in range(2)]
        probsT = [probs_region[:, (2 + b) * PROBS:(3 + b) * PROBS] for b in range(2)]
        cbc = [cbc_region[:, b * S:(b + 1) * S] for b in range(2)]
        mixT = mix_region[:, :].rearrange("p (c s) -> p c s", c=NC)
        osb = [osb_region[:, b * NT * P:(b + 1) * NT * P].rearrange("p (t n) -> p t n", t=NT) for b in range(2)]
        conv_c = local_region[:, 0:512]
        conv_u = local_region[:, 512:512 + 514]
        pool_u = [local_region[:, 1026 + 528 * c:1554 + 528 * c] for c in range(2)]
        pool_a, pool_b = ln_gb[:, 0, 0:528], ln_gb[:, 1, 0:528]
        cT = mix_region[0:4, 2 * S:3 * S]
        select_head = mix_region[0:4, 3 * S:4 * S]

        x1p = heads_region[:, :].rearrange("p (t c q) -> p t c q", t=NT, c=NC)
        x1T = probs_region[:, 0:NC * S].rearrange("p (c s) -> p c s", c=NC)
        xg = [v_region[:, b * D:(b + 1) * D] for b in range(2)]
        xgT = local_region[:, 0:NC * CAP].rearrange("p (c s) -> p c s", c=NC)
        act_g = local_region[:, 768:768 + NF * CAP]
        hT = local_region[:, 1152:1152 + NF * CAP]
        y_sb = [mix_region[:, b * D:(b + 1) * D] for b in range(2)]
        onehot = [osb_region[:, b * 2 * CAP:(b + 1) * 2 * CAP].bitcast(BF16).rearrange("p (t s) -> p t s", t=NT)
                  for b in range(2)]
        slots = cbc_region[:, 0:EROWS]
        ya = [probs_region[:, (2 * b) * D:(2 * b + 1) * D] for b in range(2)]
        yb = [probs_region[:, (2 * b + 1) * D:(2 * b + 2) * D] for b in range(2)]

        ident = cst[:, C_IDENT:C_IDENT + P]
        tri = cst[:, C_TRI:C_TRI + P]
        dil = cst[:, C_DIL:C_DIL + S]
        upper = cst[:, C_UP:C_UP + S]

        at = [0]

        def piece(n):
            at[0] += n
            return small[:, at[0] - n:at[0]]

        w_f = piece(NC * 4).rearrange("p (c n) -> p c n", c=NC)
        bf_b = piece(4)
        conv_k = piece(6).rearrange("p (c k) -> p c k", c=2)
        pool_s = piece(2)
        pool_wd = piece(2 * P).rearrange("p (c n) -> p c n", c=2)
        router_w = piece(NC * E).rearrange("p (c n) -> p c n", c=NC)
        rbias = piece(E)
        eps = piece(1)
        z_f = piece(16)
        az_f = piece(16)
        ls_f = piece(16)
        c_col = piece(16)
        peak = piece(4 * NH)
        npeak = piece(4 * NH)
        total = piece(4 * NH)
        rtotal = piece(4 * NH)
        stats = piece(12)
        moments = piece(2 * NT)
        lnv = piece(NT)
        r0 = piece(NT)
        nwt = piece(4)
        rstd = piece(NT)
        nmr = piece(NT)
        sg = piece(64)
        sel = piece(64)
        rank = piece(64)
        inpair = piece(64)
        chosen = piece(64)
        first = piece(64)
        tmp64 = piece(64)
        posm = piece(64)
        gscore = piece(16)
        grank = piece(16)
        gates = piece(2 * NT)
        gsum = piece(NT)
        yrow_f = piece(2 * NT)
        yrow = piece(2 * NT).bitcast(U32)
        idx = [piece(1).bitcast(U32) for _ in range(2)]
        most_f = piece(1)
        most = piece(1).bitcast(I32)
        at[0] += at[0] % 2
        chosen_b = piece(32).bitcast(BF16)
        upper_b = piece(64).bitcast(BF16)
        ones_b = piece(64).bitcast(BF16)
        tok_b = piece(4).bitcast(BF16)
        cmp_a = osb_region[:, 512:768]
        cmp_b = osb_region[:, 768:1024]

        bank = [ctx.enter_context(nc.psum_tensor(f"bank{b}", [P, 512], F32)) for b in range(8)]
        unit_bank = bank[0:2]
        score_bank = bank[2:4]
        turn_bank = bank[4:6]
        head_bank = bank[6]
        misc_bank = bank[7]
        logit_bank = bank[6]
        count_bank = bank[7]
        g_bank, u_bank, xg_bank, y_bank, idx_bank = bank[0], bank[1], bank[2:4], bank[4:6], bank[6]

        x_in = [sem(f"x_in{t}") for t in range(NT)]
        ident_in, wf_in, consts_in, select_in = sem("ident_in"), sem("wf_in"), sem("consts_in"), sem("select_in")
        bf_in, chan_in, router_in = sem("bf_in"), sem("chan_in"), sem("router_in")
        poolw_in, ln1_in, ln2_in, slots_in, wo_in = (sem("poolw_in"), sem("ln1_in"), sem("ln2_in"), sem("slots_in"),
                                                     sem("wo_in"))
        block_in = [sem(f"block_in_{b}") for b in BLOCKS]
        gate_in = [sem(f"gate_in{b}") for b in range(2)]
        up_in = [sem(f"up_in{b}") for b in range(2)]
        down_in = [sem(f"down_in{b}") for b in range(2)]
        unit_full, unit_act, unit_dve = sem("unit_full"), sem("unit_act"), sem("unit_dve")
        fl_full, az_ready, sp_ready, ls_ready = sem("fl_full"), sem("az_ready"), sem("sp_ready"), sem("ls_ready")
        cum_full, cum_act = sem("cum_full"), sem("cum_act")
        bias_ready = sem("bias_ready")
        score_full, peak_ready, exp_ready = sem("score_full"), sem("peak_ready"), sem("exp_ready")
        turn_full, turn_dve, turn_act = sem("turn_full"), sem("turn_dve"), sem("turn_act")
        head_full, head_dve = sem("head_full"), sem("head_dve")
        pair_full, pair_act = sem("pair_full"), sem("pair_act")
        pads_ready, pool_ready = sem("pads_ready"), sem("pool_ready")
        wo_full, wo_free = sem("wo_full"), sem("wo_free")
        var_ready, rsq_ready, ln_half, x1_dve, x1_pool, x1p_ready = (
            sem("var_ready"), sem("rsq_ready"), sem("ln_half"), sem("x1_dve"), sem("x1_pool"), sem("x1p_ready"))
        x1_out = sem("x1_out")
        x1t_full, x1t_act, x1t_dve = sem("x1t_full"), sem("x1t_act"), sem("x1t_dve")
        logit_full, esig_ready, chosen_ready, count_full = (sem("logit_full"), sem("esig_ready"),
                                                            sem("chosen_ready"), sem("count_full"))
        tok_ready, yrow_ready, most_ready, ax_ready = (sem("tok_ready"), sem("yrow_ready"), sem("most_ready"),
                                                       sem("ax_ready"))
        onehot_ready, idx_full, idx_ready = sem("onehot_ready"), sem("idx_full"), sem("idx_ready")
        rows_in = [sem(f"rows_in{b}") for b in range(2)]
        xg_full, xg_act, xg_dve = sem("xg_full"), sem("xg_act"), sem("xg_dve")
        g_full, eg_ready, silu_ready, u_full, h_ready = (sem("g_full"), sem("eg_ready"), sem("silu_ready"),
                                                         sem("u_full"), sem("h_ready"))
        y_full, y_act, y_dve = sem("y_full"), sem("y_act"), sem("y_dve")
        y_out = [sem(f"y_out{b}") for b in range(2)]
        m_step = {n: sem(f"more_{n}") for n in ("onehot", "idx_full", "idx", "rows", "xg_full", "xg", "g_full", "eg",
                                                "u_full", "h", "y_full", "y", "out", "gate_in", "up_in", "down_in",
                                                "dve", "onehot_pe")}
        ya_in = [sem(f"ya_in{b}") for b in range(2)]
        yb_in = [sem(f"yb_in{b}") for b in range(2)]
        fin_var, fin_rsq, fin_norm, fin_g, fin_ready = (sem("fin_var"), sem("fin_rsq"), sem("fin_norm"),
                                                        sem("fin_g"), sem("fin_ready"))
        fin_sum = sem("fin_sum")
        out_done = [sem(f"out_done{b}") for b in range(2)]
        dve_step, act_step, pool_step = sem("dve_step"), sem("act_step"), sem("pool_step")
        npeak_ready = sem("npeak_ready")
        gathers_begun = sem("gathers_begun")

        def unit_emptied(eng, n):
            eng.wait_ge(unit_act if unit_engine(n) == "act" else unit_dve, unit_count(n))

        def experts(eng, body):
            with eng.Fori(0, E // 2 - 1) as i:
                for b in range(2):
                    body(i * 2 + b, i, b, True, True)
            body(E - 2, E // 2 - 1, 0, True, False)
            body(E - 1, E // 2 - 1, 1, False, False)

        def more_chunks(eng, body, after=None):
            eng.wait_ge(most_ready, 1)
            peak_rows = eng.value_load(most[0:1, :], min_val=0, max_val=S)
            with eng.If(peak_rows > CAP):
                with eng.Fori(0, E) as e:
                    with eng.Fori(1, CHUNKS) as j:
                        body(e, j, e * (CHUNKS - 1) + j)
                if after:
                    after()
            return peak_rows

        block = ctx.enter_context(nc.Block())

        @block.sync
        def _(sp):
            for t in range(NT):
                sp.dma_start(x_sb[:, t, :], x_v[t]).then_inc(x_in[t], 16)
                if t == 0:
                    sp.dma_start(ident, consts[:, C_IDENT:C_IDENT + P]).then_inc(ident_in, 16)
            sp.dma_start(w_f, w_in_v[:, :, 10 * GW:10 * GW + 4]).then_inc(wf_in, 16)

            def load_block(n):
                col = BLOCK_COL[BLOCKS[n]] * GW
                sp.dma_start(in_w[n % NSLOT], w_in_v[:, :, col:col + GW]).then_inc(block_in[n], 16)

            def block_multiplied(n):
                sp.wait_ge(unit_full, unit_no((BLOCKS[n], 1)) + 1)

            load_block(0)
            load_block(1)
            sp.dma_start(bf_b, b_f.broadcast_to([P, 4])).then_inc(bf_in, 16)
            sp.dma_start(select_head, selectors).then_inc(select_in, 16)
            sp.dma_start(cst[:, P:], consts[:, P:]).then_inc(consts_in, 16)
            for n in range(2, NSLOT):
                load_block(n)
            for c in range(2):
                for k in range(3):
                    sp.dma_start(conv_k[:, c, k:k + 1],
                                 conv_w[0, k, c * P:(c + 1) * P].rearrange("(p a) -> p a", a=1)).then_inc(chan_in, 16)
                sp.dma_start(pool_s[:, c:c + 1],
                             pool_scale[0, c * P:(c + 1) * P].rearrange("(p a) -> p a", a=1)).then_inc(chan_in, 16)
            sp.wait_ge(pads_ready, 1)
            for g in range(4):
                r = 64 * (g % 2)
                sp.dma_start(pool_wd[r:r + 64, g // 2, r:r + 64], pool_w[0, g]).then_inc(poolw_in, 16)
            sp.dma_start(router_w, w_router_v).then_inc(router_in, 16)
            sp.dma_start(rbias, router_bias.rearrange("(a n) -> a n", a=1).broadcast_to([P, E]))\
                .then_inc(router_in, 16)
            for n in range(NSLOT, len(BLOCKS)):
                block_multiplied(n - NSLOT)
                load_block(n)
            sp.dma_start(o_w, w_o_v).then_inc(wo_in, 16)
            sp.wait_ge(pool_ready, 2)
            sp.dma_start(ln_gb[:, 0, :], ln1_g.broadcast_to([P, D])).then_inc(ln1_in, 16)
            sp.dma_start(ln_gb[:, 1, :], ln1_b.broadcast_to([P, D])).then_inc(ln1_in, 16)
            block_multiplied(len(BLOCKS) - 1)
            sp.dma_start(gate_w[0].rearrange("p c n -> p (c n)"), w_gate_v[0]).then_inc(gate_in[0], 16)
            sp.dma_start(up_w[0].rearrange("p c n -> p (c n)"), w_up_v[0]).then_inc(up_in[0], 16)
            sp.dma_start(down_w[0], w_down_v[0]).then_inc(down_in[0], 16)
            sp.dma_start(down_w[1], w_down_v[1]).then_inc(down_in[1], 16)
            sp.wait_ge(wo_full, 1)
            sp.dma_start(slots, slot_numbers).then_inc(slots_in, 16)
            for t in range(NT):
                sp.wait_ge(x1p_ready, t + 1)
                sp.dma_start(x1_rows_v[t], x1p[:, t].rearrange("p c q -> p (c q)")).then_inc(x1_out, 16)
            sp.dma_start(gate_w[1].rearrange("p c n -> p (c n)"), w_gate_v[1]).then_inc(gate_in[1], 16)
            sp.dma_start(up_w[1].rearrange("p c n -> p (c n)"), w_up_v[1]).then_inc(up_in[1], 16)
            sp.wait_ge(x1_dve, NT)
            sp.wait_ge(x1_pool, NT)
            sp.dma_start(ln_gb[:, 0, :], ln2_g.broadcast_to([P, D])).then_inc(ln2_in, 16)
            sp.dma_start(ln_gb[:, 1, :], ln2_b.broadcast_to([P, D])).then_inc(ln2_in, 16)

            for b in range(2):
                sp.sem_inc(y_out[b], 16)

            def expert(e, i, b, ahead1, ahead2):
                if ahead2:
                    sp.wait_ge(g_full, e + 1)
                    sp.dma_start(gate_w[b].rearrange("p c n -> p (c n)"),
                                 w_gate_v[bass.ds(e + 2, 1)].rearrange("e p n -> p (e n)")).then_inc(gate_in[b], 16)
                    sp.wait_ge(u_full, e + 1)
                    sp.dma_start(up_w[b].rearrange("p c n -> p (c n)"),
                                 w_up_v[bass.ds(e + 2, 1)].rearrange("e p n -> p (e n)")).then_inc(up_in[b], 16)
                    sp.wait_ge(y_full, e + 1)
                    sp.dma_start(down_w[b],
                                 w_down_v[bass.ds(e + 2, 1)].rearrange("e p c n -> p (e c) n")).then_inc(down_in[b], 16)
                sp.wait_ge(y_act, e + 1)
                sp.wait_ge(y_dve, e + 1)
                sp.dma_start(y_rows[bass.ds(e * CAP, CAP), :], y_sb[b][0:CAP, :]).then_inc(y_out[b], 16)

            experts(sp, expert)

            def more(e, j, n):
                sp.dma_start(gate_w[0].rearrange("p c n -> p (c n)"),
                             w_gate_v[bass.ds(e, 1)].rearrange("e p n -> p (e n)")).then_inc(m_step["gate_in"], 16)
                sp.dma_start(up_w[0].rearrange("p c n -> p (c n)"),
                             w_up_v[bass.ds(e, 1)].rearrange("e p n -> p (e n)")).then_inc(m_step["up_in"], 16)
                sp.dma_start(down_w[0],
                             w_down_v[bass.ds(e, 1)].rearrange("e p c n -> p (e c) n")).then_inc(m_step["down_in"], 16)
                sp.wait_ge(m_step["y"], n)
                sp.dma_start(y_rows[bass.ds(MAIN - CAP + e * MORE + j * CAP, CAP), :],
                             y_sb[0][0:CAP, :]).then_inc(m_step["out"], 16)

            sp.wait_ge(y_full, E)
            sp.wait_ge(y_out[0], 16 * (E // 2 + 1))
            more_chunks(sp, more, lambda: sp.wait_ge(m_step["out"], 16 * E * (CHUNKS - 1)))
            sp.wait_ge(y_out[1], 16 * (E // 2 + 1))
            for t in range(NT):
                sp.wait_ge(fin_ready, t + 1)
                sp.dma_start(out_v[t], ya[t % 2]).then_inc(out_done[t % 2], 16)
            for b in range(2):
                sp.wait_ge(out_done[b], 16 * NT // 2)

        @block.tensor
        def _(pe):
            def start_unit(n):
                if n >= 2:
                    unit_emptied(pe, n - 2)
                return unit_bank[n % 2]

            pe.wait_ge(ident_in, 16)
            for n in range(NX):
                t, half = n // 2, n % 2
                pe.wait_ge(x_in[t], 16)
                o = start_unit(n)
                for c in range(4):
                    mm = nc.tensor.transpose(o[:, c * P:(c + 1) * P],
                                             x_sb[:, t, (4 * half + c) * P:(4 * half + c + 1) * P], ident)
                mm.then_inc(unit_full, 1)

            unit_emptied(pe, NX - 2)
            unit_emptied(pe, NX - 1)
            pe.wait_ge(wf_in, 16)
            for t in range(NT):
                for c in range(NC):
                    mm = nc.tensor.matmul(misc_bank[:, 4 * t:4 * t + 4], xT[:, c, t * P:(t + 1) * P], w_f[:, c, :],
                                          start=(c == 0), stop=(c == NC - 1))
            mm.then_inc(fl_full, 1)

            def project(u):
                name, half = u
                n = unit_no(u)
                b = BLOCKS.index(name)
                w = in_w[b % NSLOT]
                pe.wait_ge(block_in[b], 16)
                o = start_unit(n)
                if name in ("fv", "dv"):
                    for k in range(2):
                        t = 2 * half + k
                        for c in range(NC):
                            mm = nc.tensor.matmul(o[:, k * GW:(k + 1) * GW], xT[:, c, t * P:(t + 1) * P], w[:, c, :],
                                                  start=(c == 0), stop=(c == NC - 1))
                else:
                    for c in range(NC):
                        mm = nc.tensor.matmul(o[:, :], w[:, c, half * P:(half + 1) * P], xT[:, c, :],
                                              start=(c == 0), stop=(c == NC - 1))
                mm.then_inc(unit_full, 1)

            def spread_sums(h):
                if h == 0:
                    pe.wait_ge(cum_act, 2)
                else:
                    pe.wait_ge(cum_act, 2 + h)
                nc.tensor.matmul(misc_bank[:, :], select_head[:, P * h:P * (h + 1)], cT,
                                 start=True, stop=True).then_inc(cum_full, 1)

            for k, u in enumerate(UNITS0):
                project(u)
                if k == 1:
                    pe.wait_ge(ls_ready, 1)
                    pe.wait_ge(consts_in, 16)
                    pe.wait_ge(select_in, 16)
                    for t in range(NT):
                        mm = nc.tensor.matmul(misc_bank[0:4, t * P:S], ls_f[:, 4 * t:4 * t + 4], upper[:, 0:S - t * P],
                                              start=(t == 0), stop=(t == NT - 1))
                    mm.then_inc(cum_full, 1)
                if k == 2:
                    pe.wait_ge(cum_act, 1)
                    for t in range(NT):
                        mm = nc.tensor.transpose(head_bank[:, 4 * t:4 * t + 4], cT[:, t * P:(t + 1) * P],
                                                 ident[0:4, 0:4])
                    mm.then_inc(cum_full, 1)
                if k == 3:
                    spread_sums(0)
                if k == 5:
                    spread_sums(1)

            def scores(h):
                g, hh = h // 4, h % 4
                r = HD * (hh % 2)
                q, k = qkT[r:r + HD, 4 * g + hh // 2, :], qkT[r:r + HD, 4 * g + 2 + hh // 2, :]
                name = "fd"[g]
                unit_emptied(pe, unit_no((name + "q", hh // 2)))
                unit_emptied(pe, unit_no((name + "k", hh // 2)))
                for i in range(NT):
                    s = NT * h + i
                    if s >= 2:
                        pe.wait_ge(peak_ready, s - 1)
                    nc.tensor.matmul(score_bank[s % 2][:, 0:(i + 1) * P], q[:, i * P:(i + 1) * P], k[:, 0:(i + 1) * P],
                                     start=True, stop=True).then_inc(score_full, 1)

            def turn_probs(h):
                for i in range(NT):
                    pe.wait_ge(exp_ready, NT * h + i + 1)
                    if i >= 2:
                        pe.wait_ge(turn_dve, 3 * h + i - 1)
                    elif h:
                        if i == 0:
                            pe.wait_ge(turn_dve, 3 * h)
                        else:
                            pe.wait_ge(turn_act, h)
                    o = turn_bank[i % 2]
                    for j in range(i + 1):
                        mm = nc.tensor.transpose(o[:, j * P:(j + 1) * P],
                                                 probs[h % 2][:, OFF[i] + j * P:OFF[i] + (j + 1) * P], ident)
                    mm.then_inc(turn_full, 1)

            def weigh_values(h):
                g, hh = h // 4, h % 4
                unit_emptied(pe, unit_no(("fd"[g] + "v", 1)))
                pe.wait_ge(turn_dve, 3 * h + 3)
                pe.wait_ge(turn_act, h + 1)
                if h:
                    pe.wait_ge(head_dve, h)
                else:
                    pe.wait_ge(cum_act, 2)
                for i in range(NT):
                    for j in range(i + 1):
                        mm = nc.tensor.matmul(head_bank[:, i * HD:(i + 1) * HD],
                                              probsT[h % 2][:, OFF[i] + j * P:OFF[i] + (j + 1) * P],
                                              v_sb[:, g, j, hh * HD:(hh + 1) * HD], start=(j == 0), stop=(j == i))
                mm.then_inc(head_full, 1)

            def turn_pair(m):
                pe.wait_ge(head_dve, 2 * m + 2)
                if m:
                    pe.wait_ge(pair_act, m)
                else:
                    pe.wait_ge(cum_act, 6)
                for t in range(NT):
                    mm = nc.tensor.transpose(misc_bank[:, t * P:(t + 1) * P], osb[m % 2][:, t, :], ident)
                mm.then_inc(pair_full, 1)

            for h in range(NH):
                scores(h)
                if h:
                    weigh_values(h - 1)
                if h <= 1:
                    spread_sums(h + 2)
                for u in FILL[h]:
                    project(u)
                turn_probs(h)
                if h and h % 2 == 0:
                    turn_pair(h // 2 - 1)
            pe.wait_ge(poolw_in, 64)
            for c in range(2):
                pe.wait_ge(pool_ready, c + 1)
                o = start_unit(unit_no(("pool", c)))
                nc.tensor.matmul(o[:, :], pool_wd[:, c, :], pool_u[c][:, 16:528], start=True,
                                 stop=True).then_inc(unit_full, 1)
            weigh_values(NH - 1)
            turn_pair(3)

            def project_out(t):
                if t == 0:
                    pe.wait_ge(wo_in, 16)
                    unit_emptied(pe, unit_no(("pool", 0)))
                    unit_emptied(pe, unit_no(("pool", 1)))
                    unit_emptied(pe, unit_no(("cb", 1)))
                    pe.wait_ge(peak_ready, NT * NH)
                if t >= 2:
                    pe.wait_ge(wo_free, t - 1)
                for k, c in enumerate([0, 1, 4, 5, 2, 6, 7, 3]):
                    if t == 0 and k == 0:
                        pe.wait_ge(pair_act, 3)
                    if t == 0 and c == 3:
                        pe.wait_ge(pair_act, 4)
                    for half in range(2):
                        mm = nc.tensor.matmul(bank[2 * (t % 2) + half][:, :], mixT[:, c, t * P:(t + 1) * P],
                                              o_w[:, c, half * 512:(half + 1) * 512], start=(k == 0),
                                              stop=(k == NC - 1))
                mm.then_inc(wo_full, 1)

            def turn_x1(t):
                pe.wait_ge(x1p_ready, t + 1)
                if t:
                    pe.wait_ge(x1t_act, t)
                    pe.wait_ge(x1t_dve, t)
                for c in range(NC):
                    mm = nc.tensor.transpose(turn_bank[c // 4][:, (c % 4) * P:(c % 4 + 1) * P], x1p[:, t, c, :], ident)
                mm.then_inc(x1t_full, 1)

            def logits(t):
                pe.wait_ge(x1t_act, t + 1)
                pe.wait_ge(x1t_dve, t + 1)
                for c in range(NC):
                    mm = nc.tensor.matmul(logit_bank[:, E * t:E * t + E], x1T[:, c, t * P:(t + 1) * P],
                                          router_w[:, c, :], start=(c == 0), stop=(c == NC - 1))
                mm.then_inc(logit_full, 1)

            project_out(0)
            project_out(1)
            pe.wait_ge(router_in, 32)
            turn_x1(0)
            project_out(2)
            logits(0)
            turn_x1(1)
            project_out(3)
            logits(1)
            turn_x1(2)
            logits(2)
            turn_x1(3)
            logits(3)

            pe.wait_ge(chosen_ready, 1)
            pe.wait_ge(tok_ready, 1)
            for t in range(NT):
                for s in range(t + 1):
                    nc.tensor.matmul(count_bank[:, E * t:E * t + E], (upper_b if s == t else ones_b),
                                     chosen_b[:, E * s:E * s + E], start=(s == 0), stop=(s == t))
            for s in range(NT):
                mm = nc.tensor.matmul(count_bank[:, E * NT:E * NT + E], ones_b, chosen_b[:, E * s:E * s + E],
                                      start=(s == 0), stop=(s == NT - 1))
            mm.then_inc(count_full, 1)

            def token_numbers(o, hot):
                for t in range(NT):
                    for k in (0, 1 + t):
                        mm = nc.tensor.matmul(o, hot[:, t, :], tok_b[:, k:k + 1], start=(t == 0 and k == 0),
                                              stop=(t == NT - 1 and k > 0))
                return mm

            def find_rows(e, b):
                pe.wait_ge(onehot_ready, e + 1)
                pe.wait_ge(idx_ready, e)
                token_numbers(idx_bank[0:CAP, 0:1], onehot[b]).then_inc(idx_full, 1)

            def turn_rows(src):
                for c in range(NC):
                    mm = nc.tensor.transpose(xg_bank[c // 4][:, (c % 4) * CAP:(c % 4 + 1) * CAP],
                                             src[0:CAP, c * P:(c + 1) * P], ident[0:CAP, 0:CAP])
                return mm

            def up_project(o, w):
                for m in range(NF):
                    for c in range(NC):
                        mm = nc.tensor.matmul(o[:, m * CAP:(m + 1) * CAP], w[:, c, m * P:(m + 1) * P], xgT[:, c, :],
                                              start=(c == 0), stop=(c == NC - 1))
                return mm

            def down_project(w):
                for c in range(NF):
                    for half in range(2):
                        mm = nc.tensor.matmul(y_bank[half][0:CAP, :], hT[:, c * CAP:(c + 1) * CAP],
                                              w[:, c, half * 512:(half + 1) * 512], start=(c == 0), stop=(c == NF - 1))
                return mm

            find_rows(0, 0)
            find_rows(1, 1)
            pe.wait_ge(rows_in[0], 16)
            turn_rows(xg[0]).then_inc(xg_full, 1)

            def expert(e, i, b, ahead1, ahead2):
                pe.wait_ge(xg_act, e + 1)
                pe.wait_ge(xg_dve, e + 1)
                pe.wait_ge(gate_in[b], i * 16 + 16)
                up_project(g_bank, gate_w[b]).then_inc(g_full, 1)
                if ahead2:
                    find_rows(e + 2, b)
                pe.wait_ge(up_in[b], i * 16 + 16)
                up_project(u_bank, up_w[b]).then_inc(u_full, 1)
                if ahead1:
                    pe.wait_ge(rows_in[1 - b], i * 16 + 16 * (b + 1))
                    turn_rows(xg[1 - b]).then_inc(xg_full, 1)
                pe.wait_ge(down_in[b], i * 16 + 16)
                pe.wait_ge(h_ready, e + 1)
                down_project(down_w[b]).then_inc(y_full, 1)

            experts(pe, expert)

            def more(e, j, n):
                pe.wait_ge(m_step["onehot"], n)
                token_numbers(idx_bank[0:CAP, 0:1], onehot[0]).then_inc(m_step["idx_full"], 1)
                pe.wait_ge(m_step["rows"], n * 16)
                turn_rows(xg[0]).then_inc(m_step["xg_full"], 1)
                pe.wait_ge(m_step["xg"], n)
                pe.wait_ge(m_step["gate_in"], n * 16)
                up_project(g_bank, gate_w[0]).then_inc(m_step["g_full"], 1)
                pe.wait_ge(m_step["up_in"], n * 16)
                up_project(u_bank, up_w[0]).then_inc(m_step["u_full"], 1)
                pe.wait_ge(m_step["down_in"], n * 16)
                pe.wait_ge(m_step["h"], n)
                down_project(down_w[0]).then_inc(m_step["y_full"], 1)
                pe.wait_ge(m_step["y"], n)

            pe.wait_ge(y_act, E)
            pe.wait_ge(y_dve, E)
            more_chunks(pe, more)

        @block.vector
        def _(dve):
            steps = [0]

            def done(ins):
                steps[0] += 1
                ins.then_inc(dve_step, 1)
                dve.wait_ge(dve_step, steps[0])

            done(nc.vector.memset(eps, EPS))
            done(nc.vector.memset(ones_b, 1.0))
            for n in range(1, NX, 2):
                t = n // 2
                dve.wait_ge(unit_full, n + 1)
                nc.vector.tensor_copy(xT[:, 4:8, t * P:(t + 1) * P],
                                      unit_bank[n % 2][:, :].rearrange("p (c q) -> p c q", c=4)).then_inc(unit_dve, 1)
            dve.wait_ge(fl_full, 1)
            dve.wait_ge(bf_in, 16)
            done(nc.vector.tensor_tensor(z_f.rearrange("p (t h) -> p t h", h=4),
                                         misc_bank[:, 0:16].rearrange("p (t h) -> p t h", h=4),
                                         bf_b.unsqueeze(1).broadcast_to([P, NT, 4]), ALU.add))
            nc.vector.scalar_tensor_tensor(out=az_f, in0=z_f, scalar=-1.0, in1=z_f, op0=ALU.mult,
                                           op1=ALU.max).then_inc(az_ready, 1)
            dve.wait_ge(sp_ready, 1)
            nc.vector.scalar_tensor_tensor(out=ls_f, in0=z_f, scalar=0.0, in1=az_f, op0=ALU.min,
                                           op1=ALU.subtract).then_inc(ls_ready, 1)
            dve.wait_ge(consts_in, 16)
            done(nc.vector.tensor_copy(upper_b, upper[:, 0:P]))
            nc.vector.tensor_copy(tok_b[:, 0:1 + NT], cst[:, C_TOK:C_TOK + 1 + NT]).then_inc(tok_ready, 1)

            def empty_values(u):
                name, half = u
                n = unit_no(u)
                dve.wait_ge(unit_full, n + 1)
                nc.vector.tensor_copy(v_sb[:, "fd".index(name[0]), 2 * half:2 * half + 2, :],
                                      unit_bank[n % 2][:, :].rearrange("p (t c) -> p t c", t=2)).then_inc(unit_dve, 1)

            empty_values(("fv", 0))
            empty_values(("fv", 1))

            def row_peaks(h):
                if h < 4:
                    dve.wait_ge(bias_ready, h + 1)
                else:
                    dve.wait_ge(turn_full, NT * (h - 1))
                for i in range(NT):
                    s = NT * h + i
                    n = (i + 1) * P
                    p = probs[h % 2][:, OFF[i]:OFF[i] + n]
                    dve.wait_ge(score_full, s + 1)
                    nc.vector.tensor_tensor_reduce(out=p, in0=score_bank[s % 2][:, 0:n],
                                                   in1=(p if h < 4 else dil[:, S - n:S]), scale=1.0, scalar=-3.0e38,
                                                   op0=ALU.add, op1=ALU.max,
                                                   accum_out=peak[:, s:s + 1]).then_inc(peak_ready, 1)
                    dve.wait_ge(peak_ready, s + 1)
                    nc.vector.tensor_scalar(npeak[:, s:s + 1], peak[:, s:s + 1], -1.0, None,
                                            ALU.mult).then_inc(npeak_ready, 1)

            def empty_head(h):
                dve.wait_ge(exp_ready, NT * (h + 1))
                done(nc.vector.reciprocal(rtotal[:, NT * h:NT * h + NT], total[:, NT * h:NT * h + NT]))
                dve.wait_ge(head_full, h + 1)
                if h >= 4:
                    dve.wait_ge(pair_full, h // 2 - 1)
                nc.vector.tensor_tensor(osb[(h // 2) % 2][:, :, (h % 2) * HD:(h % 2 + 1) * HD],
                                        head_bank[:, 0:NT * HD].rearrange("p (t n) -> p t n", t=NT),
                                        rtotal[:, NT * h:NT * h + NT].unsqueeze(2).broadcast_to([P, NT, HD]),
                                        ALU.mult).then_inc(head_dve, 1)

            def empty_turned(h):
                for i in range(3):
                    dve.wait_ge(turn_full, NT * h + i + 1)
                    if h >= 2:
                        dve.wait_ge(head_full, h - 1)
                    nc.vector.tensor_copy(probsT[h % 2][:, OFF[i]:OFF[i + 1]],
                                          turn_bank[i % 2][:, 0:(i + 1) * P]).then_inc(turn_dve, 1)

            def convolve(u):
                name, c = u
                n = unit_no(u)
                dve.wait_ge(unit_full, n + 1)
                if name == "ch":
                    if c == 0:
                        dve.wait_ge(pads_ready, 1)
                        dve.wait_ge(chan_in, 16 * 8)
                    dve.wait_ge(unit_act, unit_count(unit_no(("cc", c))))
                    nc.vector.tensor_tensor(conv_u[:, 2:514], unit_bank[n % 2][:, :], conv_c, ALU.mult)\
                        .then_inc(unit_dve, 1)
                    dve.wait_ge(unit_dve, unit_count(n))
                    done(nc.vector.tensor_scalar(conv_c, conv_u[:, 2:514], conv_k[:, c, 2:3], None, ALU.mult))
                    for k in (1, 0):
                        done(nc.vector.scalar_tensor_tensor(out=conv_c, in0=conv_u[:, k:k + S],
                                                            scalar=conv_k[:, c, k:k + 1], in1=conv_c,
                                                            op0=ALU.mult, op1=ALU.add))
                else:
                    nc.vector.tensor_tensor(mixT[:, 4 + c, :], unit_bank[n % 2][:, :], conv_c, ALU.mult)\
                        .then_inc(unit_dve, 1)

            for h in range(NH):
                row_peaks(h)
                if h:
                    empty_head(h - 1)
                for u in FILL[h]:
                    if u[0] == "dv":
                        empty_values(u)
                    elif u[0] in ("ch", "cb"):
                        convolve(u)
                empty_turned(h)
            empty_head(NH - 1)

            def rsqrt_refined(t):
                m, v = moments[:, 2 * t:2 * t + 1], moments[:, 2 * t + 1:2 * t + 2]
                r = r0[:, t:t + 1]
                done(nc.vector.tensor_scalar(nwt[:, 0:1], v, EPS, None, ALU.add))
                done(nc.vector.scalar_tensor_tensor(out=nwt[:, 1:2], in0=r, scalar=r, in1=nwt[:, 0:1],
                                                    op0=ALU.mult, op1=ALU.mult))
                done(nc.vector.tensor_scalar(nwt[:, 2:3], nwt[:, 1:2], -0.5, 1.5, ALU.mult, ALU.add))
                done(nc.vector.tensor_tensor(rstd[:, t:t + 1], nwt[:, 2:3], r, ALU.mult))

            def shift(t, signal):
                nc.vector.scalar_tensor_tensor(out=nmr[:, t:t + 1], in0=moments[:, 2 * t:2 * t + 1], scalar=-1.0,
                                               in1=rstd[:, t:t + 1], op0=ALU.mult, op1=ALU.mult).then_inc(signal, 1)

            def moments_of(src, t, signal):
                for half in range(2):
                    done(nc.vector.bn_stats(stats[:, 6 * half:6 * half + 6], src[:, half * 512:(half + 1) * 512]))
                nc.vector.bn_aggr(moments[:, 2 * t:2 * t + 2], stats).then_inc(signal, 1)

            def first_norm(t):
                dve.wait_ge(wo_full, t + 1)
                for half in range(2):
                    cols = slice(half * 512, (half + 1) * 512)
                    ins = nc.vector.scalar_tensor_tensor(out=x_sb[:, t, cols], in0=x_sb[:, t, cols], scalar=ALPHA,
                                                         in1=bank[2 * (t % 2) + half][:, :], op0=ALU.mult,
                                                         op1=ALU.add)
                ins.then_inc(wo_free, 1)
                dve.wait_ge(wo_free, t + 1)
                moments_of(x_sb[:, t, :], t, var_ready)
                dve.wait_ge(rsq_ready, t + 1)
                rsqrt_refined(t)
                shift(t, ln_half)
                dve.wait_ge(ln_half, 2 * t + 1)
                nc.vector.tensor_scalar(x_sb[:, t, :], x_sb[:, t, :], rstd[:, t:t + 1], nmr[:, t:t + 1], ALU.mult,
                                        ALU.add).then_inc(ln_half, 1)
                dve.wait_ge(ln_half, 2 * t + 2)
                if t == 0:
                    dve.wait_ge(ln1_in, 32)
                done(nc.vector.tensor_tensor(x_sb[:, t, 0:SPLIT], x_sb[:, t, 0:SPLIT], ln_gb[:, 0, 0:SPLIT], ALU.mult))
                nc.vector.tensor_tensor(x_sb[:, t, 0:SPLIT], x_sb[:, t, 0:SPLIT], ln_gb[:, 1, 0:SPLIT],
                                        ALU.add).then_inc(x1_dve, 1)

            def empty_x1(t):
                dve.wait_ge(x1t_full, t + 1)
                nc.vector.tensor_copy(x1T[:, 4:8, t * P:(t + 1) * P],
                                      turn_bank[1][:, :].rearrange("p (c q) -> p c q", c=4)).then_inc(x1t_dve, 1)

            for t in range(NT):
                first_norm(t)
                if t:
                    empty_x1(t - 1)
            empty_x1(NT - 1)

            def ranked(dst, src, groups):
                n = 16 * groups
                a, b = cmp_a[:, 0:n], cmp_b[:, 0:n]
                v = src.rearrange("p (g e) -> p g e", e=4)
                other = v.unsqueeze(2).broadcast_to([P, groups, 4, 4])
                own = v.unsqueeze(3).broadcast_to([P, groups, 4, 4])
                a4 = a.rearrange("p (g e j) -> p g e j", e=4, j=4)
                b4 = b.rearrange("p (g e j) -> p g e j", e=4, j=4)
                low = cst[:, C_LOW:C_LOW + 16].unsqueeze(1).broadcast_to([P, groups, 16])
                done(nc.vector.tensor_tensor(a4, other, own, ALU.is_equal))
                done(nc.vector.tensor_tensor(b4, other, own, ALU.is_gt))
                a3 = a.rearrange("p (g k) -> p g k", k=16)
                done(nc.vector.tensor_tensor(a3, a3, low, ALU.mult))
                done(nc.vector.tensor_tensor(a, a, b, ALU.add))
                done(nc.vector.tensor_reduce(dst, a.rearrange("p (g j) -> p g j", j=4), AX.X, ALU.add))

            def by_group(ap):
                return ap.rearrange("p (g e) -> p g e", e=4)

            dve.wait_ge(esig_ready, 1)
            done(nc.vector.tensor_scalar(tmp64, sg, 1.0, None, ALU.add))
            done(nc.vector.reciprocal(sg, tmp64))
            done(nc.vector.tensor_tensor(sel.rearrange("p (t e) -> p t e", e=E), sg.rearrange("p (t e) -> p t e", e=E),
                                         rbias.unsqueeze(1).broadcast_to([P, NT, E]), ALU.add))
            ranked(rank, sel, 16)
            done(nc.vector.tensor_scalar(inpair, rank, 1.5, None, ALU.is_lt))
            done(nc.vector.tensor_tensor(tmp64, inpair, sel, ALU.mult))
            done(nc.vector.tensor_reduce(gscore, by_group(tmp64), AX.X, ALU.add))
            ranked(grank, gscore, NT)
            done(nc.vector.tensor_scalar(grank, grank, 0.5, None, ALU.is_lt))
            best = grank.unsqueeze(2).broadcast_to([P, 16, 4])
            done(nc.vector.tensor_tensor(by_group(chosen), by_group(inpair), best, ALU.mult))
            nc.vector.tensor_copy(chosen_b, chosen).then_inc(chosen_ready, 1)
            dve.wait_ge(count_full, 1)
            done(nc.vector.tensor_tensor(posm, count_bank[:, 0:64], chosen, ALU.mult))
            done(nc.vector.tensor_scalar(posm, posm, -1.0, None, ALU.add))

            def mark_slots(e, hot, first_slot=0):
                return nc.vector.tensor_tensor(
                    hot, slots[:, bass.ds(first_slot, CAP)].unsqueeze(1).broadcast_to([P, NT, CAP]),
                    posm.rearrange("p (t e) -> p t e", e=E)[:, :, bass.ds(e, 1)].broadcast_to([P, NT, CAP]),
                    ALU.is_equal)

            def number_rows(e, b):
                dve.wait_ge(idx_full, e + 1)
                nc.vector.tensor_copy(idx[b][0:CAP, :], idx_bank[0:CAP, 0:1]).then_inc(idx_ready, 1)

            dve.wait_ge(slots_in, 16)
            for b in range(2):
                mark_slots(b, onehot[b]).then_inc(onehot_ready, 1)
            for b in range(2):
                number_rows(b, b)
            done(nc.vector.tensor_reduce(most_f[0:1, :], count_bank[0:1, 64:80], AX.X, ALU.max))
            nc.vector.tensor_copy(most[0:1, :], most_f[0:1, :]).then_inc(most_ready, 1)
            dve.wait_ge(xg_full, 1)
            nc.vector.tensor_copy(xgT[:, 4:8, :], xg_bank[1][:, 0:4 * CAP].rearrange("p (c s) -> p c s", c=4))\
                .then_inc(xg_dve, 1)
            done(nc.vector.tensor_scalar(tmp64, rank, 0.5, None, ALU.is_lt))
            done(nc.vector.tensor_tensor(by_group(first), by_group(tmp64), best, ALU.mult))
            by_tile = lambda ap: ap.rearrange("p (t e) -> p t e", e=E)
            done(nc.vector.tensor_tensor(tmp64, sg, chosen, ALU.mult))
            done(nc.vector.tensor_reduce(gsum, by_tile(tmp64), AX.X, ALU.add))
            done(nc.vector.reciprocal(gsum, gsum))
            done(nc.vector.tensor_scalar(inpair, posm, CAP - 0.5, None, ALU.is_gt))
            done(nc.vector.tensor_tensor(by_tile(inpair), by_tile(inpair),
                                         cst[:, C_ROW + E:C_ROW + 2 * E].unsqueeze(1).broadcast_to([P, NT, E]),
                                         ALU.mult))
            done(nc.vector.tensor_tensor(inpair, inpair, posm, ALU.add))
            done(nc.vector.tensor_tensor(by_tile(inpair), by_tile(inpair),
                                         cst[:, C_ROW:C_ROW + E].unsqueeze(1).broadcast_to([P, NT, E]), ALU.add))
            for k in range(2):
                if k == 1:
                    done(nc.vector.tensor_tensor(first, chosen, first, ALU.subtract))
                done(nc.vector.tensor_tensor(tmp64, sg, first, ALU.mult))
                done(nc.vector.tensor_reduce(gates[:, NT * k:NT * k + NT], by_tile(tmp64), AX.X, ALU.add))
                done(nc.vector.tensor_tensor(gates[:, NT * k:NT * k + NT], gates[:, NT * k:NT * k + NT], gsum,
                                             ALU.mult))
                done(nc.vector.tensor_tensor(tmp64, inpair, first, ALU.mult))
                done(nc.vector.tensor_reduce(yrow_f[:, NT * k:NT * k + NT], by_tile(tmp64), AX.X, ALU.add))
            nc.vector.tensor_copy(yrow, yrow_f).then_inc(yrow_ready, 1)
            for t in range(NT):
                dve.wait_ge(x1p_ready, t + 1)
                done(nc.vector.tensor_scalar(x_sb[:, t, :], x_sb[:, t, :], ALPHA, None, ALU.mult))
            base = steps[0]
            PER = 2

            def silu_up(step, n):
                nc.vector.tensor_scalar(act_g, act_g, 1.0, None, ALU.add).then_inc(step, 1)
                dve.wait_ge(step, n + 1)
                nc.vector.reciprocal(act_g, act_g).then_inc(step, 1)
                dve.wait_ge(step, n + 2)
                return nc.vector.tensor_tensor(act_g, g_bank[:, 0:NF * CAP], act_g, ALU.mult)

            def expert(e, i, b, ahead1, ahead2):
                if ahead2:
                    dve.wait_ge(idx_full, e + 1)
                    mark_slots(e + 2, onehot[b]).then_inc(onehot_ready, 1)
                dve.wait_ge(eg_ready, e + 1)
                silu_up(dve_step, e * PER + base).then_inc(silu_ready, 1)
                if ahead2:
                    dve.wait_ge(rows_in[b], i * 16 + 16)
                    number_rows(e + 2, b)
                dve.wait_ge(u_full, e + 1)
                dve.wait_ge(silu_ready, e + 1)
                nc.vector.tensor_tensor(hT, u_bank[:, 0:NF * CAP], act_g, ALU.mult).then_inc(h_ready, 1)
                if ahead1:
                    dve.wait_ge(xg_full, e + 2)
                    nc.vector.tensor_copy(xgT[:, 4:8, :], xg_bank[1][:, 0:4 * CAP]
                                          .rearrange("p (c s) -> p c s", c=4)).then_inc(xg_dve, 1)
                dve.wait_ge(y_full, e + 1)
                dve.wait_ge(y_out[b], i * 16 + 16)
                nc.vector.tensor_copy(y_sb[b][0:CAP, 512:1024], y_bank[1][0:CAP, :]).then_inc(y_dve, 1)

            experts(dve, expert)
            steps[0] = base + PER * E

            def more(e, j, n):
                mark_slots(e, onehot[0], j * CAP).then_inc(m_step["onehot"], 1)
                dve.wait_ge(m_step["idx_full"], n)
                nc.vector.tensor_copy(idx[0][0:CAP, :], idx_bank[0:CAP, 0:1]).then_inc(m_step["idx"], 1)
                dve.wait_ge(m_step["xg_full"], n)
                for k in range(2):
                    ins = nc.vector.tensor_copy(xgT[:, 4 * k:4 * k + 4, :], xg_bank[k][:, 0:4 * CAP]
                                                .rearrange("p (c s) -> p c s", c=4))
                ins.then_inc(m_step["xg"], 1)
                dve.wait_ge(m_step["eg"], n)
                silu_up(m_step["dve"], n * 3 - 3).then_inc(m_step["dve"], 1)
                dve.wait_ge(m_step["u_full"], n)
                dve.wait_ge(m_step["dve"], n * 3)
                nc.vector.tensor_tensor(hT, u_bank[:, 0:NF * CAP], act_g, ALU.mult).then_inc(m_step["h"], 1)
                dve.wait_ge(m_step["y_full"], n)
                for k in range(2):
                    ins = nc.vector.tensor_copy(y_sb[0][0:CAP, 512 * k:512 * k + 512], y_bank[k][0:CAP, :])
                ins.then_inc(m_step["y"], 1)

            dve.wait_ge(y_act, E)
            dve.wait_ge(y_out[0], 16 * (E // 2 + 1))
            more_chunks(dve, more)

            for t in range(NT):
                b = t % 2
                dve.wait_ge(ya_in[b], 16 * (t // 2 + 1))
                done(nc.vector.scalar_tensor_tensor(out=ya[b], in0=ya[b], scalar=gates[:, t:t + 1], in1=x_sb[:, t, :],
                                                    op0=ALU.mult, op1=ALU.add))
                dve.wait_ge(yb_in[b], 16 * (t // 2 + 1))
                done(nc.vector.scalar_tensor_tensor(out=ya[b], in0=yb[b], scalar=gates[:, NT + t:NT + t + 1],
                                                    in1=ya[b], op0=ALU.mult, op1=ALU.add))
                moments_of(ya[b], t, fin_var)
                dve.wait_ge(fin_rsq, t + 1)
                rsqrt_refined(t)
                shift(t, fin_sum)
                if t == 0:
                    dve.wait_ge(ln2_in, 32)
                if t:
                    dve.wait_ge(fin_g, t)
                    nc.vector.tensor_tensor(ya[1 - b], ya[1 - b], ln_gb[:, 1, :], ALU.add).then_inc(fin_ready, 1)
            dve.wait_ge(fin_g, NT)
            b = (NT - 1) % 2
            nc.vector.tensor_tensor(ya[b], ya[b], ln_gb[:, 1, :], ALU.add).then_inc(fin_ready, 1)

        @block.scalar
        def _(act):
            nc.scalar.preload_act_table_set("natural_log_exp_and_others")
            steps = [0]

            def done(ins):
                steps[0] += 1
                ins.then_inc(act_step, 1)
                act.wait_ge(act_step, steps[0])

            for n in range(0, NX, 2):
                t = n // 2
                act.wait_ge(unit_full, n + 1)
                nc.scalar.copy(xT[:, 0:4, t * P:(t + 1) * P],
                               unit_bank[n % 2][:, :].rearrange("p (c q) -> p c q", c=4)).then_inc(unit_act, 1)
            act.wait_ge(az_ready, 1)
            done(nc.scalar.activation(az_f, az_f, ACT.Exp, scale=-1.0))
            nc.scalar.activation(az_f, az_f, ACT.Ln, bias=1.0).then_inc(sp_ready, 1)

            def empty_unit(u):
                name, half = u
                n = unit_no(u)
                src = unit_bank[n % 2][:, :]
                act.wait_ge(unit_full, n + 1)
                if name in ("fq", "dq"):
                    ins = nc.scalar.mul(qkT[:, 4 * "fd".index(name[0]) + half, :], src, HD ** -0.5)
                elif name in ("fk", "dk"):
                    ins = nc.scalar.copy(qkT[:, 4 * "fd".index(name[0]) + 2 + half, :], src)
                elif name == "cc":
                    if half:
                        unit_emptied(act, unit_no(("cb", 0)))
                    ins = nc.scalar.copy(conv_c, src)
                elif name == "pu":
                    act.wait_ge(pads_ready, 1)
                    ins = nc.scalar.copy(pool_u[half][:, 16:528], src)
                else:
                    act.wait_ge(chan_in, 16 * 8)
                    ins = nc.scalar.mul(mixT[:, 6 + half, :], src, pool_s[:, half:half + 1])
                ins.then_inc(unit_act, 1)

            def empty_sums(k):
                act.wait_ge(cum_full, k + 1)
                if k == 0:
                    ins = nc.scalar.copy(cT, misc_bank[0:4, :])
                elif k == 1:
                    ins = nc.scalar.copy(c_col, head_bank[:, 0:16])
                else:
                    h = k - 2
                    if h >= 2:
                        act.wait_ge(bias_ready, h - 1)
                    ins = nc.scalar.mul(cbc[h % 2], misc_bank[:, :], -1.0)
                ins.then_inc(cum_act, 1)

            for k, u in enumerate(UNITS0):
                if unit_engine(unit_no(u)) == "act":
                    empty_unit(u)
                if k == 1:
                    empty_sums(0)
                if k == 2:
                    empty_sums(1)
                if k == 3:
                    empty_sums(2)
                if k == 5:
                    empty_sums(3)
            for h in range(NH):
                for i in range(NT):
                    s = NT * h + i
                    n = (i + 1) * P
                    p = probs[h % 2][:, OFF[i]:OFF[i] + n]
                    act.wait_ge(npeak_ready, s + 1)
                    nc.scalar.activation(p, p, ACT.Exp, bias=npeak[:, s:s + 1],
                                         accum_out=total[:, s:s + 1]).then_inc(exp_ready, 1)
                if h <= 1:
                    empty_sums(4 + h)
                for u in FILL[h]:
                    if unit_engine(unit_no(u)) == "act":
                        empty_unit(u)
                act.wait_ge(turn_full, NT * (h + 1))
                if h >= 2:
                    act.wait_ge(head_full, h - 1)
                nc.scalar.copy(probsT[h % 2][:, OFF[3]:OFF[3] + NT * P], turn_bank[1][:, :]).then_inc(turn_act, 1)
                if h and h % 2 == 0:
                    m = h // 2 - 1
                    act.wait_ge(pair_full, m + 1)
                    nc.scalar.copy(mixT[:, m, :], misc_bank[:, :]).then_inc(pair_act, 1)
            empty_unit(("pool", 0))
            empty_unit(("pool", 1))
            act.wait_ge(pair_full, 4)
            nc.scalar.copy(mixT[:, 3, :], misc_bank[:, :]).then_inc(pair_act, 1)

            def rsqrt(t, ready, signal):
                act.wait_ge(ready, t + 1)
                done(nc.scalar.activation(lnv[:, t:t + 1], moments[:, 2 * t + 1:2 * t + 2], ACT.Ln, bias=eps))
                nc.scalar.activation(r0[:, t:t + 1], lnv[:, t:t + 1], ACT.Exp, scale=-0.5).then_inc(signal, 1)

            def empty_x1(t):
                act.wait_ge(x1t_full, t + 1)
                nc.scalar.copy(x1T[:, 0:4, t * P:(t + 1) * P],
                               turn_bank[0][:, :].rearrange("p (c q) -> p c q", c=4)).then_inc(x1t_act, 1)

            for t in range(NT):
                rsqrt(t, var_ready, rsq_ready)
                act.wait_ge(x1_dve, t + 1)
                act.wait_ge(x1_pool, t + 1)
                nc.scalar.copy(x1p[:, t], x_sb[:, t, :].rearrange("p (q c) -> p c q", c=NC)).then_inc(x1p_ready, 1)
                if t:
                    empty_x1(t - 1)
            empty_x1(NT - 1)
            act.wait_ge(logit_full, NT)
            nc.scalar.activation(sg, logit_bank[:, 0:64], ACT.Exp, scale=-1.0).then_inc(esig_ready, 1)
            act.wait_ge(xg_full, 1)
            nc.scalar.copy(xgT[:, 0:4, :], xg_bank[0][:, 0:4 * CAP].rearrange("p (c s) -> p c s", c=4))\
                .then_inc(xg_act, 1)

            def expert(e, i, b, ahead1, ahead2):
                act.wait_ge(g_full, e + 1)
                nc.scalar.activation(act_g, g_bank[:, 0:NF * CAP], ACT.Exp, scale=-1.0).then_inc(eg_ready, 1)
                if ahead1:
                    act.wait_ge(xg_full, e + 2)
                    nc.scalar.copy(xgT[:, 0:4, :], xg_bank[0][:, 0:4 * CAP]
                                   .rearrange("p (c s) -> p c s", c=4)).then_inc(xg_act, 1)
                act.wait_ge(y_full, e + 1)
                act.wait_ge(y_out[b], i * 16 + 16)
                nc.scalar.copy(y_sb[b][0:CAP, 0:512], y_bank[0][0:CAP, :]).then_inc(y_act, 1)

            experts(act, expert)

            def more(e, j, n):
                act.wait_ge(m_step["g_full"], n)
                nc.scalar.activation(act_g, g_bank[:, 0:NF * CAP], ACT.Exp, scale=-1.0).then_inc(m_step["eg"], 1)

            act.wait_ge(h_ready, E)
            more_chunks(act, more)
            for t in range(NT):
                rsqrt(t, fin_var, fin_rsq)
                act.wait_ge(fin_sum, t + 1)
                nc.scalar.activation(ya[t % 2], ya[t % 2], ACT.Identity, scale=rstd[:, t:t + 1],
                                     bias=nmr[:, t:t + 1]).then_inc(fin_norm, 1)

        @block.gpsimd
        def _(pool):
            steps = [0]

            def done(ins):
                steps[0] += 1
                ins.then_inc(pool_step, 1)
                pool.wait_ge(pool_step, steps[0])

            done(nc.gpsimd.memset(pool_wd, 0.0))
            done(nc.gpsimd.memset(conv_u[:, 0:2], 0.0))
            for c in range(2):
                done(nc.gpsimd.memset(pool_u[c][:, 0:16], 0.0))
            done(nc.gpsimd.memset(pool_a[:, 0:16], 0.0))
            nc.gpsimd.memset(pool_b[:, 0:16], 0.0).then_inc(pads_ready, 1)
            pool.wait_ge(consts_in, 16)
            for h in range(4):
                pool.wait_ge(cum_act, 3 + h)
                if h >= 2:
                    pool.wait_ge(turn_full, NT * (h - 1))
                for i in range(NT):
                    p = probs[h % 2][:, OFF[i]:OFF[i] + (i + 1) * P]
                    done(nc.gpsimd.tensor_scalar(p, cbc[h % 2][:, 0:(i + 1) * P], c_col[:, 4 * i + h:4 * i + h + 1],
                                                 None, ALU.add))
                    ins = nc.gpsimd.tensor_tensor(p[:, i * P:(i + 1) * P], p[:, i * P:(i + 1) * P], tri, ALU.add)
                    if i < NT - 1:
                        done(ins)
                ins.then_inc(bias_ready, 1)

            def doubled(dst, src, w, rows=slice(0, P)):
                done(nc.gpsimd.tensor_tensor(dst[rows, 16:528], src[rows, 16:528], src[rows, 16 - w:528 - w], ALU.add))

            rc = cst[:, C_POOL:C_POOL + 32].rearrange("p (c k) -> p c k", c=2)
            low, high = slice(0, 64), slice(64, P)
            for c in range(2):
                pool.wait_ge(unit_act, unit_count(unit_no(("pu", c))))
                doubled(pool_a, pool_u[c], 1)
                if c == 0:
                    doubled(pool_b, pool_a, 2, high)
                else:
                    doubled(pool_b, pool_a, 2)
                    doubled(pool_a, pool_b, 4)
                    doubled(pool_b, pool_a, 8, high)
                for rows, sums in ((low, pool_a), (high, pool_b)):
                    done(nc.gpsimd.tensor_tensor(sums[rows, 16:32], sums[rows, 16:32], rc[rows, c, :], ALU.mult))
                    done(nc.gpsimd.tensor_scalar(sums[rows, 32:528], sums[rows, 32:528],
                                                 cst[rows, C_POOL + 32 + c:C_POOL + 33 + c], None, ALU.mult))
                    ins = nc.gpsimd.tensor_tensor(pool_u[c][rows, 16:528], sums[rows, 16:528],
                                                  pool_u[c][rows, 16:528], ALU.subtract)
                    if rows is low:
                        done(ins)
                ins.then_inc(pool_ready, 1)
                pool.wait_ge(pool_ready, c + 1)

            pool.wait_ge(ln1_in, 32)
            for t in range(NT):
                pool.wait_ge(ln_half, 2 * t + 2)
                v = x_sb[:, t, SPLIT:D]
                done(nc.gpsimd.tensor_tensor(v, v, ln_gb[:, 0, SPLIT:D], ALU.mult))
                nc.gpsimd.tensor_tensor(v, v, ln_gb[:, 1, SPLIT:D], ALU.add).then_inc(x1_pool, 1)

            def wait_apart(signal, value):
                pool.wait_ge(signal, value)
                pool.sem_inc(gathers_begun, 1)

            def gather(dst, rows, numbers, signal):
                nc.gpsimd.indirect_dma_start(dst, None, rows, bass.IndirectOffsetOnAxis(ap=numbers, axis=0))\
                    .then_inc(signal, 16)

            pool.wait_ge(x1_out, 16 * NT)
            for b in range(2):
                pool.wait_ge(idx_ready, b + 1)
                gather(xg[b][0:CAP, :], x1_rows, idx[b][0:CAP, :], rows_in[b])

            def expert(e, i, b, ahead1, ahead2):
                if ahead2:
                    pool.wait_ge(idx_ready, e + 3)
                    wait_apart(xg_full, e + 1)
                    gather(xg[b][0:CAP, :], x1_rows, idx[b][0:CAP, :], rows_in[b])

            experts(pool, expert)

            def more(e, j, n):
                wait_apart(m_step["idx"], n)
                gather(xg[0][0:CAP, :], x1_rows, idx[0][0:CAP, :], m_step["rows"])
                pool.wait_ge(m_step["out"], n * 16)

            pool.wait_ge(y_out[0], 16 * (E // 2 + 1))
            pool.wait_ge(y_out[1], 16 * (E // 2 + 1))
            peak_rows = more_chunks(pool, more)

            pool.wait_ge(yrow_ready, 1)

            def gather_results(t):
                b = t % 2
                if t >= 2:
                    pool.wait_ge(out_done[b], 16 * (t // 2))
                    pool.wait_ge(fin_var, t - 1)
                for ran, rows in ((peak_rows > CAP, y_rows), (peak_rows <= CAP, y_rows[0:MAIN, :])):
                    with pool.If(ran):
                        gather(ya[b], rows, yrow[:, t:t + 1], ya_in[b])
                        gather(yb[b], rows, yrow[:, NT + t:NT + t + 1], yb_in[b])

            gather_results(0)
            gather_results(1)
            pool.wait_ge(ln2_in, 32)
            for t in range(NT):
                pool.wait_ge(fin_norm, t + 1)
                nc.gpsimd.tensor_tensor(ya[t % 2], ya[t % 2], ln_gb[:, 0, :], ALU.mult).then_inc(fin_g, 1)
                if 1 <= t <= NT - 2:
                    gather_results(t + 1)


_INS = ["x", "w_in", "b_f", "conv_w", "pool_w", "pool_scale", "w_o", "ln1_g", "ln1_b", "w_router", "router_bias",
        "w_gate", "w_up", "w_down", "ln2_g", "ln2_b"]


def kernel(**inputs):
    import numpy as _np
    import concourse.bacc as _bacc
    from concourse import mybir as _mybir
    from concourse.bass_utils import run_bass_kernel_spmd as _run

    nc = _bacc.Bacc("TRN2", target_bir_lowering=False, num_devices=1)
    arrays, args = {}, []
    given = [(n, _np.ascontiguousarray(inputs[n])) for n in _INS]
    given += list(zip(["consts", "selectors", "slot_numbers"], constants()))
    for name, a in given:
        arrays[f"in_{name}_dram"] = a
        args.append(nc.dram_tensor(f"in_{name}_dram", a.shape, _mybir.dt.from_np(a.dtype), kind="ExternalInput").ap())
    out = nc.dram_tensor("out_0_dram", (1, S, D), F32, kind="ExternalOutput").ap()
    build(nc, *args, out)
    r = _run(nc, [arrays], core_ids=[0])
    return r.results[0]["out_0_dram"]
```

```python
from contextlib import ExitStack

import numpy as np
import concourse.bass as bass
from concourse import mybir

F32 = mybir.dt.float32
F32R = mybir.dt.float32r
BF16 = mybir.dt.bfloat16
I32 = mybir.dt.int32
U32 = mybir.dt.uint32
ALU = mybir.AluOpType
ACT = mybir.ActivationFunctionType
AX = mybir.AxisListType

P = 128
S = 512
D = 1024
NT = S // P
NC = D // P
HD = D // 16
GW = 4 * HD
NH = 8
E = 16
EG = 4
F = D // 2
NF = F // P
CAP = 96
CHUNKS = -(-S // CAP)
EROWS = CHUNKS * CAP
MAIN = E * CAP
MORE = EROWS - CAP
PATTERNS = ((128, 1), (512, 4), (2048, 16))
WINDOWS = (2, 4, 8, 16)
ALPHA = 2.0 ** 0.25
EPS = 1e-5
NEG = -1e30
OFF = [P * (i * (i + 1) // 2) for i in range(NT)]
PROBS = P * (NT * (NT + 1) // 2)

BLOCKS = ["fq", "fk", "fv", "dq", "dk", "dv", "pu", "cc", "ch", "cb"]
BLOCK_COL = dict(fq=0, fk=1, fv=2, dq=3, dk=4, dv=5, cb=6, cc=7, ch=8, pu=9)
NSLOT = 6
UNITS0 = [("fq", 0), ("fq", 1), ("fk", 0), ("fk", 1), ("fv", 0), ("fv", 1)]
FILL = [[("dq", 0), ("dq", 1)], [("dk", 0), ("dk", 1)], [("dv", 0), ("dv", 1)], [("pu", 0), ("pu", 1)],
        [("cc", 0), ("ch", 0)], [("cb", 0), ("cc", 1)], [("ch", 1), ("cb", 1)], []]
UNITS = UNITS0 + [u for f in FILL for u in f] + [("pool", 0), ("pool", 1)]
NX = 2 * NT
ON_DVE = ("fv", "dv", "ch", "cb")


def unit_engine(n):
    if n < NX:
        return "dve" if n % 2 else "act"
    return "dve" if UNITS[n - NX][0] in ON_DVE else "act"


def unit_count(n):
    return sum(unit_engine(m) == unit_engine(n) for m in range(n + 1))


def unit_no(u):
    return NX + UNITS.index(u)


C_IDENT = 0
C_TRI = C_IDENT + P
C_DIL = C_TRI + P
C_UP = C_DIL + S
C_POOL = C_UP + S
C_LOW = C_POOL + 34
C_ROW = C_LOW + 16
C_TOK = C_ROW + 2 * E
NCONST = C_TOK + 1 + NT


def constants():
    c = np.zeros((P, NCONST), np.float32)
    q, k = np.arange(P)[:, None], np.arange(P)[None, :]
    c[:, C_IDENT:C_IDENT + P] = q == k
    c[:, C_TRI:C_TRI + P] = np.where(k <= q, 0.0, NEG)
    for b in range(NT):
        dist = q + P * (NT - 1 - b) - k
        n = sum(((dist >= 0) & (dist % r == 0) & (dist // r <= w // r)).astype(np.int64) for w, r in PATTERNS)
        c[:, C_DIL + P * b:C_DIL + P * (b + 1)] = np.where(n > 0, np.log(np.maximum(n, 1)), NEG)
    c[:, C_UP:C_UP + S] = np.arange(S)[None, :] >= q
    for t in range(2):
        for half in range(2):
            w = WINDOWS[2 * t + half]
            rows = slice(64 * half, 64 * half + 64)
            c[rows, C_POOL + 16 * t:C_POOL + 16 * t + 16] = 1.0 / np.minimum(np.arange(16) + 1, w)
            c[rows, C_POOL + 32 + t] = 1.0 / w
    c[:, C_LOW:C_LOW + 16] = (np.arange(4)[None, :] < np.arange(4)[:, None]).reshape(1, 16)
    c[:, C_ROW:C_ROW + E] = CAP * np.arange(E)
    c[:, C_ROW + E:C_ROW + 2 * E] = MAIN - CAP + (MORE - CAP) * np.arange(E)
    c[:, C_TOK] = np.arange(P)
    c[:, C_TOK + 1:C_TOK + 1 + NT] = P * np.arange(NT)
    selectors = np.repeat(np.eye(4, dtype=np.float32), P, axis=1)
    return c, selectors, np.broadcast_to(np.arange(EROWS, dtype=np.float32), (P, EROWS)).copy()


def build(nc, x, w_in, b_f, conv_w, pool_w, pool_scale, w_o, ln1_g, ln1_b, w_router, router_bias,
          w_gate, w_up, w_down, ln2_g, ln2_b, consts, selectors, slot_numbers, out):
    x1_rows = nc.dram_tensor("x1_rows", [S, D], F32, kind="Internal").ap()
    y_rows = nc.dram_tensor("y_rows", [E * EROWS, D], F32, kind="Internal").ap()

    x_v = x.rearrange("a (t p) d -> (a t) p d", p=P)
    out_v = out.rearrange("a (t p) d -> (a t) p d", p=P)
    w_in_v = w_in.rearrange("l (c p) n -> p (l c) n", p=P)
    w_o_v = w_o.rearrange("l (c p) n -> p (l c) n", p=P)
    w_gate_v = w_gate.rearrange("l e (p c) n -> (l e) p (c n)", c=NC)
    w_up_v = w_up.rearrange("l e (p c) n -> (l e) p (c n)", c=NC)
    w_down_v = w_down.rearrange("l e (c p) n -> (l e) p c n", p=P)
    w_router_v = w_router.rearrange("(p c) n -> p c n", c=NC)
    x1_rows_v = x1_rows.rearrange("(t p) d -> t p d", p=P)

    with ExitStack() as ctx:
        start = {}

        def sb(name, shape, dt=F32):
            region = ctx.enter_context(nc.sbuf_tensor(name, shape, dt))
            start[name] = nc.sbuf_base - 4 * int(np.prod(shape[1:]))
            return region

        def rounded(name, region, first, n):
            return nc.alloc_sbuf_tensor_at(name, [P, n], F32R, offset=start[region] + 4 * first)

        def sem(name):
            return ctx.enter_context(nc.semaphore(name))

        WREG = NC * F
        wbuf = sb("wbuf", [P, 6 * WREG])
        x_sb = sb("x_sb", [P, NT, D])
        ln_gb = sb("ln_gb", [P, 2, D])
        heads_region = sb("heads_region", [P, NH * S])
        v_region = sb("v_region", [P, 2 * NT * GW])
        probs_region = sb("probs_region", [P, 4 * PROBS])
        cbc_region = sb("cbc_region", [P, 2 * S])
        mix_region = sb("mix_region", [P, NC * S])
        local_region = sb("local_region", [P, 2082])
        osb_region = sb("osb_region", [P, 2 * NT * P])
        cst = sb("cst", [P, NCONST])
        small = sb("small", [P, 1428])

        gate_w = [wbuf[:, 3 * b * WREG:(3 * b + 1) * WREG].rearrange("p (c n) -> p c n", c=NC) for b in range(2)]
        up_w = [wbuf[:, (3 * b + 1) * WREG:(3 * b + 2) * WREG].rearrange("p (c n) -> p c n", c=NC) for b in range(2)]
        down_w = [wbuf[:, (3 * b + 2) * WREG:(3 * b + 3) * WREG].rearrange("p (c n) -> p c n", c=NF)
                  for b in range(2)]
        in_w = [wbuf[:, s * NC * GW:(s + 1) * NC * GW].rearrange("p (c n) -> p c n", c=NC) for s in range(NSLOT)]
        o_w = wbuf[:, 3 * WREG:5 * WREG].rearrange("p (c n) -> p c n", c=NC)
        xT = wbuf[:, 5 * WREG:6 * WREG].rearrange("p (c s) -> p c s", c=NC)

        qkT = heads_region[:, :].rearrange("p (m s) -> p m s", m=NH)
        v_sb = v_region[:, :].rearrange("p (g t n) -> p g t n", g=2, t=NT)
        probs = [probs_region[:, b * PROBS:(b + 1) * PROBS] for b in range(2)]
        probsT = [probs_region[:, (2 + b) * PROBS:(3 + b) * PROBS] for b in range(2)]
        cbc = [cbc_region[:, b * S:(b + 1) * S] for b in range(2)]
        mixT = mix_region[:, :].rearrange("p (c s) -> p c s", c=NC)
        osb = [osb_region[:, b * NT * P:(b + 1) * NT * P].rearrange("p (t n) -> p t n", t=NT) for b in range(2)]
        conv_c = local_region[:, 0:512]
        conv_u = local_region[:, 512:512 + 514]
        pool_u = [local_region[:, 1026 + 528 * c:1554 + 528 * c] for c in range(2)]
        pool_a, pool_b = ln_gb[:, 0, 0:528], ln_gb[:, 1, 0:528]
        cT = mix_region[0:4, 2 * S:3 * S]
        select_head = mix_region[0:4, 3 * S:4 * S]

        x1p = heads_region[:, :].rearrange("p (t c q) -> p t c q", t=NT, c=NC)
        x1T = probs_region[:, 0:NC * S].rearrange("p (c s) -> p c s", c=NC)
        xg = [v_region[:, b * D:(b + 1) * D] for b in range(2)]
        y_sb = mix_region[:, 0:D]
        slots = cbc_region[:, 0:CAP]
        onehot = [cbc_region[:, CAP + b * 2 * CAP:CAP + (b + 1) * 2 * CAP].bitcast(BF16)
                  .rearrange("p (t s) -> p t s", t=NT) for b in range(2)]
        act_g = local_region[:, 2 * NC * CAP:2 * NC * CAP + F]
        xH = [rounded(f"xH{b}", "local_region", b * NC * CAP, NC * CAP)[:, :].rearrange("p (c s) -> p c s", c=NC)
              for b in range(2)]
        hH = rounded("hH", "cbc_region", 5 * CAP, NF * CAP)
        gate_H = rounded("gate_H", "probs_region", 0, WREG)[:, :].rearrange("p (c n) -> p c n", c=NC)
        up_H = rounded("up_H", "heads_region", 0, WREG)[:, :].rearrange("p (c n) -> p c n", c=NC)
        down_H012 = rounded("down_H012", "mix_region", D, 3 * D)
        down_H3 = rounded("down_H3", "probs_region", WREG, D)
        down_H = [down_H012[:, c * D:(c + 1) * D] for c in range(3)] + [down_H3[:, :]]
        xL = [rounded(f"xL{b}", *place, NC * CAP)[:, :].rearrange("p (c s) -> p c s", c=NC)
              for b, place in enumerate([("osb_region", 0), ("cst", C_TRI)])]
        hL = rounded("hL", "cst", C_TRI + NC * CAP, NF * CAP)
        low_w = rounded("low_w", "wbuf", 0, 6 * WREG)
        gate_L = [low_w[:, 3 * b * WREG:(3 * b + 1) * WREG].rearrange("p (c n) -> p c n", c=NC) for b in range(2)]
        up_L = [low_w[:, (3 * b + 1) * WREG:(3 * b + 2) * WREG].rearrange("p (c n) -> p c n", c=NC)
                for b in range(2)]
        down_L = [low_w[:, (3 * b + 2) * WREG:(3 * b + 3) * WREG].rearrange("p (c n) -> p c n", c=NF)
                  for b in range(2)]
        more_xT = local_region[:, 0:NC * CAP].rearrange("p (c s) -> p c s", c=NC)
        more_g = local_region[:, 768:768 + NF * CAP]
        more_hT = local_region[:, 1152:1152 + NF * CAP]
        centred = [v_region[:, b * D:(b + 1) * D] for b in range(2)]
        squares = osb_region[:, 0:D]
        ya = [wbuf[:, t * D:(t + 1) * D] for t in range(NT)]
        yb = [wbuf[:, (NT + t) * D:(NT + t + 1) * D] for t in range(NT)]
        fin_squares = wbuf[:, 2 * NT * D:(2 * NT + 1) * D]

        ident = cst[:, C_IDENT:C_IDENT + P]
        tri = cst[:, C_TRI:C_TRI + P]
        dil = cst[:, C_DIL:C_DIL + S]
        upper = cst[:, C_UP:C_UP + S]

        at = [0]

        def piece(n):
            at[0] += n
            return small[:, at[0] - n:at[0]]

        w_f = piece(NC * 4).rearrange("p (c n) -> p c n", c=NC)
        bf_b = piece(4)
        conv_k = piece(6).rearrange("p (c k) -> p c k", c=2)
        pool_s = piece(2)
        pool_wd = piece(2 * P).rearrange("p (c n) -> p c n", c=2)
        router_w = piece(NC * E).rearrange("p (c n) -> p c n", c=NC)
        rbias = piece(E)
        eps = piece(1)
        z_f = piece(16)
        az_f = piece(16)
        ls_f = piece(16)
        c_col = piece(16)
        peak = piece(4 * NH)
        npeak = piece(4 * NH)
        total = piece(4 * NH)
        rtotal = piece(4 * NH)
        rowsum = piece(2 * NT)
        nmean = piece(NT)
        devsq = piece(NT)
        lnv = piece(NT)
        r0 = piece(NT)
        nwt = piece(4)
        rstd = piece(NT)
        nmr = piece(NT)
        sg = piece(64)
        sel = piece(64)
        rank = piece(64)
        inpair = piece(64)
        chosen = piece(64)
        first = piece(64)
        tmp64 = piece(64)
        posm = piece(64)
        gscore = piece(16)
        grank = piece(16)
        gates = piece(2 * NT)
        gsum = piece(NT)
        yrow_f = piece(2 * NT)
        yrow = piece(2 * NT).bitcast(U32)
        idx = [piece(1).bitcast(U32) for _ in range(2)]
        most_f = piece(1)
        most = piece(1).bitcast(I32)
        at[0] += at[0] % 2
        chosen_b = piece(32).bitcast(BF16)
        upper_b = piece(64).bitcast(BF16)
        ones_b = piece(64).bitcast(BF16)
        tok_b = piece(4).bitcast(BF16)
        cmp_a = osb_region[:, 512:768]
        cmp_b = osb_region[:, 768:1024]

        bank = [ctx.enter_context(nc.psum_tensor(f"bank{b}", [P, 512], F32)) for b in range(8)]
        unit_bank = bank[0:2]
        score_bank = bank[2:4]
        turn_bank = bank[4:6]
        head_bank = bank[6]
        misc_bank = bank[7]
        logit_bank = bank[6]
        count_bank = bank[7]
        g_bank, u_bank, xg_bank, y_bank, idx_bank, h_bank = bank[0], bank[1], bank[2:4], bank[4:6], bank[6], bank[7]

        x_in = [sem(f"x_in{t}") for t in range(NT)]
        ident_in, wf_in, consts_in, select_in = sem("ident_in"), sem("wf_in"), sem("consts_in"), sem("select_in")
        bf_in, chan_in, router_in = sem("bf_in"), sem("chan_in"), sem("router_in")
        poolw_in, ln1_in, ln2_in, slots_in, wo_in = (sem("poolw_in"), sem("ln1_in"), sem("ln2_in"), sem("slots_in"),
                                                     sem("wo_in"))
        block_in = [sem(f"block_in_{b}") for b in BLOCKS]
        gate_in = [sem(f"gate_in{b}") for b in range(2)]
        up_in = [sem(f"up_in{b}") for b in range(2)]
        down_in = [sem(f"down_in{b}") for b in range(2)]
        unit_full, unit_act, unit_dve = sem("unit_full"), sem("unit_act"), sem("unit_dve")
        fl_full, az_ready, sp_ready, ls_ready = sem("fl_full"), sem("az_ready"), sem("sp_ready"), sem("ls_ready")
        cum_full, cum_act = sem("cum_full"), sem("cum_act")
        bias_ready = sem("bias_ready")
        score_full, peak_ready, exp_ready = sem("score_full"), sem("peak_ready"), sem("exp_ready")
        turn_full, turn_dve, turn_act = sem("turn_full"), sem("turn_dve"), sem("turn_act")
        head_full, head_dve = sem("head_full"), sem("head_dve")
        pair_full, pair_act = sem("pair_full"), sem("pair_act")
        pads_ready, pool_ready = sem("pads_ready"), sem("pool_ready")
        wo_full, wo_free = sem("wo_full"), sem("wo_free")
        mean_ready, rsq_ready, x1p_ready = sem("mean_ready"), sem("rsq_ready"), sem("x1p_ready")
        x1_out = sem("x1_out")
        x1t_full, x1t_act, x1t_dve = sem("x1t_full"), sem("x1t_act"), sem("x1t_dve")
        logit_full, esig_ready, chosen_ready, count_full = (sem("logit_full"), sem("esig_ready"),
                                                            sem("chosen_ready"), sem("count_full"))
        tok_ready, yrow_ready, most_ready, ax_ready = (sem("tok_ready"), sem("yrow_ready"), sem("most_ready"),
                                                       sem("ax_ready"))
        onehot_ready, idx_full, idx_ready = sem("onehot_ready"), sem("idx_full"), sem("idx_ready")
        rows_in = [sem(f"rows_in{b}") for b in range(2)]
        xg_full, xh_ready, xl_ready = sem("xg_full"), sem("xh_ready"), sem("xl_ready")
        gate_high, gate_low, up_high, up_low, down_high, down_low = (
            sem("gate_high"), sem("gate_low"), sem("up_high"), sem("up_low"), sem("down_high"), sem("down_low"))
        g_full, eg_ready, silu_ready, u_full, h_ready = (sem("g_full"), sem("eg_ready"), sem("silu_ready"),
                                                         sem("u_full"), sem("h_ready"))
        turned_h, hh_ready, hl_ready = sem("turned_h"), sem("hh_ready"), sem("hl_ready")
        y_full, y_ready, y_out = sem("y_full"), sem("y_ready"), sem("y_out")
        m_step = {n: sem(f"more_{n}") for n in ("onehot", "idx_full", "idx", "rows", "xg_full", "xg", "g_full", "eg",
                                                "u_full", "h", "y_full", "y", "out", "gate_in", "up_in", "down_in",
                                                "dve", "slots")}
        ya_in = [sem(f"ya_in{t}") for t in range(NT)]
        yb_in = [sem(f"yb_in{t}") for t in range(NT)]
        fin_mean, fin_rsq, fin_shift, fin_norm, fin_g, fin_ready = (
            sem("fin_mean"), sem("fin_rsq"), sem("fin_shift"), sem("fin_norm"), sem("fin_g"), sem("fin_ready"))
        out_done = [sem(f"out_done{t}") for t in range(NT)]
        dve_step, act_step, pool_step = sem("dve_step"), sem("act_step"), sem("pool_step")
        npeak_ready = sem("npeak_ready")
        gathers_begun = sem("gathers_begun")

        def unit_emptied(eng, n):
            eng.wait_ge(unit_act if unit_engine(n) == "act" else unit_dve, unit_count(n))

        def experts(eng, body):
            with eng.Fori(0, E // 2 - 2) as i:
                for b in range(2):
                    body(i * 2 + b, i, b, 3)
            for e in range(E - 4, E):
                body(e, e // 2, e % 2, min(3, E - 1 - e))

        def more_chunks(eng, body, after=None):
            eng.wait_ge(most_ready, 1)
            peak_rows = eng.value_load(most[0:1, :], min_val=0, max_val=S)
            with eng.If(peak_rows > CAP):
                with eng.Fori(0, E) as e:
                    with eng.Fori(1, CHUNKS) as j:
                        body(e, j, e * (CHUNKS - 1) + j)
                if after:
                    after()
            return peak_rows

        block = ctx.enter_context(nc.Block())

        @block.sync
        def _(sp):
            for t in range(NT):
                sp.dma_start(x_sb[:, t, :], x_v[t]).then_inc(x_in[t], 16)
                if t == 0:
                    sp.dma_start(ident, consts[:, C_IDENT:C_IDENT + P]).then_inc(ident_in, 16)
            sp.dma_start(w_f, w_in_v[:, :, 10 * GW:10 * GW + 4]).then_inc(wf_in, 16)

            def load_block(n):
                col = BLOCK_COL[BLOCKS[n]] * GW
                sp.dma_start(in_w[n % NSLOT], w_in_v[:, :, col:col + GW]).then_inc(block_in[n], 16)

            def block_multiplied(n):
                sp.wait_ge(unit_full, unit_no((BLOCKS[n], 1)) + 1)

            load_block(0)
            load_block(1)
            sp.dma_start(bf_b, b_f.broadcast_to([P, 4])).then_inc(bf_in, 16)
            sp.dma_start(select_head, selectors).then_inc(select_in, 16)
            sp.dma_start(cst[:, P:], consts[:, P:]).then_inc(consts_in, 16)
            for n in range(2, NSLOT):
                load_block(n)
            for c in range(2):
                for k in range(3):
                    sp.dma_start(conv_k[:, c, k:k + 1],
                                 conv_w[0, k, c * P:(c + 1) * P].rearrange("(p a) -> p a", a=1)).then_inc(chan_in, 16)
                sp.dma_start(pool_s[:, c:c + 1],
                             pool_scale[0, c * P:(c + 1) * P].rearrange("(p a) -> p a", a=1)).then_inc(chan_in, 16)
            sp.wait_ge(pads_ready, 1)
            for g in range(4):
                r = 64 * (g % 2)
                sp.dma_start(pool_wd[r:r + 64, g // 2, r:r + 64], pool_w[0, g]).then_inc(poolw_in, 16)
            sp.dma_start(router_w, w_router_v).then_inc(router_in, 16)
            sp.dma_start(rbias, router_bias.rearrange("(a n) -> a n", a=1).broadcast_to([P, E]))\
                .then_inc(router_in, 16)
            for n in range(NSLOT, len(BLOCKS)):
                block_multiplied(n - NSLOT)
                load_block(n)
            sp.dma_start(o_w, w_o_v).then_inc(wo_in, 16)
            sp.wait_ge(pool_ready, 2)
            sp.dma_start(ln_gb[:, 0, :], ln1_g.broadcast_to([P, D])).then_inc(ln1_in, 16)
            sp.dma_start(ln_gb[:, 1, :], ln1_b.broadcast_to([P, D])).then_inc(ln1_in, 16)
            block_multiplied(len(BLOCKS) - 1)
            sp.dma_start(gate_w[0].rearrange("p c n -> p (c n)"), w_gate_v[0]).then_inc(gate_in[0], 16)
            sp.dma_start(up_w[0].rearrange("p c n -> p (c n)"), w_up_v[0]).then_inc(up_in[0], 16)
            sp.dma_start(down_w[0], w_down_v[0]).then_inc(down_in[0], 16)
            sp.dma_start(down_w[1], w_down_v[1]).then_inc(down_in[1], 16)
            sp.wait_ge(wo_full, 1)
            sp.dma_start(slots, slot_numbers[:, 0:CAP]).then_inc(slots_in, 16)
            for t in range(NT):
                sp.wait_ge(x1p_ready, 2 * t + 2)
                sp.dma_start(x1_rows_v[t], x1p[:, t].rearrange("p c q -> p (c q)")).then_inc(x1_out, 16)
            sp.dma_start(gate_w[1].rearrange("p c n -> p (c n)"), w_gate_v[1]).then_inc(gate_in[1], 16)
            sp.dma_start(up_w[1].rearrange("p c n -> p (c n)"), w_up_v[1]).then_inc(up_in[1], 16)
            sp.dma_start(ln_gb[:, 0, :], ln2_g.broadcast_to([P, D])).then_inc(ln2_in, 16)
            sp.dma_start(ln_gb[:, 1, :], ln2_b.broadcast_to([P, D])).then_inc(ln2_in, 16)

            sp.sem_inc(y_out, 16)

            def expert(e, i, b, ahead):
                if ahead >= 2:
                    sp.wait_ge(g_full, e + 1)
                    sp.dma_start(gate_w[b].rearrange("p c n -> p (c n)"),
                                 w_gate_v[bass.ds(e + 2, 1)].rearrange("e p n -> p (e n)")).then_inc(gate_in[b], 16)
                    sp.wait_ge(u_full, e + 1)
                    sp.dma_start(up_w[b].rearrange("p c n -> p (c n)"),
                                 w_up_v[bass.ds(e + 2, 1)].rearrange("e p n -> p (e n)")).then_inc(up_in[b], 16)
                    sp.wait_ge(y_full, e + 1)
                    sp.dma_start(down_w[b],
                                 w_down_v[bass.ds(e + 2, 1)].rearrange("e p c n -> p (e c) n")).then_inc(down_in[b], 16)
                sp.wait_ge(y_ready, e + 1)
                sp.dma_start(y_rows[bass.ds(e * CAP, CAP), :], y_sb[0:CAP, :]).then_inc(y_out, 16)

            experts(sp, expert)

            def more(e, j, n):
                sp.dma_start(slots, slot_numbers[:, bass.ds(j * CAP, CAP)]).then_inc(m_step["slots"], 16)
                sp.dma_start(gate_w[0].rearrange("p c n -> p (c n)"),
                             w_gate_v[bass.ds(e, 1)].rearrange("e p n -> p (e n)")).then_inc(m_step["gate_in"], 16)
                sp.dma_start(up_w[0].rearrange("p c n -> p (c n)"),
                             w_up_v[bass.ds(e, 1)].rearrange("e p n -> p (e n)")).then_inc(m_step["up_in"], 16)
                sp.dma_start(down_w[0],
                             w_down_v[bass.ds(e, 1)].rearrange("e p c n -> p (e c) n")).then_inc(m_step["down_in"], 16)
                sp.wait_ge(m_step["y"], n)
                sp.dma_start(y_rows[bass.ds(MAIN - CAP + e * MORE + j * CAP, CAP), :],
                             y_sb[0:CAP, :]).then_inc(m_step["out"], 16)

            sp.wait_ge(y_out, 16 * (E + 1))
            more_chunks(sp, more, lambda: sp.wait_ge(m_step["out"], 16 * E * (CHUNKS - 1)))
            for t in range(NT - 1):
                sp.wait_ge(fin_ready, t + 1)
                sp.dma_start(out_v[t], ya[t]).then_inc(out_done[t], 16)
            for half in range(2):
                cols = slice(half * 512, (half + 1) * 512)
                sp.wait_ge(fin_ready, NT + half)
                sp.dma_start(out_v[NT - 1][:, cols], ya[NT - 1][:, cols]).then_inc(out_done[(NT - 1) * half], 16)
            for t in range(NT):
                sp.wait_ge(out_done[t], 32 if t == 0 else 16)

        @block.tensor
        def _(pe):
            def start_unit(n):
                if n >= 2:
                    unit_emptied(pe, n - 2)
                return unit_bank[n % 2]

            pe.wait_ge(ident_in, 16)
            for n in range(NX):
                t, half = n // 2, n % 2
                pe.wait_ge(x_in[t], 16)
                o = start_unit(n)
                for c in range(4):
                    mm = nc.tensor.transpose(o[:, c * P:(c + 1) * P],
                                             x_sb[:, t, (4 * half + c) * P:(4 * half + c + 1) * P], ident)
                mm.then_inc(unit_full, 1)

            unit_emptied(pe, NX - 2)
            unit_emptied(pe, NX - 1)
            pe.wait_ge(wf_in, 16)
            for t in range(NT):
                for c in range(NC):
                    mm = nc.tensor.matmul(misc_bank[:, 4 * t:4 * t + 4], xT[:, c, t * P:(t + 1) * P], w_f[:, c, :],
                                          start=(c == 0), stop=(c == NC - 1))
            mm.then_inc(fl_full, 1)

            def project(u):
                name, half = u
                n = unit_no(u)
                b = BLOCKS.index(name)
                w = in_w[b % NSLOT]
                pe.wait_ge(block_in[b], 16)
                o = start_unit(n)
                if name in ("fv", "dv"):
                    for k in range(2):
                        t = 2 * half + k
                        for c in range(NC):
                            mm = nc.tensor.matmul(o[:, k * GW:(k + 1) * GW], xT[:, c, t * P:(t + 1) * P], w[:, c, :],
                                                  start=(c == 0), stop=(c == NC - 1))
                else:
                    for c in range(NC):
                        mm = nc.tensor.matmul(o[:, :], w[:, c, half * P:(half + 1) * P], xT[:, c, :],
                                              start=(c == 0), stop=(c == NC - 1))
                mm.then_inc(unit_full, 1)

            def spread_sums(h):
                if h == 0:
                    pe.wait_ge(cum_act, 2)
                else:
                    pe.wait_ge(cum_act, 2 + h)
                nc.tensor.matmul(misc_bank[:, :], select_head[:, P * h:P * (h + 1)], cT,
                                 start=True, stop=True).then_inc(cum_full, 1)

            for k, u in enumerate(UNITS0):
                project(u)
                if k == 1:
                    pe.wait_ge(ls_ready, 1)
                    pe.wait_ge(consts_in, 16)
                    pe.wait_ge(select_in, 16)
                    for t in range(NT):
                        mm = nc.tensor.matmul(misc_bank[0:4, t * P:S], ls_f[:, 4 * t:4 * t + 4], upper[:, 0:S - t * P],
                                              start=(t == 0), stop=(t == NT - 1))
                    mm.then_inc(cum_full, 1)
                if k == 2:
                    pe.wait_ge(cum_act, 1)
                    for t in range(NT):
                        mm = nc.tensor.transpose(head_bank[:, 4 * t:4 * t + 4], cT[:, t * P:(t + 1) * P],
                                                 ident[0:4, 0:4])
                    mm.then_inc(cum_full, 1)
                if k == 3:
                    spread_sums(0)
                if k == 5:
                    spread_sums(1)

            def scores(h):
                g, hh = h // 4, h % 4
                r = HD * (hh % 2)
                q, k = qkT[r:r + HD, 4 * g + hh // 2, :], qkT[r:r + HD, 4 * g + 2 + hh // 2, :]
                name = "fd"[g]
                unit_emptied(pe, unit_no((name + "q", hh // 2)))
                unit_emptied(pe, unit_no((name + "k", hh // 2)))
                for i in range(NT):
                    s = NT * h + i
                    if s >= 2:
                        pe.wait_ge(peak_ready, s - 1)
                    nc.tensor.matmul(score_bank[s % 2][:, 0:(i + 1) * P], q[:, i * P:(i + 1) * P], k[:, 0:(i + 1) * P],
                                     start=True, stop=True).then_inc(score_full, 1)

            def turn_probs(h):
                for i in range(NT):
                    pe.wait_ge(exp_ready, NT * h + i + 1)
                    if i >= 2:
                        pe.wait_ge(turn_dve, 3 * h + i - 1)
                    elif h:
                        if i == 0:
                            pe.wait_ge(turn_dve, 3 * h)
                        else:
                            pe.wait_ge(turn_act, h)
                    o = turn_bank[i % 2]
                    for j in range(i + 1):
                        mm = nc.tensor.transpose(o[:, j * P:(j + 1) * P],
                                                 probs[h % 2][:, OFF[i] + j * P:OFF[i] + (j + 1) * P], ident)
                    mm.then_inc(turn_full, 1)

            def weigh_values(h):
                g, hh = h // 4, h % 4
                unit_emptied(pe, unit_no(("fd"[g] + "v", 1)))
                pe.wait_ge(turn_dve, 3 * h + 3)
                pe.wait_ge(turn_act, h + 1)
                if h:
                    pe.wait_ge(head_dve, h)
                else:
                    pe.wait_ge(cum_act, 2)
                for i in range(NT):
                    for j in range(i + 1):
                        mm = nc.tensor.matmul(head_bank[:, i * HD:(i + 1) * HD],
                                              probsT[h % 2][:, OFF[i] + j * P:OFF[i] + (j + 1) * P],
                                              v_sb[:, g, j, hh * HD:(hh + 1) * HD], start=(j == 0), stop=(j == i))
                mm.then_inc(head_full, 1)

            def turn_pair(m):
                pe.wait_ge(head_dve, 2 * m + 2)
                if m:
                    pe.wait_ge(pair_act, m)
                else:
                    pe.wait_ge(cum_act, 6)
                for t in range(NT):
                    mm = nc.tensor.transpose(misc_bank[:, t * P:(t + 1) * P], osb[m % 2][:, t, :], ident)
                mm.then_inc(pair_full, 1)

            for h in range(NH):
                scores(h)
                if h:
                    weigh_values(h - 1)
                if h <= 1:
                    spread_sums(h + 2)
                for u in FILL[h]:
                    project(u)
                turn_probs(h)
                if h and h % 2 == 0:
                    turn_pair(h // 2 - 1)
            pe.wait_ge(poolw_in, 64)
            for c in range(2):
                pe.wait_ge(pool_ready, c + 1)
                o = start_unit(unit_no(("pool", c)))
                nc.tensor.matmul(o[:, :], pool_wd[:, c, :], pool_u[c][:, 16:528], start=True,
                                 stop=True).then_inc(unit_full, 1)
            weigh_values(NH - 1)
            turn_pair(3)

            def project_out(t, half):
                if t == 0 and half == 0:
                    pe.wait_ge(wo_in, 16)
                    unit_emptied(pe, unit_no(("pool", 0)))
                    unit_emptied(pe, unit_no(("pool", 1)))
                    unit_emptied(pe, unit_no(("cb", 1)))
                    pe.wait_ge(peak_ready, NT * NH)
                    pe.wait_ge(pair_act, 3)
                if t >= 2:
                    pe.wait_ge(wo_free, 2 * (t - 2) + half + 1)
                for k, c in enumerate([0, 1, 4, 5, 2, 6, 7, 3]):
                    if t == 0 and half == 0 and c == 3:
                        pe.wait_ge(pair_act, 4)
                    mm = nc.tensor.matmul(bank[2 * (t % 2) + half][:, :], mixT[:, c, t * P:(t + 1) * P],
                                          o_w[:, c, half * 512:(half + 1) * 512], start=(k == 0),
                                          stop=(k == NC - 1))
                mm.then_inc(wo_full, 1)

            def turn_x1(t):
                for half, emptied in enumerate((x1t_act, x1t_dve)):
                    pe.wait_ge(x1p_ready, 2 * t + half + 1)
                    if t:
                        pe.wait_ge(emptied, t)
                    for c in range(4):
                        mm = nc.tensor.transpose(turn_bank[half][:, c * P:(c + 1) * P], x1p[:, t, 4 * half + c, :],
                                                 ident)
                    mm.then_inc(x1t_full, 1)

            def logits(t):
                for c in range(NC):
                    if c % 4 == 0:
                        pe.wait_ge(x1t_dve if c else x1t_act, t + 1)
                    mm = nc.tensor.matmul(logit_bank[:, E * t:E * t + E], x1T[:, c, t * P:(t + 1) * P],
                                          router_w[:, c, :], start=(c == 0), stop=(c == NC - 1))
                mm.then_inc(logit_full, 1)

            pe.wait_ge(router_in, 32)
            for t in range(NT):
                project_out(t, 0)
                if t:
                    turn_x1(t - 1)
                project_out(t, 1)
                if t:
                    logits(t - 1)
            turn_x1(NT - 1)
            logits(NT - 1)

            pe.wait_ge(chosen_ready, 1)
            pe.wait_ge(tok_ready, 1)
            for t in range(NT):
                for s in range(t + 1):
                    nc.tensor.matmul(count_bank[:, E * t:E * t + E], (upper_b if s == t else ones_b),
                                     chosen_b[:, E * s:E * s + E], start=(s == 0), stop=(s == t))
            for s in range(NT):
                mm = nc.tensor.matmul(count_bank[:, E * NT:E * NT + E], ones_b, chosen_b[:, E * s:E * s + E],
                                      start=(s == 0), stop=(s == NT - 1))
            mm.then_inc(count_full, 1)

            def token_numbers(o, hot):
                for t in range(NT):
                    for k in (0, 1 + t):
                        mm = nc.tensor.matmul(o, hot[:, t, :], tok_b[:, k:k + 1], start=(t == 0 and k == 0),
                                              stop=(t == NT - 1 and k > 0))
                return mm

            def find_rows(e, b):
                pe.wait_ge(onehot_ready, e + 1)
                pe.wait_ge(idx_ready, e)
                token_numbers(idx_bank[0:CAP, 0:1], onehot[b]).then_inc(idx_full, 1)

            def turn_rows(src):
                for c in range(NC):
                    mm = nc.tensor.transpose(xg_bank[c // 4][:, (c % 4) * CAP:(c % 4 + 1) * CAP],
                                             src[0:CAP, c * P:(c + 1) * P], ident[0:CAP, 0:CAP])
                return mm

            def turn_h():
                for c in range(NF):
                    mm = nc.tensor.transpose(h_bank[:, c * CAP:(c + 1) * CAP], act_g[0:CAP, c * P:(c + 1) * P],
                                             ident[0:CAP, 0:CAP])
                return mm

            def times_high(o, b, w, high_ready, n):
                for c in range(NC):
                    if c % 2 == 0:
                        pe.wait_ge(high_ready, n + c // 2 + 1)
                    nc.tensor.matmul(o[0:CAP, :], xH[b][:, c, :], w[:, c, :], start=(c == 0), stop=False)
                    nc.tensor.matmul(o[0:CAP, :], xL[b][:, c, :], w[:, c, :], start=False, stop=False)

            def times_low(o, b, w, low_ready, n):
                for c in range(NC):
                    if c % 2 == 0:
                        pe.wait_ge(low_ready, n + c // 2 + 1)
                    mm = nc.tensor.matmul(o[0:CAP, :], xH[b][:, c, :], w[:, c, :], start=False, stop=(c == NC - 1))
                return mm

            def down_project(b, n):
                for c in range(NF):
                    pe.wait_ge(down_high, n + c + 1)
                    for part in (hH, hL):
                        for half in range(2):
                            nc.tensor.matmul(y_bank[half][0:CAP, :], part[:, c * CAP:(c + 1) * CAP],
                                             down_H[c][:, half * 512:(half + 1) * 512],
                                             start=(c == 0 and part is hH), stop=False)
                for c in range(NF):
                    pe.wait_ge(down_low, n + c + 1)
                    for half in range(2):
                        mm = nc.tensor.matmul(y_bank[half][0:CAP, :], hH[:, c * CAP:(c + 1) * CAP],
                                              down_L[b][:, c, half * 512:(half + 1) * 512],
                                              start=False, stop=(c == NF - 1))
                return mm

            find_rows(0, 0)
            find_rows(1, 1)
            pe.wait_ge(rows_in[0], 16)
            turn_rows(xg[0]).then_inc(xg_full, 1)
            find_rows(2, 0)
            pe.wait_ge(xh_ready, 1)
            pe.wait_ge(xl_ready, 1)
            times_high(g_bank, 0, gate_H, gate_high, 0)
            times_low(g_bank, 0, gate_L[0], gate_low, 0).then_inc(g_full, 1)

            def expert(e, i, b, ahead):
                if ahead >= 1:
                    pe.wait_ge(rows_in[1 - b], i * 16 + 16 * (b + 1))
                    turn_rows(xg[1 - b]).then_inc(xg_full, 1)
                times_high(u_bank, b, up_H, up_high, e * 4)
                times_low(u_bank, b, up_L[b], up_low, e * 4).then_inc(u_full, 1)
                if ahead >= 3:
                    find_rows(e + 3, 1 - b)
                if ahead >= 1:
                    pe.wait_ge(xh_ready, e + 2)
                    pe.wait_ge(xl_ready, e + 2)
                    times_high(g_bank, 1 - b, gate_H, gate_high, e * 4 + 4)
                pe.wait_ge(h_ready, e + 1)
                turn_h().then_inc(turned_h, 1)
                if ahead >= 1:
                    times_low(g_bank, 1 - b, gate_L[1 - b], gate_low, e * 4 + 4).then_inc(g_full, 1)
                pe.wait_ge(hh_ready, e + 1)
                pe.wait_ge(hl_ready, e + 1)
                down_project(b, e * 4).then_inc(y_full, 1)

            experts(pe, expert)

            def more_up(o, w):
                for m in range(NF):
                    for c in range(NC):
                        mm = nc.tensor.matmul(o[:, m * CAP:(m + 1) * CAP], w[:, c, m * P:(m + 1) * P],
                                              more_xT[:, c, :], start=(c == 0), stop=(c == NC - 1))
                return mm

            def more_down(w):
                for c in range(NF):
                    for half in range(2):
                        mm = nc.tensor.matmul(y_bank[half][0:CAP, :], more_hT[:, c * CAP:(c + 1) * CAP],
                                              w[:, c, half * 512:(half + 1) * 512], start=(c == 0), stop=(c == NF - 1))
                return mm

            def more(e, j, n):
                pe.wait_ge(m_step["onehot"], n)
                token_numbers(idx_bank[0:CAP, 0:1], onehot[0]).then_inc(m_step["idx_full"], 1)
                pe.wait_ge(m_step["rows"], n * 16)
                turn_rows(xg[0]).then_inc(m_step["xg_full"], 1)
                pe.wait_ge(m_step["xg"], n)
                pe.wait_ge(m_step["gate_in"], n * 16)
                more_up(g_bank, gate_w[0]).then_inc(m_step["g_full"], 1)
                pe.wait_ge(m_step["up_in"], n * 16)
                more_up(u_bank, up_w[0]).then_inc(m_step["u_full"], 1)
                pe.wait_ge(m_step["down_in"], n * 16)
                pe.wait_ge(m_step["h"], n)
                more_down(down_w[0]).then_inc(m_step["y_full"], 1)
                pe.wait_ge(m_step["y"], n)

            pe.wait_ge(y_ready, E)
            more_chunks(pe, more)

        @block.vector
        def _(dve):
            steps = [0]

            def done(ins):
                steps[0] += 1
                ins.then_inc(dve_step, 1)
                dve.wait_ge(dve_step, steps[0])

            done(nc.vector.memset(eps, EPS))
            done(nc.vector.memset(ones_b, 1.0))
            for n in range(1, NX, 2):
                t = n // 2
                dve.wait_ge(unit_full, n + 1)
                nc.vector.tensor_copy(xT[:, 4:8, t * P:(t + 1) * P],
                                      unit_bank[n % 2][:, :].rearrange("p (c q) -> p c q", c=4)).then_inc(unit_dve, 1)
            dve.wait_ge(fl_full, 1)
            dve.wait_ge(bf_in, 16)
            done(nc.vector.tensor_tensor(z_f.rearrange("p (t h) -> p t h", h=4),
                                         misc_bank[:, 0:16].rearrange("p (t h) -> p t h", h=4),
                                         bf_b.unsqueeze(1).broadcast_to([P, NT, 4]), ALU.add))
            nc.vector.scalar_tensor_tensor(out=az_f, in0=z_f, scalar=-1.0, in1=z_f, op0=ALU.mult,
                                           op1=ALU.max).then_inc(az_ready, 1)
            dve.wait_ge(sp_ready, 1)
            nc.vector.scalar_tensor_tensor(out=ls_f, in0=z_f, scalar=0.0, in1=az_f, op0=ALU.min,
                                           op1=ALU.subtract).then_inc(ls_ready, 1)
            dve.wait_ge(consts_in, 16)
            done(nc.vector.tensor_copy(upper_b, upper[:, 0:P]))
            nc.vector.tensor_copy(tok_b[:, 0:1 + NT], cst[:, C_TOK:C_TOK + 1 + NT]).then_inc(tok_ready, 1)

            def empty_values(u):
                name, half = u
                n = unit_no(u)
                dve.wait_ge(unit_full, n + 1)
                nc.vector.tensor_copy(v_sb[:, "fd".index(name[0]), 2 * half:2 * half + 2, :],
                                      unit_bank[n % 2][:, :].rearrange("p (t c) -> p t c", t=2)).then_inc(unit_dve, 1)

            empty_values(("fv", 0))
            empty_values(("fv", 1))

            def row_peaks(h):
                if h < 4:
                    dve.wait_ge(bias_ready, h + 1)
                else:
                    dve.wait_ge(turn_full, NT * (h - 1))
                for i in range(NT):
                    s = NT * h + i
                    n = (i + 1) * P
                    p = probs[h % 2][:, OFF[i]:OFF[i] + n]
                    dve.wait_ge(score_full, s + 1)
                    nc.vector.tensor_tensor_reduce(out=p, in0=score_bank[s % 2][:, 0:n],
                                                   in1=(p if h < 4 else dil[:, S - n:S]), scale=1.0, scalar=-3.0e38,
                                                   op0=ALU.add, op1=ALU.max,
                                                   accum_out=peak[:, s:s + 1]).then_inc(peak_ready, 1)
                    dve.wait_ge(peak_ready, s + 1)
                    nc.vector.tensor_scalar(npeak[:, s:s + 1], peak[:, s:s + 1], -1.0, None,
                                            ALU.mult).then_inc(npeak_ready, 1)

            def empty_head(h):
                dve.wait_ge(exp_ready, NT * (h + 1))
                done(nc.vector.reciprocal(rtotal[:, NT * h:NT * h + NT], total[:, NT * h:NT * h + NT]))
                dve.wait_ge(head_full, h + 1)
                if h >= 4:
                    dve.wait_ge(pair_full, h // 2 - 1)
                nc.vector.tensor_tensor(osb[(h // 2) % 2][:, :, (h % 2) * HD:(h % 2 + 1) * HD],
                                        head_bank[:, 0:NT * HD].rearrange("p (t n) -> p t n", t=NT),
                                        rtotal[:, NT * h:NT * h + NT].unsqueeze(2).broadcast_to([P, NT, HD]),
                                        ALU.mult).then_inc(head_dve, 1)

            def empty_turned(h):
                for i in range(3):
                    dve.wait_ge(turn_full, NT * h + i + 1)
                    if h >= 2:
                        dve.wait_ge(head_full, h - 1)
                    nc.vector.tensor_copy(probsT[h % 2][:, OFF[i]:OFF[i + 1]],
                                          turn_bank[i % 2][:, 0:(i + 1) * P]).then_inc(turn_dve, 1)

            def convolve(u):
                name, c = u
                n = unit_no(u)
                dve.wait_ge(unit_full, n + 1)
                if name == "ch":
                    if c == 0:
                        dve.wait_ge(pads_ready, 1)
                        dve.wait_ge(chan_in, 16 * 8)
                    dve.wait_ge(unit_act, unit_count(unit_no(("cc", c))))
                    nc.vector.tensor_tensor(conv_u[:, 2:514], unit_bank[n % 2][:, :], conv_c, ALU.mult)\
                        .then_inc(unit_dve, 1)
                    dve.wait_ge(unit_dve, unit_count(n))
                    done(nc.vector.tensor_scalar(conv_c, conv_u[:, 2:514], conv_k[:, c, 2:3], None, ALU.mult))
                    for k in (1, 0):
                        done(nc.vector.scalar_tensor_tensor(out=conv_c, in0=conv_u[:, k:k + S],
                                                            scalar=conv_k[:, c, k:k + 1], in1=conv_c,
                                                            op0=ALU.mult, op1=ALU.add))
                else:
                    nc.vector.tensor_tensor(mixT[:, 4 + c, :], unit_bank[n % 2][:, :], conv_c, ALU.mult)\
                        .then_inc(unit_dve, 1)

            for h in range(NH):
                row_peaks(h)
                if h:
                    empty_head(h - 1)
                for u in FILL[h]:
                    if u[0] == "dv":
                        empty_values(u)
                    elif u[0] in ("ch", "cb"):
                        convolve(u)
                empty_turned(h)
            empty_head(NH - 1)

            def rsqrt_refined(t):
                r = r0[:, t:t + 1]
                done(nc.vector.tensor_scalar(nwt[:, 0:1], devsq[:, t:t + 1], 1.0 / D, EPS, ALU.mult, ALU.add))
                done(nc.vector.scalar_tensor_tensor(out=nwt[:, 1:2], in0=r, scalar=r, in1=nwt[:, 0:1],
                                                    op0=ALU.mult, op1=ALU.mult))
                done(nc.vector.tensor_scalar(nwt[:, 2:3], nwt[:, 1:2], -0.5, 1.5, ALU.mult, ALU.add))
                done(nc.vector.tensor_tensor(rstd[:, t:t + 1], nwt[:, 2:3], r, ALU.mult))

            def empty_x1(t):
                dve.wait_ge(x1t_full, 2 * t + 2)
                nc.vector.tensor_copy(x1T[:, 4:8, t * P:(t + 1) * P],
                                      turn_bank[1][:, :].rearrange("p (c q) -> p c q", c=4)).then_inc(x1t_dve, 1)

            def contraction_order(ap):
                return ap.rearrange("p (q c) -> p c q", c=NC)

            def first_norm(t):
                for half in range(2):
                    cols = slice(half * 512, (half + 1) * 512)
                    dve.wait_ge(wo_full, 2 * t + half + 1)
                    nc.vector.scalar_tensor_tensor(out=x_sb[:, t, cols], in0=x_sb[:, t, cols], scalar=ALPHA,
                                                   in1=bank[2 * (t % 2) + half][:, :], op0=ALU.mult, op1=ALU.add,
                                                   accum_out=rowsum[:, 2 * t + half:2 * t + half + 1])\
                        .then_inc(wo_free, 1)
                    if t and half == 0:
                        empty_x1(t - 1)
                dve.wait_ge(wo_free, 2 * t + 2)
                nc.vector.tensor_scalar(nmean[:, t:t + 1], rowsum[:, 2 * t:2 * t + 1], rowsum[:, 2 * t + 1:2 * t + 2],
                                        -1.0 / D, ALU.add, ALU.mult).then_inc(mean_ready, 1)
                dve.wait_ge(mean_ready, t + 1)
                if t == 0:
                    dve.wait_ge(ln1_in, 32)
                tmp = centred[t % 2]
                done(nc.vector.scalar_tensor_tensor(out=tmp, in0=x_sb[:, t, :], scalar=nmean[:, t:t + 1],
                                                    in1=ln_gb[:, 0, :], op0=ALU.add, op1=ALU.mult))
                dve.wait_ge(rsq_ready, t + 1)
                rsqrt_refined(t)
                for half in range(2):
                    c = slice(4 * half, 4 * half + 4)
                    nc.vector.scalar_tensor_tensor(out=x1p[:, t, c, :], in0=contraction_order(tmp)[:, c, :],
                                                   scalar=rstd[:, t:t + 1],
                                                   in1=contraction_order(ln_gb[:, 1, :])[:, c, :],
                                                   op0=ALU.mult, op1=ALU.add).then_inc(x1p_ready, 1)

            for t in range(NT):
                first_norm(t)
            empty_x1(NT - 1)

            def ranked(dst, src, groups):
                n = 16 * groups
                a, b = cmp_a[:, 0:n], cmp_b[:, 0:n]
                v = src.rearrange("p (g e) -> p g e", e=4)
                other = v.unsqueeze(2).broadcast_to([P, groups, 4, 4])
                own = v.unsqueeze(3).broadcast_to([P, groups, 4, 4])
                a4 = a.rearrange("p (g e j) -> p g e j", e=4, j=4)
                b4 = b.rearrange("p (g e j) -> p g e j", e=4, j=4)
                low = cst[:, C_LOW:C_LOW + 16].unsqueeze(1).broadcast_to([P, groups, 16])
                done(nc.vector.tensor_tensor(a4, other, own, ALU.is_equal))
                done(nc.vector.tensor_tensor(b4, other, own, ALU.is_gt))
                a3 = a.rearrange("p (g k) -> p g k", k=16)
                done(nc.vector.tensor_tensor(a3, a3, low, ALU.mult))
                done(nc.vector.tensor_tensor(a, a, b, ALU.add))
                done(nc.vector.tensor_reduce(dst, a.rearrange("p (g j) -> p g j", j=4), AX.X, ALU.add))

            def by_group(ap):
                return ap.rearrange("p (g e) -> p g e", e=4)

            dve.wait_ge(esig_ready, 1)
            done(nc.vector.tensor_scalar(tmp64, sg, 1.0, None, ALU.add))
            done(nc.vector.reciprocal(sg, tmp64))
            done(nc.vector.tensor_tensor(sel.rearrange("p (t e) -> p t e", e=E), sg.rearrange("p (t e) -> p t e", e=E),
                                         rbias.unsqueeze(1).broadcast_to([P, NT, E]), ALU.add))
            ranked(rank, sel, 16)
            done(nc.vector.tensor_scalar(inpair, rank, 1.5, None, ALU.is_lt))
            done(nc.vector.tensor_tensor(tmp64, inpair, sel, ALU.mult))
            done(nc.vector.tensor_reduce(gscore, by_group(tmp64), AX.X, ALU.add))
            ranked(grank, gscore, NT)
            done(nc.vector.tensor_scalar(grank, grank, 0.5, None, ALU.is_lt))
            best = grank.unsqueeze(2).broadcast_to([P, 16, 4])
            done(nc.vector.tensor_tensor(by_group(chosen), by_group(inpair), best, ALU.mult))
            nc.vector.tensor_copy(chosen_b, chosen).then_inc(chosen_ready, 1)
            dve.wait_ge(count_full, 1)
            done(nc.vector.tensor_tensor(posm, count_bank[:, 0:64], chosen, ALU.mult))
            done(nc.vector.tensor_scalar(posm, posm, -1.0, None, ALU.add))

            def mark_slots(e, hot):
                return nc.vector.tensor_tensor(
                    hot, slots.unsqueeze(1).broadcast_to([P, NT, CAP]),
                    posm.rearrange("p (t e) -> p t e", e=E)[:, :, bass.ds(e, 1)].broadcast_to([P, NT, CAP]),
                    ALU.is_equal)

            def number_rows(e, b):
                dve.wait_ge(idx_full, e + 1)
                nc.vector.tensor_copy(idx[b][0:CAP, :], idx_bank[0:CAP, 0:1]).then_inc(idx_ready, 1)

            def split_quarter(high, w, low, k, high_ready, low_ready, n):
                c = slice(2 * k, 2 * k + 2)
                dve.wait_ge(high_ready, n + k + 1)
                nc.vector.tensor_tensor(low[:, c, :], w[:, c, :], high[:, c, :].bitcast(F32), ALU.subtract)\
                    .then_inc(low_ready, 1)

            def split_rows(e, b):
                dve.wait_ge(xh_ready, e + 1)
                for k in range(2):
                    c = slice(4 * k, 4 * k + 4)
                    ins = nc.vector.tensor_tensor(xL[b][:, c, :], xg_bank[k][:, 0:4 * CAP]
                                                  .rearrange("p (c s) -> p c s", c=4),
                                                  xH[b][:, c, :].bitcast(F32), ALU.subtract)
                ins.then_inc(xl_ready, 1)

            dve.wait_ge(slots_in, 16)
            for b in range(2):
                mark_slots(b, onehot[b]).then_inc(onehot_ready, 1)
            for b in range(2):
                number_rows(b, b)
            done(nc.vector.tensor_reduce(most_f[0:1, :], count_bank[0:1, 64:80], AX.X, ALU.max))
            nc.vector.tensor_copy(most[0:1, :], most_f[0:1, :]).then_inc(most_ready, 1)
            for k in range(4):
                split_quarter(gate_H, gate_w[0], gate_L[0], k, gate_high, gate_low, 0)
            split_rows(0, 0)
            mark_slots(2, onehot[0]).then_inc(onehot_ready, 1)
            number_rows(2, 0)
            for k in range(4):
                split_quarter(up_H, up_w[0], up_L[0], k, up_high, up_low, 0)
            done(nc.vector.tensor_scalar(tmp64, rank, 0.5, None, ALU.is_lt))
            done(nc.vector.tensor_tensor(by_group(first), by_group(tmp64), best, ALU.mult))
            by_tile = lambda ap: ap.rearrange("p (t e) -> p t e", e=E)
            done(nc.vector.tensor_tensor(tmp64, sg, chosen, ALU.mult))
            done(nc.vector.tensor_reduce(gsum, by_tile(tmp64), AX.X, ALU.add))
            done(nc.vector.reciprocal(gsum, gsum))
            done(nc.vector.tensor_scalar(inpair, posm, CAP - 0.5, None, ALU.is_gt))
            done(nc.vector.tensor_tensor(by_tile(inpair), by_tile(inpair),
                                         cst[:, C_ROW + E:C_ROW + 2 * E].unsqueeze(1).broadcast_to([P, NT, E]),
                                         ALU.mult))
            done(nc.vector.tensor_tensor(inpair, inpair, posm, ALU.add))
            done(nc.vector.tensor_tensor(by_tile(inpair), by_tile(inpair),
                                         cst[:, C_ROW:C_ROW + E].unsqueeze(1).broadcast_to([P, NT, E]), ALU.add))
            for k in range(2):
                if k == 1:
                    done(nc.vector.tensor_tensor(first, chosen, first, ALU.subtract))
                done(nc.vector.tensor_tensor(tmp64, sg, first, ALU.mult))
                done(nc.vector.tensor_reduce(gates[:, NT * k:NT * k + NT], by_tile(tmp64), AX.X, ALU.add))
                done(nc.vector.tensor_tensor(gates[:, NT * k:NT * k + NT], gates[:, NT * k:NT * k + NT], gsum,
                                             ALU.mult))
                done(nc.vector.tensor_tensor(tmp64, inpair, first, ALU.mult))
                done(nc.vector.tensor_reduce(yrow_f[:, NT * k:NT * k + NT], by_tile(tmp64), AX.X, ALU.add))
            nc.vector.tensor_copy(yrow, yrow_f).then_inc(yrow_ready, 1)
            base = steps[0]
            PER = 2

            def silu_up(step, n, g, src):
                nc.vector.tensor_scalar(g, g, 1.0, None, ALU.add).then_inc(step, 1)
                dve.wait_ge(step, n + 1)
                nc.vector.reciprocal(g, g).then_inc(step, 1)
                dve.wait_ge(step, n + 2)
                return nc.vector.tensor_tensor(g, src, g, ALU.mult)

            gates_silu = act_g[0:CAP, :]

            def silu(e):
                dve.wait_ge(eg_ready, e + 1)
                silu_up(dve_step, e * PER + base, gates_silu, g_bank[0:CAP, :]).then_inc(silu_ready, 1)

            silu(0)

            def expert(e, i, b, ahead):
                if ahead >= 3:
                    dve.wait_ge(idx_full, e + 2)
                    mark_slots(e + 3, onehot[1 - b]).then_inc(onehot_ready, 1)
                if ahead >= 1:
                    split_rows(e + 1, 1 - b)
                    for k in range(4):
                        split_quarter(gate_H, gate_w[1 - b], gate_L[1 - b], k, gate_high, gate_low, e * 4 + 4)
                dve.wait_ge(u_full, e + 1)
                dve.wait_ge(silu_ready, e + 1)
                nc.vector.tensor_tensor(gates_silu, u_bank[0:CAP, :], gates_silu, ALU.mult).then_inc(h_ready, 1)
                if ahead >= 3:
                    number_rows(e + 3, 1 - b)
                dve.wait_ge(hh_ready, e + 1)
                nc.vector.tensor_tensor(hL[:, :], h_bank[:, 0:NF * CAP], hH[:, :].bitcast(F32), ALU.subtract)\
                    .then_inc(hl_ready, 1)
                if ahead >= 1:
                    for k in range(4):
                        split_quarter(up_H, up_w[1 - b], up_L[1 - b], k, up_high, up_low, e * 4 + 4)
                    silu(e + 1)

            experts(dve, expert)
            steps[0] = base + PER * E

            def more(e, j, n):
                dve.wait_ge(m_step["slots"], n * 16)
                mark_slots(e, onehot[0]).then_inc(m_step["onehot"], 1)
                dve.wait_ge(m_step["idx_full"], n)
                nc.vector.tensor_copy(idx[0][0:CAP, :], idx_bank[0:CAP, 0:1]).then_inc(m_step["idx"], 1)
                dve.wait_ge(m_step["xg_full"], n)
                for k in range(2):
                    ins = nc.vector.tensor_copy(more_xT[:, 4 * k:4 * k + 4, :], xg_bank[k][:, 0:4 * CAP]
                                                .rearrange("p (c s) -> p c s", c=4))
                ins.then_inc(m_step["xg"], 1)
                dve.wait_ge(m_step["eg"], n)
                silu_up(m_step["dve"], n * 3 - 3, more_g, g_bank[:, 0:NF * CAP]).then_inc(m_step["dve"], 1)
                dve.wait_ge(m_step["u_full"], n)
                dve.wait_ge(m_step["dve"], n * 3)
                nc.vector.tensor_tensor(more_hT, u_bank[:, 0:NF * CAP], more_g, ALU.mult).then_inc(m_step["h"], 1)
                dve.wait_ge(m_step["y_full"], n)
                for k in range(2):
                    ins = nc.vector.tensor_copy(y_sb[0:CAP, 512 * k:512 * k + 512], y_bank[k][0:CAP, :])
                ins.then_inc(m_step["y"], 1)

            dve.wait_ge(y_out, 16 * (E + 1))
            more_chunks(dve, more)

            def add_rows(t):
                dve.wait_ge(ya_in[t], 16)
                done(nc.vector.scalar_tensor_tensor(out=ya[t], in0=ya[t], scalar=gates[:, t:t + 1],
                                                    in1=x_sb[:, t, :], op0=ALU.mult, op1=ALU.add))
                dve.wait_ge(yb_in[t], 16)
                done(nc.vector.scalar_tensor_tensor(out=ya[t], in0=yb[t], scalar=gates[:, NT + t:NT + t + 1],
                                                    in1=ya[t], op0=ALU.mult, op1=ALU.add,
                                                    accum_out=rowsum[:, t:t + 1]))
                nc.vector.tensor_scalar(nmean[:, t:t + 1], rowsum[:, t:t + 1], -1.0 / D, None,
                                        ALU.mult).then_inc(fin_mean, 1)

            def shift(t):
                dve.wait_ge(fin_rsq, t + 1)
                rsqrt_refined(t)
                nc.vector.tensor_tensor(nmr[:, t:t + 1], nmean[:, t:t + 1], rstd[:, t:t + 1],
                                        ALU.mult).then_inc(fin_shift, 1)

            def add_b(t):
                dve.wait_ge(fin_g, t + 1)
                nc.vector.tensor_tensor(ya[t], ya[t], ln_gb[:, 1, :], ALU.add).then_inc(fin_ready, 1)

            dve.wait_ge(ax_ready, NT)
            dve.wait_ge(ln2_in, 32)
            last = NT - 1
            for t in range(NT):
                add_rows(t)
                if t:
                    shift(t - 1)
                if t >= 2:
                    add_b(t - 2)
            dve.wait_ge(fin_mean, NT)
            dve.wait_ge(fin_rsq, NT)
            done(nc.vector.scalar_tensor_tensor(out=ya[last], in0=ya[last], scalar=nmean[:, last:NT],
                                                in1=ln_gb[:, 0, :], op0=ALU.add, op1=ALU.mult))
            rsqrt_refined(last)
            add_b(last - 1)
            for half in range(2):
                cols = slice(half * 512, (half + 1) * 512)
                nc.vector.scalar_tensor_tensor(out=ya[last][:, cols], in0=ya[last][:, cols],
                                               scalar=rstd[:, last:NT], in1=ln_gb[:, 1, cols], op0=ALU.mult,
                                               op1=ALU.add).then_inc(fin_ready, 1)

        @block.scalar
        def _(act):
            nc.scalar.preload_act_table_set("natural_log_exp_and_others")
            steps = [0]

            def done(ins):
                steps[0] += 1
                ins.then_inc(act_step, 1)
                act.wait_ge(act_step, steps[0])

            for n in range(0, NX, 2):
                t = n // 2
                act.wait_ge(unit_full, n + 1)
                nc.scalar.copy(xT[:, 0:4, t * P:(t + 1) * P],
                               unit_bank[n % 2][:, :].rearrange("p (c q) -> p c q", c=4)).then_inc(unit_act, 1)
            act.wait_ge(az_ready, 1)
            done(nc.scalar.activation(az_f, az_f, ACT.Exp, scale=-1.0))
            nc.scalar.activation(az_f, az_f, ACT.Ln, bias=1.0).then_inc(sp_ready, 1)

            def empty_unit(u):
                name, half = u
                n = unit_no(u)
                src = unit_bank[n % 2][:, :]
                act.wait_ge(unit_full, n + 1)
                if name in ("fq", "dq"):
                    ins = nc.scalar.mul(qkT[:, 4 * "fd".index(name[0]) + half, :], src, HD ** -0.5)
                elif name in ("fk", "dk"):
                    ins = nc.scalar.copy(qkT[:, 4 * "fd".index(name[0]) + 2 + half, :], src)
                elif name == "cc":
                    if half:
                        unit_emptied(act, unit_no(("cb", 0)))
                    ins = nc.scalar.copy(conv_c, src)
                elif name == "pu":
                    act.wait_ge(pads_ready, 1)
                    ins = nc.scalar.copy(pool_u[half][:, 16:528], src)
                else:
                    act.wait_ge(chan_in, 16 * 8)
                    ins = nc.scalar.mul(mixT[:, 6 + half, :], src, pool_s[:, half:half + 1])
                ins.then_inc(unit_act, 1)

            def empty_sums(k):
                act.wait_ge(cum_full, k + 1)
                if k == 0:
                    ins = nc.scalar.copy(cT, misc_bank[0:4, :])
                elif k == 1:
                    ins = nc.scalar.copy(c_col, head_bank[:, 0:16])
                else:
                    h = k - 2
                    if h >= 2:
                        act.wait_ge(bias_ready, h - 1)
                    ins = nc.scalar.mul(cbc[h % 2], misc_bank[:, :], -1.0)
                ins.then_inc(cum_act, 1)

            for k, u in enumerate(UNITS0):
                if unit_engine(unit_no(u)) == "act":
                    empty_unit(u)
                if k == 1:
                    empty_sums(0)
                if k == 2:
                    empty_sums(1)
                if k == 3:
                    empty_sums(2)
                if k == 5:
                    empty_sums(3)
            for h in range(NH):
                for i in range(NT):
                    s = NT * h + i
                    n = (i + 1) * P
                    p = probs[h % 2][:, OFF[i]:OFF[i] + n]
                    act.wait_ge(npeak_ready, s + 1)
                    nc.scalar.activation(p, p, ACT.Exp, bias=npeak[:, s:s + 1],
                                         accum_out=total[:, s:s + 1]).then_inc(exp_ready, 1)
                if h <= 1:
                    empty_sums(4 + h)
                for u in FILL[h]:
                    if unit_engine(unit_no(u)) == "act":
                        empty_unit(u)
                act.wait_ge(turn_full, NT * (h + 1))
                if h >= 2:
                    act.wait_ge(head_full, h - 1)
                nc.scalar.copy(probsT[h % 2][:, OFF[3]:OFF[3] + NT * P], turn_bank[1][:, :]).then_inc(turn_act, 1)
                if h and h % 2 == 0:
                    m = h // 2 - 1
                    act.wait_ge(pair_full, m + 1)
                    nc.scalar.copy(mixT[:, m, :], misc_bank[:, :]).then_inc(pair_act, 1)
            empty_unit(("pool", 0))
            empty_unit(("pool", 1))
            act.wait_ge(pair_full, 4)
            nc.scalar.copy(mixT[:, 3, :], misc_bank[:, :]).then_inc(pair_act, 1)

            def rsqrt(t, src, junk, signal):
                done(nc.scalar.activation(junk, src, ACT.Square, bias=nmean[:, t:t + 1],
                                          accum_out=devsq[:, t:t + 1]))
                done(nc.scalar.activation(lnv[:, t:t + 1], devsq[:, t:t + 1], ACT.Ln, bias=eps, scale=1.0 / D))
                nc.scalar.activation(r0[:, t:t + 1], lnv[:, t:t + 1], ACT.Exp, scale=-0.5).then_inc(signal, 1)

            def empty_x1(t):
                act.wait_ge(x1t_full, 2 * t + 1)
                nc.scalar.copy(x1T[:, 0:4, t * P:(t + 1) * P],
                               turn_bank[0][:, :].rearrange("p (c q) -> p c q", c=4)).then_inc(x1t_act, 1)

            for t in range(NT):
                if t:
                    empty_x1(t - 1)
                act.wait_ge(mean_ready, t + 1)
                rsqrt(t, x_sb[:, t, :], squares, rsq_ready)
            empty_x1(NT - 1)
            act.wait_ge(logit_full, NT)
            nc.scalar.activation(sg, logit_bank[:, 0:64], ACT.Exp, scale=-1.0).then_inc(esig_ready, 1)

            def split_quarters(e, loaded, count, w, high, high_ready):
                act.wait_ge(loaded, count)
                for k in range(4):
                    c = slice(2 * k, 2 * k + 2)
                    nc.scalar.copy(high[:, c, :], w[:, c, :]).then_inc(high_ready, 1)

            def split_rows(e, b):
                act.wait_ge(xg_full, e + 1)
                for k in range(2):
                    ins = nc.scalar.copy(xH[b][:, 4 * k:4 * k + 4, :], xg_bank[k][:, 0:4 * CAP]
                                         .rearrange("p (c s) -> p c s", c=4))
                ins.then_inc(xh_ready, 1)

            def exp_gates(e):
                act.wait_ge(g_full, e + 1)
                nc.scalar.activation(act_g[0:CAP, :], g_bank[0:CAP, :], ACT.Exp, scale=-1.0).then_inc(eg_ready, 1)

            split_quarters(0, gate_in[0], 16, gate_w[0], gate_H, gate_high)
            split_rows(0, 0)
            act.wait_ge(x1_out, 16 * NT)
            act.wait_ge(ax_ready, NT)
            split_quarters(0, up_in[0], 16, up_w[0], up_H, up_high)
            exp_gates(0)

            def expert(e, i, b, ahead):
                if ahead >= 1:
                    split_rows(e + 1, 1 - b)
                    split_quarters(e + 1, gate_in[1 - b], i * 16 + 16 * (b + 1), gate_w[1 - b], gate_H, gate_high)
                act.wait_ge(down_in[b], i * 16 + 16)
                for c in range(NF):
                    nc.scalar.copy(down_H[c], down_w[b][:, c, :]).then_inc(down_high, 1)
                act.wait_ge(turned_h, e + 1)
                nc.scalar.copy(hH[:, :], h_bank[:, 0:NF * CAP]).then_inc(hh_ready, 1)
                if ahead >= 1:
                    split_quarters(e + 1, up_in[1 - b], i * 16 + 16 * (b + 1), up_w[1 - b], up_H, up_high)
                    exp_gates(e + 1)
                act.wait_ge(y_full, e + 1)
                act.wait_ge(y_out, e * 16 + 16)
                for half in range(2):
                    ins = nc.scalar.copy(y_sb[0:CAP, half * 512:(half + 1) * 512], y_bank[half][0:CAP, :])
                ins.then_inc(y_ready, 1)

            experts(act, expert)

            def more(e, j, n):
                act.wait_ge(m_step["g_full"], n)
                nc.scalar.activation(more_g, g_bank[:, 0:NF * CAP], ACT.Exp, scale=-1.0).then_inc(m_step["eg"], 1)

            more_chunks(act, more)
            for t in range(NT):
                act.wait_ge(fin_mean, t + 1)
                rsqrt(t, ya[t], fin_squares, fin_rsq)
                if t:
                    act.wait_ge(fin_shift, t)
                    nc.scalar.activation(ya[t - 1], ya[t - 1], ACT.Identity, scale=rstd[:, t - 1:t],
                                         bias=nmr[:, t - 1:t]).then_inc(fin_norm, 1)

        @block.gpsimd
        def _(pool):
            steps = [0]

            def done(ins):
                steps[0] += 1
                ins.then_inc(pool_step, 1)
                pool.wait_ge(pool_step, steps[0])

            done(nc.gpsimd.memset(pool_wd, 0.0))
            done(nc.gpsimd.memset(conv_u[:, 0:2], 0.0))
            for c in range(2):
                done(nc.gpsimd.memset(pool_u[c][:, 0:16], 0.0))
            done(nc.gpsimd.memset(pool_a[:, 0:16], 0.0))
            nc.gpsimd.memset(pool_b[:, 0:16], 0.0).then_inc(pads_ready, 1)
            pool.wait_ge(consts_in, 16)
            for h in range(4):
                pool.wait_ge(cum_act, 3 + h)
                if h >= 2:
                    pool.wait_ge(turn_full, NT * (h - 1))
                for i in range(NT):
                    p = probs[h % 2][:, OFF[i]:OFF[i] + (i + 1) * P]
                    done(nc.gpsimd.tensor_scalar(p, cbc[h % 2][:, 0:(i + 1) * P], c_col[:, 4 * i + h:4 * i + h + 1],
                                                 None, ALU.add))
                    ins = nc.gpsimd.tensor_tensor(p[:, i * P:(i + 1) * P], p[:, i * P:(i + 1) * P], tri, ALU.add)
                    if i < NT - 1:
                        done(ins)
                ins.then_inc(bias_ready, 1)

            def doubled(dst, src, w, rows=slice(0, P)):
                done(nc.gpsimd.tensor_tensor(dst[rows, 16:528], src[rows, 16:528], src[rows, 16 - w:528 - w], ALU.add))

            rc = cst[:, C_POOL:C_POOL + 32].rearrange("p (c k) -> p c k", c=2)
            low, high = slice(0, 64), slice(64, P)
            for c in range(2):
                pool.wait_ge(unit_act, unit_count(unit_no(("pu", c))))
                doubled(pool_a, pool_u[c], 1)
                if c == 0:
                    doubled(pool_b, pool_a, 2, high)
                else:
                    doubled(pool_b, pool_a, 2)
                    doubled(pool_a, pool_b, 4)
                    doubled(pool_b, pool_a, 8, high)
                for rows, sums in ((low, pool_a), (high, pool_b)):
                    done(nc.gpsimd.tensor_tensor(sums[rows, 16:32], sums[rows, 16:32], rc[rows, c, :], ALU.mult))
                    done(nc.gpsimd.tensor_scalar(sums[rows, 32:528], sums[rows, 32:528],
                                                 cst[rows, C_POOL + 32 + c:C_POOL + 33 + c], None, ALU.mult))
                    ins = nc.gpsimd.tensor_tensor(pool_u[c][rows, 16:528], sums[rows, 16:528],
                                                  pool_u[c][rows, 16:528], ALU.subtract)
                    if rows is low:
                        done(ins)
                ins.then_inc(pool_ready, 1)
                pool.wait_ge(pool_ready, c + 1)

            def wait_apart(signal, value):
                pool.wait_ge(signal, value)
                pool.sem_inc(gathers_begun, 1)

            def gather(dst, rows, numbers, signal):
                nc.gpsimd.indirect_dma_start(dst, None, rows, bass.IndirectOffsetOnAxis(ap=numbers, axis=0))\
                    .then_inc(signal, 16)

            for t in range(NT):
                pool.wait_ge(x1p_ready, 2 * t + 2)
                nc.gpsimd.tensor_scalar(x_sb[:, t, :].rearrange("p (q c) -> p c q", c=NC), x1p[:, t], ALPHA, None,
                                        ALU.mult).then_inc(ax_ready, 1)
            pool.wait_ge(x1_out, 16 * NT)
            for b in range(2):
                pool.wait_ge(idx_ready, b + 1)
                gather(xg[b][0:CAP, :], x1_rows, idx[b][0:CAP, :], rows_in[b])
            pool.wait_ge(idx_ready, 3)
            pool.wait_ge(xg_full, 1)
            gather(xg[0][0:CAP, :], x1_rows, idx[0][0:CAP, :], rows_in[0])

            def expert(e, i, b, ahead):
                for c in range(NF):
                    if c == 2 and ahead >= 3:
                        wait_apart(idx_ready, e + 4)
                        wait_apart(xg_full, e + 2)
                        gather(xg[1 - b][0:CAP, :], x1_rows, idx[1 - b][0:CAP, :], rows_in[1 - b])
                    pool.wait_ge(down_high, e * 4 + c + 1)
                    nc.gpsimd.tensor_tensor(down_L[b][:, c, :], down_w[b][:, c, :], down_H[c].bitcast(F32),
                                            ALU.subtract).then_inc(down_low, 1)

            experts(pool, expert)

            def more(e, j, n):
                wait_apart(m_step["idx"], n)
                gather(xg[0][0:CAP, :], x1_rows, idx[0][0:CAP, :], m_step["rows"])
                pool.wait_ge(m_step["out"], n * 16)

            pool.wait_ge(y_out, 16 * (E + 1))
            peak_rows = more_chunks(pool, more)

            pool.wait_ge(yrow_ready, 1)

            for ran, rows in ((peak_rows > CAP, y_rows), (peak_rows <= CAP, y_rows[0:MAIN, :])):
                with pool.If(ran):
                    for t in range(NT):
                        gather(ya[t], rows, yrow[:, t:t + 1], ya_in[t])
                        gather(yb[t], rows, yrow[:, NT + t:NT + t + 1], yb_in[t])
            for t in range(NT - 1):
                pool.wait_ge(fin_norm, t + 1)
                nc.gpsimd.tensor_tensor(ya[t], ya[t], ln_gb[:, 0, :], ALU.mult).then_inc(fin_g, 1)


_INS = ["x", "w_in", "b_f", "conv_w", "pool_w", "pool_scale", "w_o", "ln1_g", "ln1_b", "w_router", "router_bias",
        "w_gate", "w_up", "w_down", "ln2_g", "ln2_b"]


def kernel(**inputs):
    import numpy as _np
    import concourse.bacc as _bacc
    from concourse import mybir as _mybir
    from concourse.bass_utils import run_bass_kernel_spmd as _run

    nc = _bacc.Bacc("TRN2", target_bir_lowering=False, num_devices=1)
    arrays, args = {}, []
    given = [(n, _np.ascontiguousarray(inputs[n])) for n in _INS]
    given += list(zip(["consts", "selectors", "slot_numbers"], constants()))
    for name, a in given:
        arrays[f"in_{name}_dram"] = a
        args.append(nc.dram_tensor(f"in_{name}_dram", a.shape, _mybir.dt.from_np(a.dtype), kind="ExternalInput").ap())
    out = nc.dram_tensor("out_0_dram", (1, S, D), F32, kind="ExternalOutput").ap()
    build(nc, *args, out)
    r = _run(nc, [arrays], core_ids=[0])
    return r.results[0]["out_0_dram"]
```

```python
from contextlib import ExitStack

import numpy as np
import concourse.bass as bass
from concourse import mybir

F32 = mybir.dt.float32
F32R = mybir.dt.float32r
BF16 = mybir.dt.bfloat16
I32 = mybir.dt.int32
U32 = mybir.dt.uint32
ALU = mybir.AluOpType
ACT = mybir.ActivationFunctionType
AX = mybir.AxisListType

P = 128
S = 512
D = 1024
NT = S // P
NC = D // P
HD = D // 16
GW = 4 * HD
NH = 8
E = 16
F = D // 2
NF = F // P
CAP = 96
CHUNKS = -(-S // CAP)
EROWS = CHUNKS * CAP
MAIN = (E - 1) * CAP
ROUNDS = E * (CHUNKS - 1)
PATTERNS = ((128, 1), (512, 4), (2048, 16))
WINDOWS = (2, 4, 8, 16)
ALPHA = 2.0 ** 0.25
EPS = 1e-5
NEG = -1e30
OFF = [P * (i * (i + 1) // 2) for i in range(NT)]
PROBS = P * (NT * (NT + 1) // 2)

BLOCKS = ["fq", "fk", "fv", "dq", "dk", "dv", "pu", "cc", "ch", "cb"]
BLOCK_COL = dict(fq=0, fk=1, fv=2, dq=3, dk=4, dv=5, cb=6, cc=7, ch=8, pu=9)
NSLOT = 4
UNITS0 = [("fq", 0), ("fq", 1), ("fk", 0), ("fk", 1), ("fv", 0), ("fv", 1)]
FILL = [[("dq", 0), ("dq", 1)], [("dk", 0), ("dk", 1)], [("dv", 0), ("dv", 1)], [("pu", 0), ("pu", 1)],
        [("cc", 0), ("ch", 0)], [("cb", 0), ("cc", 1)], [("ch", 1), ("cb", 1)], []]
UNITS = UNITS0 + [u for f in FILL for u in f] + [("pool", 0), ("pool", 1)]
NX = 2 * NT
ON_DVE = ("fv", "dv", "ch", "cb")


def unit_engine(n):
    if n < NX:
        return "dve"
    return "dve" if UNITS[n - NX][0] in ON_DVE else "act"


def unit_count(n):
    return sum(unit_engine(m) == unit_engine(n) for m in range(n + 1))


def unit_no(u):
    return NX + UNITS.index(u)


PIECES = [u for u in UNITS if u[0] != "pool"]
NPIECE = 4


MIX_ORDER = [0, 1, 2, 4, 5, 6, 7, 3]


def last_unit_of(k):
    name = PIECES[k][0]
    return unit_no((name, 1)) if name in ("fv", "dv") else unit_no(PIECES[k])


def piece_of(ap, k):
    name, half = PIECES[k]
    return ap[:, 4 * half:4 * half + 4, :] if name in ("fv", "dv") else ap[:, :, half * P:(half + 1) * P]


C_IDENT = 0
C_TRI = C_IDENT + P
C_DIL = C_TRI + P
C_UP = C_DIL + S
C_POOL = C_UP + S
C_LOW = C_POOL + 34
C_ROW = C_LOW + 16
C_TOK = C_ROW + 2 * E
NCONST = C_TOK + 1 + NT


def constants():
    c = np.zeros((P, NCONST), np.float32)
    q, k = np.arange(P)[:, None], np.arange(P)[None, :]
    c[:, C_IDENT:C_IDENT + P] = q == k
    c[:, C_TRI:C_TRI + P] = np.where(k <= q, 0.0, NEG)
    for b in range(NT):
        dist = q + P * (NT - 1 - b) - k
        n = sum(((dist >= 0) & (dist % r == 0) & (dist // r <= w // r)).astype(np.int64) for w, r in PATTERNS)
        c[:, C_DIL + P * b:C_DIL + P * (b + 1)] = np.where(n > 0, np.log(np.maximum(n, 1)), NEG)
    c[:, C_UP:C_UP + S] = np.arange(S)[None, :] >= q
    for t in range(2):
        for half in range(2):
            w = WINDOWS[2 * t + half]
            rows = slice(64 * half, 64 * half + 64)
            c[rows, C_POOL + 16 * t:C_POOL + 16 * t + 16] = 1.0 / np.minimum(np.arange(16) + 1, w)
            c[rows, C_POOL + 32 + t] = 1.0 / w
    c[:, C_LOW:C_LOW + 16] = (np.arange(4)[None, :] < np.arange(4)[:, None]).reshape(1, 16)
    c[:, C_ROW:C_ROW + E] = CAP * np.arange(E)
    c[:, C_ROW + E:C_ROW + 2 * E] = np.arange(E) < E - 1
    c[:, C_TOK] = np.arange(P)
    c[:, C_TOK + 1:C_TOK + 1 + NT] = P * np.arange(NT)
    selectors = np.repeat(np.eye(4, dtype=np.float32), P, axis=1)
    return c, selectors, np.broadcast_to(np.arange(EROWS, dtype=np.float32), (P, EROWS)).copy()


def build(nc, x, w_in, b_f, conv_w, pool_w, pool_scale, w_o, ln1_g, ln1_b, w_router, router_bias,
          w_gate, w_up, w_down, ln2_g, ln2_b, consts, selectors, slot_numbers, out):
    x1_rows = nc.dram_tensor("x1_rows", [S, D], F32, kind="Internal").ap()
    y_rows = nc.dram_tensor("y_rows", [MAIN, D], F32, kind="Internal").ap()

    x_v = x.rearrange("a (t p) d -> (a t) p d", p=P)
    out_v = out.rearrange("a (t p) d -> (a t) p d", p=P)
    w_in_v = w_in.rearrange("l (c p) n -> p (l c) n", p=P)
    w_o_v = w_o.rearrange("l (c p) n -> p (l c) n", p=P)
    w_gate_v = w_gate.rearrange("l e (p c) n -> (l e) p (c n)", c=NC)
    w_up_v = w_up.rearrange("l e (p c) n -> (l e) p (c n)", c=NC)
    w_down_v = w_down.rearrange("l e (c p) n -> (l e) p c n", p=P)
    w_router_v = w_router.rearrange("(p c) n -> p c n", c=NC)
    x1_rows_v = x1_rows.rearrange("(t p) d -> t p d", p=P)

    with ExitStack() as ctx:
        start = {}

        def sb(name, shape, dt=F32):
            region = ctx.enter_context(nc.sbuf_tensor(name, shape, dt))
            start[name] = nc.sbuf_base - 4 * int(np.prod(shape[1:]))
            return region

        def rounded(name, region, first, n):
            return nc.alloc_sbuf_tensor_at(name, [P, n], F32R, offset=start[region] + 4 * first)

        def sem(name):
            return ctx.enter_context(nc.semaphore(name))

        WREG = NC * F
        wbuf = sb("wbuf", [P, 6 * WREG])
        x_sb = sb("x_sb", [P, NT, D])
        ln_gb = sb("ln_gb", [P, 2, D])
        heads_region = sb("heads_region", [P, NH * S])
        v_region = sb("v_region", [P, 2 * NT * GW])
        probs_region = sb("probs_region", [P, 4 * PROBS])
        cbc_region = sb("cbc_region", [P, 2 * S])
        mix_region = sb("mix_region", [P, NC * S])
        local_region = sb("local_region", [P, 2082])
        osb_region = sb("osb_region", [P, 2 * NT * P])
        cst = sb("cst", [P, NCONST])
        small = sb("small", [P, 1492])

        gate_w = [wbuf[:, 3 * b * WREG:(3 * b + 1) * WREG].rearrange("p (c n) -> p c n", c=NC) for b in range(2)]
        up_w = [wbuf[:, (3 * b + 1) * WREG:(3 * b + 2) * WREG].rearrange("p (c n) -> p c n", c=NC) for b in range(2)]
        down_w = [wbuf[:, (3 * b + 2) * WREG:(3 * b + 3) * WREG].rearrange("p (c n) -> p c n", c=NF)
                  for b in range(2)]
        low_w = rounded("low_w", "wbuf", 0, 6 * WREG)
        in_w = [wbuf[:, s * NC * GW:(s + 1) * NC * GW].rearrange("p (c n) -> p c n", c=NC) for s in range(NSLOT)]
        in_L = [low_w[:, s * NC * GW:(s + 1) * NC * GW].rearrange("p (c n) -> p c n", c=NC) for s in range(NSLOT)]
        in_H_ring = rounded("in_H", "wbuf", 2 * WREG, NPIECE * NC * P)
        o_w = wbuf[:, 3 * WREG:5 * WREG].rearrange("p (c n) -> p c n", c=NC)
        xT_H = rounded("xT_H", "wbuf", 5 * WREG, NC * S)[:, :].rearrange("p (t c q) -> p t c q", t=NT, c=NC)
        xT_L = rounded("xT_L", "x_sb", 0, NC * S)[:, :].rearrange("p (t c q) -> p t c q", t=NT, c=NC)

        def in_H(k):
            h = in_H_ring[:, (k % NPIECE) * NC * P:(k % NPIECE + 1) * NC * P]
            return h.rearrange("p (c n) -> p c n", c=4 if PIECES[k][0] in ("fv", "dv") else NC)

        def slot_of(k):
            return BLOCKS.index(PIECES[k][0]) % NSLOT

        qkT = heads_region[:, :].rearrange("p (m s) -> p m s", m=NH)
        v_sb = v_region[:, :].rearrange("p (g t n) -> p g t n", g=2, t=NT)
        probs = [probs_region[:, b * PROBS:(b + 1) * PROBS] for b in range(2)]
        probsT = [probs_region[:, (2 + b) * PROBS:(3 + b) * PROBS] for b in range(2)]
        cbc = [cbc_region[:, b * S:(b + 1) * S] for b in range(2)]
        mixT = mix_region[:, :].rearrange("p (c s) -> p c s", c=NC)
        osb = [osb_region[:, b * NT * P:(b + 1) * NT * P].rearrange("p (t n) -> p t n", t=NT) for b in range(2)]
        conv_c = local_region[:, 0:512]
        conv_u = local_region[:, 512:512 + 514]
        pool_u = [local_region[:, 1026 + 528 * c:1554 + 528 * c] for c in range(2)]
        pool_a, pool_b = ln_gb[:, 0, 0:528], ln_gb[:, 1, 0:528]
        cT = mix_region[0:4, 2 * S:3 * S]
        select_head = mix_region[0:4, 3 * S:4 * S]

        mix_H = rounded("mix_H", "heads_region", 0, NC * S)[:, :].rearrange("p (c s) -> p c s", c=NC)
        mix_L = rounded("mix_L", "mix_region", 0, NC * S)[:, :].rearrange("p (c s) -> p c s", c=NC)
        o_L = low_w[:, 3 * WREG:5 * WREG].rearrange("p (c n) -> p c n", c=NC)
        o_H0 = rounded("o_H0", "wbuf", 5 * WREG, WREG)
        o_H1 = [rounded(f"o_H1_{c}", *place, 512) for c, place in enumerate(
            [("local_region", 512 * c) for c in range(4)]
            + [("cst", C_TRI), ("cst", C_TRI + 512), ("cbc_region", 512), ("probs_region", WREG)])]
        o_H = [[o_H0[:, 512 * c:512 * (c + 1)] for c in range(NC)], [w[:, :] for w in o_H1]]

        def x1p(t, half):
            if t == NT - 1:
                return v_region[:, 512 * half:512 * (half + 1)].rearrange("p (c q) -> p c q", c=4)
            return o_w[:, 2 * t + half, 0:512].rearrange("p (c q) -> p c q", c=4)

        x1T = probs_region[:, 0:NC * S].rearrange("p (c s) -> p c s", c=NC)
        xg = [v_region[:, b * D:(b + 1) * D] for b in range(2)]
        y_sb = mix_region[:, 0:D]
        slots = cbc_region[:, 0:CAP]
        onehot = [cbc_region[:, CAP + b * 2 * CAP:CAP + (b + 1) * 2 * CAP].bitcast(BF16)
                  .rearrange("p (t s) -> p t s", t=NT) for b in range(2)]
        act_g = local_region[:, 2 * NC * CAP:2 * NC * CAP + F]
        xH = [rounded(f"xH{b}", "local_region", b * NC * CAP, NC * CAP)[:, :].rearrange("p (c s) -> p c s", c=NC)
              for b in range(2)]
        hH = rounded("hH", "cbc_region", 5 * CAP, NF * CAP)
        gate_H = rounded("gate_H", "heads_region", 0, WREG)[:, :].rearrange("p (c n) -> p c n", c=NC)
        up_H = rounded("up_H", "probs_region", 0, WREG)[:, :].rearrange("p (c n) -> p c n", c=NC)
        down_H012 = rounded("down_H012", "mix_region", D, 3 * D)
        down_H3 = rounded("down_H3", "probs_region", WREG, D)
        down_H = [down_H012[:, c * D:(c + 1) * D] for c in range(3)] + [down_H3[:, :]]
        first_gate_L = [down_H[k].rearrange("p (c n) -> p c n", c=2) for k in range(4)]
        xL = [rounded(f"xL{b}", *place, NC * CAP)[:, :].rearrange("p (c s) -> p c s", c=NC)
              for b, place in enumerate([("osb_region", 0), ("cst", C_TRI)])]
        hL = rounded("hL", "cst", C_TRI + NC * CAP, NF * CAP)
        gate_L = [low_w[:, 3 * b * WREG:(3 * b + 1) * WREG].rearrange("p (c n) -> p c n", c=NC) for b in range(2)]
        up_L = [low_w[:, (3 * b + 1) * WREG:(3 * b + 2) * WREG].rearrange("p (c n) -> p c n", c=NC)
                for b in range(2)]
        down_L = [low_w[:, (3 * b + 2) * WREG:(3 * b + 3) * WREG].rearrange("p (c n) -> p c n", c=NF)
                  for b in range(2)]
        hot = v_region[:, D + S:D + S + NT * CAP].rearrange("p (t s) -> p t s", t=NT)
        hotT = rounded("hotT", "v_region", D, S)
        last_yH = rounded("last_yH", "mix_region", 0, D)
        last_yL = rounded("last_yL", "mix_region", D, D)
        more_hot = mix_region[:, 3 * D + S:3 * D + S + NT * CAP].rearrange("p (t s) -> p t s", t=NT)
        more_hotT = rounded("more_hotT", "mix_region", 3 * D, S)
        more_yH = rounded("more_yH", "mix_region", 2 * D, D)
        more_yL = rounded("more_yL", "probs_region", WREG, D)
        more_xT = local_region[:, 0:NC * CAP].rearrange("p (c s) -> p c s", c=NC)
        more_g = local_region[:, 768:768 + NF * CAP]
        more_hT = local_region[:, 1152:1152 + NF * CAP]
        centred = [v_region[:, b * D:(b + 1) * D] for b in range(2)]
        squares = osb_region[:, 0:D]
        ya = [wbuf[:, t * D:(t + 1) * D] for t in range(NT)]
        yb = [wbuf[:, (NT + t) * D:(NT + t + 1) * D] for t in range(NT)]
        fin_squares = wbuf[:, 2 * NT * D:(2 * NT + 1) * D]
        add_banks = [(0, 1), (2, 3), (6, 7), (4, 5)]

        ident = cst[:, C_IDENT:C_IDENT + P]
        tri = cst[:, C_TRI:C_TRI + P]
        dil = cst[:, C_DIL:C_DIL + S]
        upper = cst[:, C_UP:C_UP + S]

        at = [0]

        def piece(n):
            at[0] += n
            return small[:, at[0] - n:at[0]]

        w_f = piece(NC * 4).rearrange("p (c n) -> p c n", c=NC)
        at[0] += NC * 8
        wf_parts = rounded("wf_parts", "small", NC * 4, NC * 8)[:, :].rearrange("p (c n) -> p c n", c=NC)
        bf_b = piece(4)
        conv_k = piece(6).rearrange("p (c k) -> p c k", c=2)
        pool_s = piece(2)
        pool_wd = piece(2 * P).rearrange("p (c n) -> p c n", c=2)
        router_w = piece(NC * E).rearrange("p (c n) -> p c n", c=NC)
        rbias = piece(E)
        eps = piece(1)
        z_f = piece(16)
        az_f = piece(16)
        ls_f = piece(16)
        c_col = piece(16)
        peak = piece(4 * NH)
        npeak = piece(4 * NH)
        total = piece(4 * NH)
        rtotal = piece(4 * NH)
        rowsum = piece(2 * NT)
        nmean = piece(NT)
        devsq = piece(NT)
        lnv = piece(NT)
        r0 = piece(NT)
        nwt = piece(4)
        rstd = piece(NT)
        nmr = piece(NT)
        sg = piece(64)
        sel = piece(64)
        rank = piece(64)
        inpair = piece(64)
        chosen = piece(64)
        first = piece(64)
        tmp64 = piece(64)
        posm = piece(64)
        gscore = piece(16)
        grank = piece(16)
        gates = piece(2 * NT)
        gsum = piece(NT)
        gate_all = sel
        more_gate = z_f[:, 0:NT]
        yrow_f = piece(2 * NT)
        yrow = piece(2 * NT).bitcast(U32)
        idx = [piece(1).bitcast(U32) for _ in range(2)]
        most_f = piece(1)
        most = piece(1).bitcast(I32)
        at[0] += at[0] % 2
        chosen_b = piece(32).bitcast(BF16)
        upper_b = piece(64).bitcast(BF16)
        ones_b = piece(64).bitcast(BF16)
        tok_b = piece(4).bitcast(BF16)
        cmp_a = osb_region[:, 512:768]
        cmp_b = osb_region[:, 768:1024]

        bank = [ctx.enter_context(nc.psum_tensor(f"bank{b}", [P, 512], F32)) for b in range(8)]
        unit_bank = bank[0:2]
        score_bank = bank[2:4]
        turn_bank = bank[4:6]
        head_bank = bank[6]
        misc_bank = bank[7]
        logit_bank = bank[6]
        count_bank = bank[7]
        g_bank, u_bank, xg_bank, y_bank, idx_bank, h_bank = bank[0], bank[1], bank[2:4], bank[4:6], bank[6], bank[7]

        x_in = [sem(f"x_in{t}") for t in range(NT)]
        ident_in, wf_in, consts_in, select_in = sem("ident_in"), sem("wf_in"), sem("consts_in"), sem("select_in")
        chan_in, router_in = sem("chan_in"), sem("router_in")
        poolw_in, ln1_in, ln2_in, slots_in, wo_in = (sem("poolw_in"), sem("ln1_in"), sem("ln2_in"), sem("slots_in"),
                                                     sem("wo_in"))
        block_in = [sem(f"block_in{b}") for b in range(NSLOT)]
        gate_in = [sem(f"gate_in{b}") for b in range(2)]
        up_in = [sem(f"up_in{b}") for b in range(2)]
        down_in = [sem(f"down_in{b}") for b in range(2)]
        xt_high, wf_high, wf_low, in_high, in_low = (sem("xt_high"), sem("wf_high"), sem("wf_low"), sem("in_high"),
                                                     sem("in_low"))
        unit_full, unit_act, unit_dve = sem("unit_full"), sem("unit_act"), sem("unit_dve")
        fl_full, az_ready, sp_ready, ls_ready = sem("fl_full"), sem("az_ready"), sem("sp_ready"), sem("ls_ready")
        cum_full, cum_act = sem("cum_full"), sem("cum_act")
        bias_ready = sem("bias_ready")
        score_full, peak_ready, exp_ready = sem("score_full"), sem("peak_ready"), sem("exp_ready")
        turn_full, turn_dve, turn_act = sem("turn_full"), sem("turn_dve"), sem("turn_act")
        head_full, head_dve = sem("head_full"), sem("head_dve")
        pair_full, pair_act = sem("pair_full"), sem("pair_act")
        pads_ready, pool_ready = sem("pads_ready"), sem("pool_ready")
        wo_full, wo_free = sem("wo_full"), sem("wo_free")
        mean_ready, rsq_ready, x1p_ready = sem("mean_ready"), sem("rsq_ready"), sem("x1p_ready")
        x1_out = [sem(f"x1_out{t}") for t in range(NT)]
        mix_high, mix_low, o_high, o_low, o_low_last = (sem("mix_high"), sem("mix_low"), sem("o_high"), sem("o_low"),
                                                        sem("o_low_last"))
        x1t_full, x1t_act = sem("x1t_full"), sem("x1t_act")
        logit_full, esig_ready, chosen_ready, count_full = (sem("logit_full"), sem("esig_ready"),
                                                            sem("chosen_ready"), sem("count_full"))
        tok_ready, yrow_ready, most_ready, ax_ready, ax_last = (sem("tok_ready"), sem("yrow_ready"), sem("most_ready"),
                                                                sem("ax_ready"), sem("ax_last"))
        onehot_ready, idx_full, idx_ready = sem("onehot_ready"), sem("idx_full"), sem("idx_ready")
        rows_in = [sem(f"rows_in{b}") for b in range(2)]
        xg_full, xh_ready, xl_ready = sem("xg_full"), sem("xh_ready"), sem("xl_ready")
        gate_high, gate_low, up_high, up_low, up_low_last, down_high, down_low = (
            sem("gate_high"), sem("gate_low"), sem("up_high"), sem("up_low"), sem("up_low_last"), sem("down_high"),
            sem("down_low"))
        g_full, eg_ready, silu_ready, u_full, h_ready = (sem("g_full"), sem("eg_ready"), sem("silu_ready"),
                                                         sem("u_full"), sem("h_ready"))
        u_low_used = sem("u_low_used")
        turned_h, hh_ready, hl_ready = sem("turned_h"), sem("hh_ready"), sem("hl_ready")
        y_full, y_ready, y_out = sem("y_full"), sem("y_ready"), sem("y_out")
        hot_ready, hot_turned, hot_act = sem("hot_ready"), sem("hot_turned"), sem("hot_act")
        last_high, last_low, last_full, acc_ready = (sem("last_high"), sem("last_low"), sem("last_full"),
                                                     sem("acc_ready"))
        m_step = {n: sem(f"more_{n}") for n in ("onehot", "idx_full", "idx", "rows", "xg_full", "xg", "g_full", "eg",
                                                "u_full", "h", "y_full", "weights", "dve", "slots",
                                                "turned", "hotT", "high", "low", "full", "read", "added", "gate")}
        y_in = [sem(f"y_in{t}") for t in range(NT)]
        fin_shift, fin_norm, fin_pool, fin_ready = sem("fin_shift"), sem("fin_norm"), sem("fin_pool"), sem("fin_ready")
        out_done = [sem(f"out_done{k}") for k in range(NT)]
        scaled_g = sem("scaled_g")
        gate_step, first_scaled, first_added = sem("gate_step"), sem("first_scaled"), sem("first_added")
        dve_step, act_step, pool_step = sem("dve_step"), sem("act_step"), sem("pool_step")
        npeak_ready = sem("npeak_ready")
        gathers_begun = sem("gathers_begun")

        def unit_emptied(eng, n):
            eng.wait_ge(unit_act if unit_engine(n) == "act" else unit_dve, unit_count(n))

        def experts(eng, body):
            body(0, 0, 0, 4)
            body(1, 0, 1, 3)
            with eng.Fori(1, E // 2 - 2) as i:
                for b in range(2):
                    body(i * 2 + b, i, b, 3)
            for e in range(E - 4, E):
                body(e, e // 2, e % 2, min(3, E - 1 - e))

        def load_peak(eng):
            eng.wait_ge(most_ready, 1)
            return eng.value_load(most[0:1, :], min_val=0, max_val=S)

        def more_chunks(eng, peak_rows, body, after=None, before=None, otherwise=None):
            if otherwise:
                with eng.If(peak_rows <= CAP):
                    otherwise()
            with eng.If(peak_rows > CAP):
                if before:
                    before()
                with eng.Fori(0, E) as e:
                    with eng.Fori(1, CHUNKS) as j:
                        body(e, j, e * (CHUNKS - 1) + j)
                if after:
                    after()

        block = ctx.enter_context(nc.Block())

        @block.sync
        def _(sp):
            for t in range(NT):
                sp.dma_start(x_sb[:, t, :], x_v[t]).then_inc(x_in[t], 16)
                if t == 0:
                    sp.dma_start(ident, consts[:, C_IDENT:C_IDENT + P]).then_inc(ident_in, 16)
            sp.dma_start(w_f, w_in_v[:, :, 10 * GW:10 * GW + 4]).then_inc(wf_in, 16)
            sp.dma_start(bf_b, b_f.broadcast_to([P, 4])).then_inc(wf_in, 16)

            def load_block(n):
                col = BLOCK_COL[BLOCKS[n]] * GW
                sp.dma_start(in_w[n % NSLOT], w_in_v[:, :, col:col + GW])\
                    .then_inc(block_in[n % NSLOT], 16)

            def block_multiplied(n):
                sp.wait_ge(unit_full, unit_no((BLOCKS[n], 1)) + 1)

            load_block(0)
            load_block(1)
            sp.dma_start(select_head, selectors).then_inc(select_in, 16)
            sp.dma_start(cst[:, P:], consts[:, P:]).then_inc(consts_in, 16)
            for n in range(2, NSLOT):
                load_block(n)
            for c in range(2):
                for k in range(3):
                    sp.dma_start(conv_k[:, c, k:k + 1],
                                 conv_w[0, k, c * P:(c + 1) * P].rearrange("(p a) -> p a", a=1)).then_inc(chan_in, 16)
                sp.dma_start(pool_s[:, c:c + 1],
                             pool_scale[0, c * P:(c + 1) * P].rearrange("(p a) -> p a", a=1)).then_inc(chan_in, 16)
            sp.wait_ge(pads_ready, 1)
            for g in range(4):
                r = 64 * (g % 2)
                sp.dma_start(pool_wd[r:r + 64, g // 2, r:r + 64], pool_w[0, g]).then_inc(poolw_in, 16)
            sp.dma_start(router_w, w_router_v).then_inc(router_in, 16)
            sp.dma_start(rbias, router_bias.rearrange("(a n) -> a n", a=1).broadcast_to([P, E]))\
                .then_inc(router_in, 16)
            for n in range(NSLOT, len(BLOCKS)):
                block_multiplied(n - NSLOT)
                load_block(n)
            sp.dma_start(o_w, w_o_v).then_inc(wo_in, 16)
            sp.wait_ge(pool_ready, 2)
            sp.dma_start(ln_gb[:, 0, :], ln1_g.broadcast_to([P, D])).then_inc(ln1_in, 16)
            sp.dma_start(ln_gb[:, 1, :], ln1_b.broadcast_to([P, D])).then_inc(ln1_in, 16)
            block_multiplied(len(BLOCKS) - 1)
            for t in range(NT):
                sp.dma_start(x_sb[:, t, :], x_v[t]).then_inc(x_in[t], 16)
            sp.dma_start(gate_w[0].rearrange("p c n -> p (c n)"), w_gate_v[0]).then_inc(gate_in[0], 16)
            sp.dma_start(up_w[0].rearrange("p c n -> p (c n)"), w_up_v[0]).then_inc(up_in[0], 16)
            sp.dma_start(down_w[0], w_down_v[0]).then_inc(down_in[0], 16)
            sp.wait_ge(wo_full, 1)
            sp.dma_start(slots, slot_numbers[:, 0:CAP]).then_inc(slots_in, 16)
            sp.wait_ge(wo_full, NT)
            sp.dma_start(down_w[1], w_down_v[1]).then_inc(down_in[1], 16)

            def keep_x1(t):
                sp.wait_ge(x1p_ready, 2 * t + 2)
                src = (v_region[:, 0:D].rearrange("p (a n) -> p a n", a=2) if t == NT - 1
                       else o_w[:, 2 * t:2 * t + 2, 0:512])
                sp.dma_start(x1_rows_v[t].rearrange("p (a n) -> p a n", a=2), src).then_inc(x1_out[t], 16)

            for t in range(NT - 1):
                keep_x1(t)
            sp.wait_ge(wo_full, 2 * NT)
            for t in range(2):
                sp.wait_ge(x1_out[t], 16)
            sp.wait_ge(ax_ready, 2)
            sp.wait_ge(x1t_full, 4)
            sp.dma_start(gate_w[1].rearrange("p c n -> p (c n)"), w_gate_v[1]).then_inc(gate_in[1], 16)
            keep_x1(NT - 1)
            sp.wait_ge(x1_out[2], 16)
            sp.wait_ge(ax_ready, 3)
            sp.wait_ge(x1t_full, 6)
            sp.dma_start(up_w[1].rearrange("p c n -> p (c n)"), w_up_v[1]).then_inc(up_in[1], 16)
            sp.dma_start(ln_gb[:, 0, :], ln2_g.broadcast_to([P, D])).then_inc(ln2_in, 16)
            sp.dma_start(ln_gb[:, 1, :], ln2_b.broadcast_to([P, D])).then_inc(ln2_in, 16)
            sp.wait_ge(rows_in[0], 16)
            sp.wait_ge(gate_low, 4)
            sp.dma_start(gate_w[0].rearrange("p c n -> p (c n)"), w_gate_v[2]).then_inc(gate_in[0], 16)

            sp.sem_inc(y_out, 16)

            def expert(e, i, b, ahead):
                if ahead >= 2:
                    sp.wait_ge(u_low_used, e + 1)
                    sp.dma_start(up_w[b].rearrange("p c n -> p (c n)"),
                                 w_up_v[bass.ds(e + 2, 1)].rearrange("e p n -> p (e n)")).then_inc(up_in[b], 16)
                if ahead >= 3:
                    sp.wait_ge(g_full, e + 2)
                    sp.dma_start(gate_w[1 - b].rearrange("p c n -> p (c n)"),
                                 w_gate_v[bass.ds(e + 3, 1)].rearrange("e p n -> p (e n)"))\
                        .then_inc(gate_in[1 - b], 16)
                if ahead >= 2:
                    sp.wait_ge(y_full, e + 1)
                    sp.dma_start(down_w[b],
                                 w_down_v[bass.ds(e + 2, 1)].rearrange("e p c n -> p (e c) n")).then_inc(down_in[b], 16)
                if ahead >= 1:
                    sp.wait_ge(y_ready, e + 1)
                    sp.dma_start(y_rows[bass.ds(e * CAP, CAP), :], y_sb[0:CAP, :]).then_inc(y_out, 16)

            experts(sp, expert)

            def more(e, j, n):
                sp.wait_ge(m_step["added"], n)
                sp.dma_start(slots, slot_numbers[:, bass.ds(j * CAP, CAP)]).then_inc(m_step["slots"], 16)
                sp.dma_start(gate_w[0].rearrange("p c n -> p (c n)"),
                             w_gate_v[bass.ds(e, 1)].rearrange("e p n -> p (e n)")).then_inc(m_step["weights"], 16)
                sp.dma_start(up_w[0].rearrange("p c n -> p (c n)"),
                             w_up_v[bass.ds(e, 1)].rearrange("e p n -> p (e n)")).then_inc(m_step["weights"], 16)
                sp.dma_start(down_w[0],
                             w_down_v[bass.ds(e, 1)].rearrange("e p c n -> p (e c) n")).then_inc(m_step["weights"], 16)

            peak_rows = load_peak(sp)
            sp.wait_ge(y_out, 16 * E)
            sp.wait_ge(first_added, 3)
            sp.wait_ge(acc_ready, NT - 1)
            sp.sem_inc(m_step["added"], 1)
            more_chunks(sp, peak_rows, more)
            sp.wait_ge(fin_pool, 1)
            sp.dma_start(out_v[0], x_sb[:, 0, :]).then_inc(out_done[0], 16)
            for n, (t, half) in enumerate(((3, 0), (3, 1), (2, 0), (2, 1))):
                cols = slice(half * 512, (half + 1) * 512)
                sp.wait_ge(fin_ready, n + 1)
                sp.dma_start(out_v[t][:, cols], x_sb[:, t, cols]).then_inc(out_done[t], 16)
            for t in range(NT):
                sp.wait_ge(out_done[t], 32 if t >= 2 else 16)

        @block.tensor
        def _(pe):
            def start_unit(n):
                if n >= 2:
                    unit_emptied(pe, n - 2)
                return unit_bank[n % 2]

            pe.wait_ge(ident_in, 16)
            for n in range(NX):
                t, half = n // 2, n % 2
                pe.wait_ge(x_in[t], 16)
                o = start_unit(n)
                for c in range(4):
                    mm = nc.tensor.transpose(o[:, c * P:(c + 1) * P],
                                             x_sb[:, t, (4 * half + c) * P:(4 * half + c + 1) * P], ident)
                mm.then_inc(unit_full, 1)

            unit_emptied(pe, NX - 2)
            unit_emptied(pe, NX - 1)
            pe.wait_ge(wf_high, 1)
            pe.wait_ge(wf_low, 1)
            for t in range(NT):
                for c in range(NC):
                    nc.tensor.matmul(misc_bank[:, 8 * t:8 * t + 8], xT_H[:, t, c, :], wf_parts[:, c, :],
                                     start=(c == 0), stop=False)
                    mm = nc.tensor.matmul(misc_bank[:, 8 * t:8 * t + 4], xT_L[:, t, c, :], wf_parts[:, c, 0:4],
                                          start=False, stop=(c == NC - 1))
            mm.then_inc(fl_full, 1)

            def project(u):
                name, half = u
                n = unit_no(u)
                k = PIECES.index(u)
                o = start_unit(n)
                if name in ("fv", "dv"):
                    k -= half
                    low = in_L[slot_of(k)]
                    pe.wait_ge(in_high, k + 2)
                    pe.wait_ge(in_low, k + 2)
                    for j in range(2):
                        t = 2 * half + j
                        tile = o[:, j * GW:(j + 1) * GW]
                        for c in range(NC):
                            high = in_H(k + c // 4)[:, c % 4, :]
                            nc.tensor.matmul(tile, xT_H[:, t, c, :], high, start=(c == 0), stop=False)
                            nc.tensor.matmul(tile, xT_H[:, t, c, :], low[:, c, :], start=False, stop=False)
                            mm = nc.tensor.matmul(tile, xT_L[:, t, c, :], high, start=False, stop=(c == NC - 1))
                else:
                    tile = o[:, :].rearrange("p (t q) -> p t q", t=NT)
                    pe.wait_ge(in_high, k + 1)
                    for c in range(NC):
                        nc.tensor.matmul(tile, in_H(k)[:, c, :], xT_H[:, :, c, :], start=(c == 0), stop=False)
                        nc.tensor.matmul(tile, in_H(k)[:, c, :], xT_L[:, :, c, :], start=False, stop=False)
                    pe.wait_ge(in_low, k + 1)
                    for c in range(NC):
                        mm = nc.tensor.matmul(tile, piece_of(in_L[slot_of(k)], k)[:, c, :], xT_H[:, :, c, :],
                                              start=False, stop=(c == NC - 1))
                mm.then_inc(unit_full, 1)

            def spread_sums(h):
                if h == 0:
                    pe.wait_ge(cum_act, 2)
                else:
                    pe.wait_ge(cum_act, 2 + h)
                nc.tensor.matmul(misc_bank[:, :], select_head[:, P * h:P * (h + 1)], cT,
                                 start=True, stop=True).then_inc(cum_full, 1)

            for k, u in enumerate(UNITS0):
                project(u)
                if k == 1:
                    pe.wait_ge(ls_ready, 1)
                    pe.wait_ge(consts_in, 16)
                    pe.wait_ge(select_in, 16)
                    for t in range(NT):
                        mm = nc.tensor.matmul(misc_bank[0:4, t * P:S], ls_f[:, 4 * t:4 * t + 4], upper[:, 0:S - t * P],
                                              start=(t == 0), stop=(t == NT - 1))
                    mm.then_inc(cum_full, 1)
                if k == 2:
                    pe.wait_ge(cum_act, 1)
                    for t in range(NT):
                        mm = nc.tensor.transpose(head_bank[:, 4 * t:4 * t + 4], cT[:, t * P:(t + 1) * P],
                                                 ident[0:4, 0:4])
                    mm.then_inc(cum_full, 1)
                if k == 3:
                    spread_sums(0)
                if k == 5:
                    spread_sums(1)

            def scores(h):
                g, hh = h // 4, h % 4
                r = HD * (hh % 2)
                q, k = qkT[r:r + HD, 4 * g + hh // 2, :], qkT[r:r + HD, 4 * g + 2 + hh // 2, :]
                name = "fd"[g]
                unit_emptied(pe, unit_no((name + "q", hh // 2)))
                unit_emptied(pe, unit_no((name + "k", hh // 2)))
                for i in range(NT):
                    s = NT * h + i
                    if s >= 2:
                        pe.wait_ge(peak_ready, s - 1)
                    nc.tensor.matmul(score_bank[s % 2][:, 0:(i + 1) * P], q[:, i * P:(i + 1) * P], k[:, 0:(i + 1) * P],
                                     start=True, stop=True).then_inc(score_full, 1)

            def turn_probs(h):
                for i in range(NT):
                    pe.wait_ge(exp_ready, NT * h + i + 1)
                    if i >= 2:
                        pe.wait_ge(turn_dve, 3 * h + i - 1)
                    elif h:
                        if i == 0:
                            pe.wait_ge(turn_dve, 3 * h)
                        else:
                            pe.wait_ge(turn_act, h)
                    o = turn_bank[i % 2]
                    for j in range(i + 1):
                        mm = nc.tensor.transpose(o[:, j * P:(j + 1) * P],
                                                 probs[h % 2][:, OFF[i] + j * P:OFF[i] + (j + 1) * P], ident)
                    mm.then_inc(turn_full, 1)

            def weigh_values(h):
                g, hh = h // 4, h % 4
                unit_emptied(pe, unit_no(("fd"[g] + "v", 1)))
                pe.wait_ge(turn_dve, 3 * h + 3)
                pe.wait_ge(turn_act, h + 1)
                if h:
                    pe.wait_ge(head_dve, h)
                else:
                    pe.wait_ge(cum_act, 2)
                for i in range(NT):
                    for j in range(i + 1):
                        mm = nc.tensor.matmul(head_bank[:, i * HD:(i + 1) * HD],
                                              probsT[h % 2][:, OFF[i] + j * P:OFF[i] + (j + 1) * P],
                                              v_sb[:, g, j, hh * HD:(hh + 1) * HD], start=(j == 0), stop=(j == i))
                mm.then_inc(head_full, 1)

            def turn_pair(m):
                pe.wait_ge(head_dve, 2 * m + 2)
                if m:
                    pe.wait_ge(pair_act, m)
                else:
                    pe.wait_ge(cum_act, 6)
                for t in range(NT):
                    mm = nc.tensor.transpose(misc_bank[:, t * P:(t + 1) * P], osb[m % 2][:, t, :], ident)
                mm.then_inc(pair_full, 1)

            for h in range(NH):
                scores(h)
                if h:
                    weigh_values(h - 1)
                if h <= 1:
                    spread_sums(h + 2)
                for u in FILL[h]:
                    project(u)
                turn_probs(h)
                if h and h % 2 == 0:
                    turn_pair(h // 2 - 1)
            pe.wait_ge(poolw_in, 64)
            for c in range(2):
                pe.wait_ge(pool_ready, c + 1)
                o = start_unit(unit_no(("pool", c)))
                nc.tensor.matmul(o[:, :], pool_wd[:, c, :], pool_u[c][:, 16:528], start=True,
                                 stop=True).then_inc(unit_full, 1)
            weigh_values(NH - 1)

            def out_high(t, half):
                if half == 0 and t == 0:
                    unit_emptied(pe, unit_no(("pool", 0)))
                    unit_emptied(pe, unit_no(("pool", 1)))
                    unit_emptied(pe, unit_no(("cb", 1)))
                    pe.wait_ge(peak_ready, NT * NH)
                if half == 1:
                    pe.wait_ge(wo_free, t + 1)
                    pe.wait_ge(o_high, 8)
                for k, c in enumerate(MIX_ORDER):
                    if half == 0 and t == 0:
                        if k == 4:
                            turn_pair(3)
                        pe.wait_ge(o_high, c // 2 + 1)
                        pe.wait_ge(mix_high, k + 1)
                        pe.wait_ge(mix_low, k + 1)
                    for part in (mix_H, mix_L):
                        nc.tensor.matmul(bank[t][:, :], part[:, c, t * P:(t + 1) * P], o_H[half][c],
                                         start=(k == 0 and part is mix_H), stop=False)

            def out_low(t, half):
                pe.wait_ge(o_low, 3 + 4 * half)
                pe.wait_ge(o_low_last, 1)
                for c in range(NC):
                    mm = nc.tensor.matmul(bank[t][:, :], mix_H[:, c, t * P:(t + 1) * P],
                                          o_L[:, c, half * 512:(half + 1) * 512], start=False, stop=(c == NC - 1))
                mm.then_inc(wo_full, 1)

            def turn_x1(t):
                for half in range(2):
                    pe.wait_ge(x1p_ready, 2 * t + half + 1)
                    if t:
                        pe.wait_ge(x1t_act, 2 * t - 1 + half)
                    for c in range(4):
                        mm = nc.tensor.transpose(turn_bank[half][:, c * P:(c + 1) * P], x1p(t, half)[:, c, :], ident)
                    mm.then_inc(x1t_full, 1)

            def logits(t):
                for c in range(NC):
                    if c % 4 == 0:
                        pe.wait_ge(x1t_act, 2 * t + c // 4 + 1)
                    mm = nc.tensor.matmul(logit_bank[:, E * t:E * t + E], x1T[:, c, t * P:(t + 1) * P],
                                          router_w[:, c, :], start=(c == 0), stop=(c == NC - 1))
                mm.then_inc(logit_full, 1)

            pe.wait_ge(router_in, 32)
            out_high(0, 0)
            out_high(1, 0)
            out_low(0, 0)
            out_low(1, 0)
            for t in (2, 3):
                out_high(t, 0)
                out_low(t, 0)
            for t in range(NT):
                out_high(t, 1)
                out_low(t, 1)
                if t == 1:
                    turn_x1(0)
                if t == 2:
                    logits(0)
            for t in range(1, NT):
                turn_x1(t)
                logits(t)

            pe.wait_ge(chosen_ready, 1)
            pe.wait_ge(tok_ready, 1)
            for t in range(NT):
                for s in range(t + 1):
                    nc.tensor.matmul(count_bank[:, E * t:E * t + E], (upper_b if s == t else ones_b),
                                     chosen_b[:, E * s:E * s + E], start=(s == 0), stop=(s == t))
            for s in range(NT):
                mm = nc.tensor.matmul(count_bank[:, E * NT:E * NT + E], ones_b, chosen_b[:, E * s:E * s + E],
                                      start=(s == 0), stop=(s == NT - 1))
            mm.then_inc(count_full, 1)

            def token_numbers(o, hot):
                for t in range(NT):
                    for k in (0, 1 + t):
                        mm = nc.tensor.matmul(o, hot[:, t, :], tok_b[:, k:k + 1], start=(t == 0 and k == 0),
                                              stop=(t == NT - 1 and k > 0))
                return mm

            def find_rows(e, b):
                pe.wait_ge(onehot_ready, e + 1)
                pe.wait_ge(idx_ready, e)
                token_numbers(idx_bank[0:CAP, 0:1], onehot[b]).then_inc(idx_full, 1)

            def turn_rows(src):
                for c in range(NC):
                    mm = nc.tensor.transpose(xg_bank[c // 4][:, (c % 4) * CAP:(c % 4 + 1) * CAP],
                                             src[0:CAP, c * P:(c + 1) * P], ident[0:CAP, 0:CAP])
                return mm

            def turn_h():
                for c in range(NF):
                    mm = nc.tensor.transpose(h_bank[:, c * CAP:(c + 1) * CAP], act_g[0:CAP, c * P:(c + 1) * P],
                                             ident[0:CAP, 0:CAP])
                return mm

            def times_high(o, b, w, high_ready, e):
                for c in range(NC):
                    if c % 2 == 0:
                        pe.wait_ge(high_ready, e * 4 + c // 2 + 1)
                    nc.tensor.matmul(o[0:CAP, :], xH[b][:, c, :], w[:, c, :], start=(c == 0), stop=False)
                    nc.tensor.matmul(o[0:CAP, :], xL[b][:, c, :], w[:, c, :], start=False, stop=False)

            def times_low(o, b, w, c, stop=False):
                return nc.tensor.matmul(o[0:CAP, :], xH[b][:, c, :], w, start=False, stop=stop)

            def down_project(b, n, together=False):
                for c in range(NF):
                    pe.wait_ge(down_high, n + c + 1)
                    for part in (hH, hL):
                        for half in range(2):
                            nc.tensor.matmul(y_bank[half][0:CAP, :], part[:, c * CAP:(c + 1) * CAP],
                                             down_H[c][:, half * 512:(half + 1) * 512],
                                             start=(c == 0 and part is hH), stop=False)
                for c in range(NF):
                    pe.wait_ge(down_low, n + (NF if together else c + 1))
                    for half in range(2):
                        mm = nc.tensor.matmul(y_bank[half][0:CAP, :], hH[:, c * CAP:(c + 1) * CAP],
                                              down_L[b][:, c, half * 512:(half + 1) * 512],
                                              start=False, stop=(c == NF - 1))
                return mm

            find_rows(0, 0)
            def stay_awake(n, o=None):
                for _ in range(n):
                    nc.tensor.matmul((turn_bank[0] if o is None else o)[:, 0:P], ident, ident, start=True, stop=True)

            find_rows(1, 1)
            stay_awake(7)
            pe.wait_ge(rows_in[0], 16)
            turn_rows(xg[0]).then_inc(xg_full, 1)
            stay_awake(5)

            def up_low_parts(e, b):
                for c in range(NC):
                    if c == NC - 2:
                        pe.wait_ge(up_low_last, e + 1)
                    elif c % 2 == 0:
                        pe.wait_ge(up_low, e * 3 + c // 2 + 1)
                    mm = nc.tensor.matmul(u_bank[0:CAP, :], xH[b][:, c, :], up_L[b][:, c, :], start=(c == 0),
                                          stop=False)
                mm.then_inc(u_low_used, 1)

            pe.wait_ge(xh_ready, 1)
            up_low_parts(0, 0)
            pe.wait_ge(xl_ready, 1)
            pe.wait_ge(rows_in[1], 16)
            turn_rows(xg[1]).then_inc(xg_full, 1)
            find_rows(2, 0)
            times_high(g_bank, 0, gate_H, gate_high, 0)
            for c in range(NC):
                pe.wait_ge(gate_low, c // 2 + 1)
                mm = times_low(g_bank, 0, first_gate_L[c // 2][:, c % 2, :], c, c == NC - 1)
            mm.then_inc(g_full, 1)
            find_rows(3, 1)

            def turn_hot(src, o):
                for t in range(NT):
                    mm = nc.tensor.transpose(o[0:CAP, t * P:(t + 1) * P], src[:, t, :], ident)
                return mm

            def spread_half(yH, yL, turned, banks, half):
                cols = slice(half * 512, (half + 1) * 512)
                nc.tensor.matmul(bank[banks[half]][:, :], turned, yH[0:CAP, cols], start=True, stop=False)
                return nc.tensor.matmul(bank[banks[half]][:, :], turned, yL[0:CAP, cols], start=False, stop=True)

            def spread_rows(yH, yL, turned, banks):
                spread_half(yH, yL, turned, banks, 0)
                return spread_half(yH, yL, turned, banks, 1)

            def expert(e, i, b, ahead):
                if 1 <= ahead <= 3:
                    pe.wait_ge(rows_in[1 - b], i * 16 + 16 * (b + 1))
                    turn_rows(xg[1 - b]).then_inc(xg_full, 1)
                if ahead <= 3:
                    up_low_parts(e, b)
                for c in range(NC):
                    if c % 2 == 0:
                        pe.wait_ge(up_high, e * 4 + c // 2 + 1)
                    nc.tensor.matmul(u_bank[0:CAP, :], xH[b][:, c, :], up_H[:, c, :], start=False, stop=False)
                    mm = nc.tensor.matmul(u_bank[0:CAP, :], xL[b][:, c, :], up_H[:, c, :], start=False,
                                          stop=(c == NC - 1))
                mm.then_inc(u_full, 1)
                if ahead == 3:
                    find_rows(e + 3, 1 - b)
                if ahead == 0:
                    pe.wait_ge(hot_ready, 1)
                    turn_hot(hot, xg_bank[0]).then_inc(hot_turned, 1)
                    stay_awake(1, xg_bank[1])
                if ahead >= 1:
                    pe.wait_ge(xh_ready, e + 2)
                    pe.wait_ge(xl_ready, e + 2)
                    if ahead == 4:
                        pe.wait_ge(silu_ready, 1)
                    times_high(g_bank, 1 - b, gate_H, gate_high, e + 1)
                pe.wait_ge(h_ready, e + 1)
                turn_h().then_inc(turned_h, 1)
                if ahead == 0:
                    stay_awake(5, xg_bank[1])
                if ahead >= 1:
                    for c in range(NC):
                        if ahead == 4:
                            pe.wait_ge(gate_low, 8)
                        elif c % 2 == 0:
                            pe.wait_ge(gate_low, e * 4 + c // 2 + 5)
                        mm = times_low(g_bank, 1 - b, gate_L[1 - b][:, c, :], c, c == NC - 1)
                    mm.then_inc(g_full, 1)
                pe.wait_ge(hh_ready, e + 1)
                pe.wait_ge(hl_ready, e + 1)
                down_project(b, e * 4, ahead == 4).then_inc(y_full, 1)

            experts(pe, expert)

            def more_up(o, w):
                for m in range(NF):
                    for c in range(NC):
                        mm = nc.tensor.matmul(o[:, m * CAP:(m + 1) * CAP], w[:, c, m * P:(m + 1) * P],
                                              more_xT[:, c, :], start=(c == 0), stop=(c == NC - 1))
                return mm

            def more_down(w):
                for c in range(NF):
                    for half in range(2):
                        mm = nc.tensor.matmul(y_bank[half][0:CAP, :], more_hT[:, c * CAP:(c + 1) * CAP],
                                              w[:, c, half * 512:(half + 1) * 512], start=(c == 0), stop=(c == NF - 1))
                return mm

            def more(e, j, n):
                pe.wait_ge(m_step["onehot"], n)
                token_numbers(idx_bank[0:CAP, 0:1], onehot[0]).then_inc(m_step["idx_full"], 1)
                pe.wait_ge(m_step["rows"], n * 16)
                turn_rows(xg[0]).then_inc(m_step["xg_full"], 1)
                pe.wait_ge(m_step["xg"], n)
                pe.wait_ge(m_step["weights"], n * 48)
                more_up(g_bank, gate_w[0]).then_inc(m_step["g_full"], 1)
                more_up(u_bank, up_w[0]).then_inc(m_step["u_full"], 1)
                pe.wait_ge(m_step["h"], n)
                more_down(down_w[0]).then_inc(m_step["y_full"], 1)
                turn_hot(more_hot, h_bank).then_inc(m_step["turned"], 1)
                pe.wait_ge(m_step["hotT"], n)
                pe.wait_ge(m_step["high"], n)
                pe.wait_ge(m_step["low"], n)
                for t in range(NT):
                    if t >= 2:
                        pe.wait_ge(m_step["read"], n * 4 + t - 5)
                    spread_rows(more_yH, more_yL, more_hotT[0:CAP, t * P:(t + 1) * P], add_banks[t % 2])\
                        .then_inc(m_step["full"], 1)

            peak_rows = load_peak(pe)
            pe.wait_ge(hot_act, 1)
            stay_awake(12, xg_bank[0])
            more_chunks(pe, peak_rows, more, lambda: pe.wait_ge(m_step["added"], ROUNDS + 1),
                        lambda: pe.wait_ge(last_low, 2))
            for half in range(2):
                pe.wait_ge(last_low, half + 1)
                mm = spread_half(last_yH, last_yL, hotT[0:CAP, 0:P], add_banks[0], half)
            mm.then_inc(last_full, 1)
            for t in range(1, NT):
                spread_rows(last_yH, last_yL, hotT[0:CAP, t * P:(t + 1) * P], add_banks[t]).then_inc(last_full, 1)

        @block.vector
        def _(dve):
            steps = [0]

            def done(ins):
                steps[0] += 1
                ins.then_inc(dve_step, 1)
                dve.wait_ge(dve_step, steps[0])

            done(nc.vector.memset(eps, EPS))
            done(nc.vector.memset(ones_b, 1.0))
            for n in range(NX):
                c = slice(4 * (n % 2), 4 * (n % 2) + 4)
                dve.wait_ge(xt_high, n + 1)
                nc.vector.tensor_tensor(xT_L[:, n // 2, c, :], unit_bank[n % 2][:, :].rearrange("p (c q) -> p c q", c=4),
                                        xT_H[:, n // 2, c, :].bitcast(F32), ALU.subtract).then_inc(unit_dve, 1)
            dve.wait_ge(wf_high, 1)
            nc.vector.tensor_tensor(wf_parts[:, :, 4:8], w_f, wf_parts[:, :, 0:4].bitcast(F32),
                                    ALU.subtract).then_inc(wf_low, 1)

            def split_low(k):
                dve.wait_ge(in_high, k + 1)
                nc.vector.tensor_tensor(piece_of(in_L[slot_of(k)], k), piece_of(in_w[slot_of(k)], k),
                                        in_H(k).bitcast(F32), ALU.subtract).then_inc(in_low, 1)

            for k in range(NPIECE):
                split_low(k)
            dve.wait_ge(fl_full, 1)
            z_parts = misc_bank[:, 0:32].rearrange("p (t h) -> p t h", h=8)
            z = z_f.rearrange("p (t h) -> p t h", h=4)
            done(nc.vector.tensor_tensor(z, z_parts[:, :, 0:4], bf_b.unsqueeze(1).broadcast_to([P, NT, 4]), ALU.add))
            done(nc.vector.tensor_tensor(z, z, z_parts[:, :, 4:8], ALU.add))
            nc.vector.scalar_tensor_tensor(out=az_f, in0=z_f, scalar=-1.0, in1=z_f, op0=ALU.mult,
                                           op1=ALU.max).then_inc(az_ready, 1)
            dve.wait_ge(sp_ready, 1)
            nc.vector.scalar_tensor_tensor(out=ls_f, in0=z_f, scalar=0.0, in1=az_f, op0=ALU.min,
                                           op1=ALU.subtract).then_inc(ls_ready, 1)
            dve.wait_ge(consts_in, 16)
            done(nc.vector.tensor_copy(upper_b, upper[:, 0:P]))
            nc.vector.tensor_copy(tok_b[:, 0:1 + NT], cst[:, C_TOK:C_TOK + 1 + NT]).then_inc(tok_ready, 1)

            def empty_values(u):
                name, half = u
                n = unit_no(u)
                dve.wait_ge(unit_full, n + 1)
                nc.vector.tensor_copy(v_sb[:, "fd".index(name[0]), 2 * half:2 * half + 2, :],
                                      unit_bank[n % 2][:, :].rearrange("p (t c) -> p t c", t=2)).then_inc(unit_dve, 1)

            for k in range(NPIECE, 2 * NPIECE):
                split_low(k)
            empty_values(("fv", 0))
            empty_values(("fv", 1))

            def row_peaks(h):
                if h < 4:
                    dve.wait_ge(bias_ready, h + 1)
                else:
                    dve.wait_ge(turn_full, NT * (h - 1))
                for i in range(NT):
                    s = NT * h + i
                    n = (i + 1) * P
                    p = probs[h % 2][:, OFF[i]:OFF[i] + n]
                    dve.wait_ge(score_full, s + 1)
                    nc.vector.tensor_tensor_reduce(out=p, in0=score_bank[s % 2][:, 0:n],
                                                   in1=(p if h < 4 else dil[:, S - n:S]), scale=1.0, scalar=-3.0e38,
                                                   op0=ALU.add, op1=ALU.max,
                                                   accum_out=peak[:, s:s + 1]).then_inc(peak_ready, 1)
                    dve.wait_ge(peak_ready, s + 1)
                    nc.vector.tensor_scalar(npeak[:, s:s + 1], peak[:, s:s + 1], -1.0, None,
                                            ALU.mult).then_inc(npeak_ready, 1)

            def empty_head(h):
                dve.wait_ge(exp_ready, NT * (h + 1))
                done(nc.vector.reciprocal(rtotal[:, NT * h:NT * h + NT], total[:, NT * h:NT * h + NT]))
                dve.wait_ge(head_full, h + 1)
                if h >= 4:
                    dve.wait_ge(pair_full, h // 2 - 1)
                nc.vector.tensor_tensor(osb[(h // 2) % 2][:, :, (h % 2) * HD:(h % 2 + 1) * HD],
                                        head_bank[:, 0:NT * HD].rearrange("p (t n) -> p t n", t=NT),
                                        rtotal[:, NT * h:NT * h + NT].unsqueeze(2).broadcast_to([P, NT, HD]),
                                        ALU.mult).then_inc(head_dve, 1)

            def empty_turned(h):
                for i in range(3):
                    dve.wait_ge(turn_full, NT * h + i + 1)
                    if h >= 2:
                        dve.wait_ge(head_full, h - 1)
                    nc.vector.tensor_copy(probsT[h % 2][:, OFF[i]:OFF[i + 1]],
                                          turn_bank[i % 2][:, 0:(i + 1) * P]).then_inc(turn_dve, 1)

            def convolve(u):
                name, c = u
                n = unit_no(u)
                dve.wait_ge(unit_full, n + 1)
                if name == "ch":
                    if c == 0:
                        dve.wait_ge(pads_ready, 1)
                        dve.wait_ge(chan_in, 16 * 8)
                    dve.wait_ge(unit_act, unit_count(unit_no(("cc", c))))
                    nc.vector.tensor_tensor(conv_u[:, 2:514], unit_bank[n % 2][:, :], conv_c, ALU.mult)\
                        .then_inc(unit_dve, 1)
                    dve.wait_ge(unit_dve, unit_count(n))
                    done(nc.vector.tensor_scalar(conv_c, conv_u[:, 2:514], conv_k[:, c, 2:3], None, ALU.mult))
                    for k in (1, 0):
                        done(nc.vector.scalar_tensor_tensor(out=conv_c, in0=conv_u[:, k:k + S],
                                                            scalar=conv_k[:, c, k:k + 1], in1=conv_c,
                                                            op0=ALU.mult, op1=ALU.add))
                else:
                    nc.vector.tensor_tensor(mixT[:, 4 + c, :], unit_bank[n % 2][:, :], conv_c, ALU.mult)\
                        .then_inc(unit_dve, 1)

            for h in range(NH):
                row_peaks(h)
                if h:
                    empty_head(h - 1)
                for k in range(2 * NPIECE + 2 * h, min(2 * NPIECE + 2 * h + 2, len(PIECES))):
                    split_low(k)
                for u in FILL[h]:
                    if u[0] == "dv":
                        empty_values(u)
                    elif u[0] in ("ch", "cb"):
                        convolve(u)
                if h < NH - 1:
                    empty_turned(h)

            def split_mix(c):
                dve.wait_ge(mix_high, MIX_ORDER.index(c) + 1)
                nc.vector.tensor_tensor(mix_L[:, c, :], mixT[:, c, :], mix_H[:, c, :].bitcast(F32),
                                        ALU.subtract).then_inc(mix_low, 1)

            def split_out(half, k):
                cols = slice(half * 512, (half + 1) * 512)
                dve.wait_ge(o_high, 4 * half + k + 1)
                for c in (2 * k, 2 * k + 1):
                    ins = nc.vector.tensor_tensor(o_L[:, c, cols], o_w[:, c, cols], o_H[half][c].bitcast(F32),
                                                  ALU.subtract)
                ins.then_inc(o_low, 1)

            empty_turned(NH - 1)
            for c in MIX_ORDER[:3]:
                split_mix(c)
            empty_head(NH - 1)
            for c in MIX_ORDER[3:7]:
                split_mix(c)
            dve.wait_ge(mix_high, NC)
            nc.vector.tensor_tensor(mix_L[:, 3, :], misc_bank[:, :], mix_H[:, 3, :].bitcast(F32),
                                    ALU.subtract).then_inc(mix_low, 1)
            for k in range(3):
                split_out(0, k)

            def rsqrt_refined(t):
                r = r0[:, t:t + 1]
                done(nc.vector.tensor_scalar(nwt[:, 0:1], devsq[:, t:t + 1], -0.5 / D, -0.5 * EPS, ALU.mult, ALU.add))
                done(nc.vector.scalar_tensor_tensor(out=nwt[:, 1:2], in0=nwt[:, 0:1], scalar=r, in1=r,
                                                    op0=ALU.mult, op1=ALU.mult))
                done(nc.vector.scalar_tensor_tensor(out=rstd[:, t:t + 1], in0=nwt[:, 1:2], scalar=1.5, in1=r,
                                                    op0=ALU.add, op1=ALU.mult))

            def contraction_order(ap):
                return ap.rearrange("p (q c) -> p c q", c=NC)

            def add_x(t, half):
                cols = slice(half * 512, (half + 1) * 512)
                dve.wait_ge(wo_full, NT * half + t + 1)
                dve.wait_ge(x_in[t], 32)
                nc.vector.scalar_tensor_tensor(out=x_sb[:, t, cols], in0=x_sb[:, t, cols], scalar=ALPHA,
                                               in1=bank[t][:, :], op0=ALU.mult, op1=ALU.add,
                                               accum_out=rowsum[:, 2 * t + half:2 * t + half + 1])\
                    .then_inc(wo_free, 1)

            def first_norm(t):
                dve.wait_ge(wo_free, NT + t + 1)
                nc.vector.tensor_scalar(nmean[:, t:t + 1], rowsum[:, 2 * t:2 * t + 1], rowsum[:, 2 * t + 1:2 * t + 2],
                                        -1.0 / D, ALU.add, ALU.mult).then_inc(mean_ready, 1)
                dve.wait_ge(mean_ready, t + 1)
                if t == 0:
                    dve.wait_ge(ln1_in, 32)
                tmp = centred[t % 2]
                done(nc.vector.scalar_tensor_tensor(out=tmp, in0=x_sb[:, t, :], scalar=nmean[:, t:t + 1],
                                                    in1=ln_gb[:, 0, :], op0=ALU.add, op1=ALU.mult))
                dve.wait_ge(rsq_ready, t + 1)
                rsqrt_refined(t)
                for half in range(2):
                    c = slice(4 * half, 4 * half + 4)
                    nc.vector.scalar_tensor_tensor(out=x1p(t, half), in0=contraction_order(tmp)[:, c, :],
                                                   scalar=rstd[:, t:t + 1],
                                                   in1=contraction_order(ln_gb[:, 1, :])[:, c, :],
                                                   op0=ALU.mult, op1=ALU.add).then_inc(x1p_ready, 1)

            for t in range(NT):
                add_x(t, 0)
                split_out(1, t)
            for t in range(NT):
                add_x(t, 1)
                first_norm(t)

            def ranked(dst, src, groups):
                n = 16 * groups
                a, b = cmp_a[:, 0:n], cmp_b[:, 0:n]
                v = src.rearrange("p (g e) -> p g e", e=4)
                other = v.unsqueeze(2).broadcast_to([P, groups, 4, 4])
                own = v.unsqueeze(3).broadcast_to([P, groups, 4, 4])
                a4 = a.rearrange("p (g e j) -> p g e j", e=4, j=4)
                b4 = b.rearrange("p (g e j) -> p g e j", e=4, j=4)
                low = cst[:, C_LOW:C_LOW + 16].unsqueeze(1).broadcast_to([P, groups, 16])
                done(nc.vector.tensor_tensor(a4, other, own, ALU.is_equal))
                done(nc.vector.tensor_tensor(b4, other, own, ALU.is_gt))
                a3 = a.rearrange("p (g k) -> p g k", k=16)
                done(nc.vector.tensor_tensor(a3, a3, low, ALU.mult))
                done(nc.vector.tensor_tensor(a, a, b, ALU.add))
                done(nc.vector.tensor_reduce(dst, a.rearrange("p (g j) -> p g j", j=4), AX.X, ALU.add))

            def by_group(ap):
                return ap.rearrange("p (g e) -> p g e", e=4)

            dve.wait_ge(esig_ready, 1)
            done(nc.vector.tensor_scalar(tmp64, sg, 1.0, None, ALU.add))
            done(nc.vector.reciprocal(sg, tmp64))
            done(nc.vector.tensor_tensor(sel.rearrange("p (t e) -> p t e", e=E), sg.rearrange("p (t e) -> p t e", e=E),
                                         rbias.unsqueeze(1).broadcast_to([P, NT, E]), ALU.add))
            ranked(rank, sel, 16)
            done(nc.vector.tensor_scalar(inpair, rank, 1.5, None, ALU.is_lt))
            done(nc.vector.tensor_tensor(tmp64, inpair, sel, ALU.mult))
            done(nc.vector.tensor_reduce(gscore, by_group(tmp64), AX.X, ALU.add))
            ranked(grank, gscore, NT)
            done(nc.vector.tensor_scalar(grank, grank, 0.5, None, ALU.is_lt))
            best = grank.unsqueeze(2).broadcast_to([P, 16, 4])
            done(nc.vector.tensor_tensor(by_group(chosen), by_group(inpair), best, ALU.mult))
            nc.vector.tensor_copy(chosen_b, chosen).then_inc(chosen_ready, 1)
            dve.wait_ge(count_full, 1)
            done(nc.vector.tensor_tensor(posm, count_bank[:, 0:64], chosen, ALU.mult))
            done(nc.vector.tensor_scalar(posm, posm, -1.0, None, ALU.add))

            def mark_slots(e, hot):
                return nc.vector.tensor_tensor(
                    hot, slots.unsqueeze(1).broadcast_to([P, NT, CAP]),
                    posm.rearrange("p (t e) -> p t e", e=E)[:, :, bass.ds(e, 1)].broadcast_to([P, NT, CAP]),
                    ALU.is_equal)

            def number_rows(e, b):
                dve.wait_ge(idx_full, e + 1)
                nc.vector.tensor_copy(idx[b][0:CAP, :], idx_bank[0:CAP, 0:1]).then_inc(idx_ready, 1)

            def split_gates(e, b, quarters=range(4)):
                for k in quarters:
                    c = slice(2 * k, 2 * k + 2)
                    dve.wait_ge(gate_high, e * 4 + k + 1)
                    nc.vector.tensor_tensor(gate_L[b][:, c, :], gate_w[b][:, c, :], gate_H[:, c, :].bitcast(F32),
                                            ALU.subtract).then_inc(gate_low, 1)

            def split_ups(e, b):
                for k in range(3):
                    c = slice(2 * k, 2 * k + 2)
                    dve.wait_ge(up_high, e * 4 + k + 1)
                    nc.vector.tensor_tensor(up_L[b][:, c, :], up_w[b][:, c, :], up_H[:, c, :].bitcast(F32),
                                            ALU.subtract).then_inc(up_low, 1)

            def split_rows(e, b):
                dve.wait_ge(xh_ready, e + 1)
                for k in range(2):
                    c = slice(4 * k, 4 * k + 4)
                    ins = nc.vector.tensor_tensor(xL[b][:, c, :], xg_bank[k][:, 0:4 * CAP]
                                                  .rearrange("p (c s) -> p c s", c=4),
                                                  xH[b][:, c, :].bitcast(F32), ALU.subtract)
                ins.then_inc(xl_ready, 1)

            dve.wait_ge(slots_in, 16)
            for b in range(2):
                mark_slots(b, onehot[b]).then_inc(onehot_ready, 1)
            for b in range(2):
                number_rows(b, b)
            done(nc.vector.tensor_reduce(most_f[0:1, :], count_bank[0:1, 64:80], AX.X, ALU.max))
            nc.vector.tensor_copy(most[0:1, :], most_f[0:1, :]).then_inc(most_ready, 1)
            split_ups(0, 0)
            split_rows(0, 0)
            mark_slots(2, onehot[0]).then_inc(onehot_ready, 1)
            split_rows(1, 1)
            by_tile = lambda ap: ap.rearrange("p (t e) -> p t e", e=E)
            parts = [0]

            def then(ins):
                parts[0] += 1
                ins.then_inc(gate_step, 1)
                dve.wait_ge(gate_step, parts[0])

            def weigh_choices():
                then(nc.vector.tensor_scalar(tmp64, rank, 0.5, None, ALU.is_lt))
                then(nc.vector.tensor_tensor(by_group(first), by_group(tmp64), best, ALU.mult))
                then(nc.vector.tensor_tensor(gate_all, sg, chosen, ALU.mult))
                then(nc.vector.tensor_reduce(gsum, by_tile(gate_all), AX.X, ALU.add))
                then(nc.vector.reciprocal(gsum, gsum))
                then(nc.vector.tensor_tensor(by_tile(gate_all), by_tile(gate_all),
                                             gsum.unsqueeze(2).broadcast_to([P, NT, E]), ALU.mult))

            def place_choices():
                then(nc.vector.tensor_scalar(inpair, posm, CAP - 0.5, None, ALU.is_lt))
                then(nc.vector.tensor_tensor(by_tile(inpair), by_tile(inpair),
                                             cst[:, C_ROW + E:C_ROW + 2 * E].unsqueeze(1).broadcast_to([P, NT, E]),
                                             ALU.mult))
                then(nc.vector.tensor_tensor(by_tile(rank), by_tile(posm),
                                             cst[:, C_ROW:C_ROW + E].unsqueeze(1).broadcast_to([P, NT, E]), ALU.add))
                then(nc.vector.tensor_tensor(first, first, inpair, ALU.mult))
                then(nc.vector.tensor_tensor(inpair, inpair, chosen, ALU.mult))

            def find_results():
                for k in range(2):
                    if k == 1:
                        then(nc.vector.tensor_tensor(first, inpair, first, ALU.subtract))
                    then(nc.vector.tensor_tensor(tmp64, gate_all, first, ALU.mult))
                    then(nc.vector.tensor_reduce(gates[:, NT * k:NT * k + NT], by_tile(tmp64), AX.X, ALU.add))
                    then(nc.vector.tensor_tensor(tmp64, rank, first, ALU.mult))
                    then(nc.vector.tensor_reduce(yrow_f[:, NT * k:NT * k + NT], by_tile(tmp64), AX.X, ALU.add))
                nc.vector.tensor_copy(yrow, yrow_f).then_inc(yrow_ready, 1)

            base = steps[0]
            PER = 2

            def silu_up(step, n, g, src):
                nc.vector.tensor_scalar(g, g, 1.0, None, ALU.add).then_inc(step, 1)
                dve.wait_ge(step, n + 1)
                nc.vector.reciprocal(g, g).then_inc(step, 1)
                dve.wait_ge(step, n + 2)
                return nc.vector.tensor_tensor(g, src, g, ALU.mult)

            gates_silu = act_g[0:CAP, :]

            def silu(e):
                dve.wait_ge(eg_ready, e + 1)
                silu_up(dve_step, e * PER + base, gates_silu, g_bank[0:CAP, :]).then_inc(silu_ready, 1)

            number_rows(2, 0)
            mark_slots(3, onehot[1]).then_inc(onehot_ready, 1)
            number_rows(3, 1)
            silu(0)

            def split_down(e, b, c):
                dve.wait_ge(down_high, e * 4 + c + 1)
                nc.vector.tensor_tensor(down_L[b][:, c, :], down_w[b][:, c, :], down_H[c].bitcast(F32),
                                        ALU.subtract).then_inc(down_low, 1)

            def expert(e, i, b, ahead):
                if ahead == 3:
                    dve.wait_ge(idx_full, e + 2)
                    mark_slots(e + 3, onehot[1 - b]).then_inc(onehot_ready, 1)
                if ahead == 2:
                    weigh_choices()
                if 1 <= ahead <= 3:
                    split_rows(e + 1, 1 - b)
                if ahead == 2:
                    place_choices()
                if ahead == 1:
                    mark_slots(e + 1, hot).then_inc(hot_ready, 1)
                    find_results()
                if 1 <= ahead <= 3:
                    split_gates(e + 1, 1 - b)

                if ahead == 0:
                    for c in range(2):
                        split_down(e, b, c)
                dve.wait_ge(u_full, e + 1)
                dve.wait_ge(silu_ready, e + 1)
                nc.vector.tensor_tensor(gates_silu, u_bank[0:CAP, :], gates_silu, ALU.mult).then_inc(h_ready, 1)
                if ahead == 4:
                    split_gates(1, 1, range(2, 4))
                    for c in (2, 3):
                        split_down(e, b, c)
                if ahead == 3:
                    number_rows(e + 3, 1 - b)
                dve.wait_ge(hh_ready, e + 1)
                nc.vector.tensor_tensor(hL[:, :], h_bank[:, 0:NF * CAP], hH[:, :].bitcast(F32), ALU.subtract)\
                    .then_inc(hl_ready, 1)
                if ahead == 0:
                    for c in range(2, NF):
                        split_down(e, b, c)
                if ahead >= 1:
                    split_ups(e + 1, 1 - b)
                    silu(e + 1)

            experts(dve, expert)
            steps[0] = base + PER * E

            def more(e, j, n):
                dve.wait_ge(m_step["slots"], n * 16)
                nc.vector.tensor_copy(more_gate, gate_all.rearrange("p (t e) -> p t e", e=E)[:, :, bass.ds(e, 1)])\
                    .then_inc(m_step["gate"], 1)
                mark_slots(e, more_hot)
                mark_slots(e, onehot[0]).then_inc(m_step["onehot"], 1)
                dve.wait_ge(m_step["idx_full"], n)
                nc.vector.tensor_copy(idx[0][0:CAP, :], idx_bank[0:CAP, 0:1]).then_inc(m_step["idx"], 1)
                dve.wait_ge(m_step["xg_full"], n)
                for k in range(2):
                    ins = nc.vector.tensor_copy(more_xT[:, 4 * k:4 * k + 4, :], xg_bank[k][:, 0:4 * CAP]
                                                .rearrange("p (c s) -> p c s", c=4))
                ins.then_inc(m_step["xg"], 1)
                dve.wait_ge(m_step["eg"], n)
                silu_up(m_step["dve"], n * 3 - 3, more_g, g_bank[:, 0:NF * CAP]).then_inc(m_step["dve"], 1)
                dve.wait_ge(m_step["u_full"], n)
                dve.wait_ge(m_step["dve"], n * 3)
                nc.vector.tensor_tensor(more_hT, u_bank[:, 0:NF * CAP], more_g, ALU.mult).then_inc(m_step["h"], 1)
                dve.wait_ge(m_step["high"], n)
                for k in range(2):
                    cols = slice(512 * k, 512 * k + 512)
                    ins = nc.vector.tensor_tensor(more_yL[0:CAP, cols], y_bank[k][0:CAP, :],
                                                  more_yH[0:CAP, cols].bitcast(F32), ALU.subtract)
                ins.then_inc(m_step["low"], 1)
                dve.wait_ge(m_step["gate"], n)
                for t in range(NT):
                    dve.wait_ge(m_step["full"], n * 4 + t - 3)
                    for half in range(2):
                        cols = slice(512 * half, 512 * half + 512)
                        ins = nc.vector.scalar_tensor_tensor(out=x_sb[:, t, cols], in0=bank[add_banks[t % 2][half]][:, :],
                                                             scalar=more_gate[:, t:t + 1], in1=x_sb[:, t, cols],
                                                             op0=ALU.mult, op1=ALU.add)
                    ins.then_inc(m_step["read"], 1)
                dve.wait_ge(m_step["read"], n * 4)
                done_round = nc.vector.tensor_copy(more_gate, more_gate)
                done_round.then_inc(m_step["added"], 1)

            dve.wait_ge(ax_ready, NT - 1)
            dve.wait_ge(ax_last, 1)
            def add_choice(t, k):
                ins = nc.vector.scalar_tensor_tensor(out=x_sb[:, t, :], in0=(ya[t], yb[t])[k],
                                                     scalar=gates[:, NT * k + t:NT * k + t + 1],
                                                     in1=x_sb[:, t, :], op0=ALU.mult, op1=ALU.add)
                if k == 0:
                    done(ins)
                else:
                    ins.then_inc(acc_ready, 1)
                    dve.wait_ge(acc_ready, t + 1)

            peak_rows = load_peak(dve)
            for t in range(2):
                dve.wait_ge(y_in[t], 32)
                add_choice(t, 0)
                add_choice(t, 1)
            for k in range(2):
                cols = slice(512 * k, 512 * k + 512)
                dve.wait_ge(last_high, k + 1)
                nc.vector.tensor_tensor(last_yL[0:CAP, cols], y_bank[k][0:CAP, :],
                                        last_yH[0:CAP, cols].bitcast(F32), ALU.subtract).then_inc(last_low, 1)

            def add_second(t):
                dve.wait_ge(first_added, t - 1)
                add_choice(t, 1)

            def add_last(t):
                dve.wait_ge(last_full, t + 1)
                for half in range(2):
                    cols = slice(512 * half, 512 * half + 512)
                    done(nc.vector.scalar_tensor_tensor(out=x_sb[:, t, cols], in0=bank[add_banks[t][half]][:, :],
                                                        scalar=gate_all[:, E * t + E - 1:E * t + E],
                                                        in1=x_sb[:, t, cols], op0=ALU.mult, op1=ALU.add,
                                                        accum_out=rowsum[:, 2 * t + half:2 * t + half + 1]))
                nc.vector.tensor_scalar(nmean[:, t:t + 1], rowsum[:, 2 * t:2 * t + 1], rowsum[:, 2 * t + 1:2 * t + 2],
                                        -1.0 / D, ALU.add, ALU.mult).then_inc(mean_ready, 1)

            def shift(t):
                dve.wait_ge(rsq_ready, NT + t + 1)
                rsqrt_refined(t)
                nc.vector.tensor_tensor(nmr[:, t:t + 1], nmean[:, t:t + 1], rstd[:, t:t + 1],
                                        ALU.mult).then_inc(fin_shift, 1)

            before_last = steps[0]

            def no_more():
                add_last(0)
                add_last(1)
                shift(0)
                add_second(2)
                add_last(2)
                shift(1)
                dve.wait_ge(first_added, 3)
                add_last(3)

            def before_more():
                steps[0] = before_last
                add_second(2)
                dve.wait_ge(first_added, 3)

            def after_more():
                add_last(0)
                add_last(1)
                shift(0)
                add_last(2)
                shift(1)
                add_last(3)

            more_chunks(dve, peak_rows, more, after_more, before_more, no_more)

            def scale_g(t):
                dve.wait_ge(mean_ready, NT + t + 1)
                dve.wait_ge(rsq_ready, NT + t + 1)
                nc.vector.scalar_tensor_tensor(out=x_sb[:, t, :], in0=x_sb[:, t, :], scalar=nmean[:, t:t + 1],
                                               in1=ln_gb[:, 0, :], op0=ALU.add, op1=ALU.mult).then_inc(scaled_g, 1)

            def scale_rstd(t, cols):
                nc.vector.scalar_tensor_tensor(out=x_sb[:, t, cols], in0=x_sb[:, t, cols], scalar=rstd[:, t:t + 1],
                                               in1=ln_gb[:, 1, cols], op0=ALU.mult, op1=ALU.add).then_inc(fin_ready, 1)

            dve.wait_ge(ln2_in, 32)
            scale_g(2)
            rsqrt_refined(2)
            scale_g(3)
            rsqrt_refined(3)
            dve.wait_ge(scaled_g, 2)
            scale_rstd(3, slice(0, 512))
            scale_rstd(3, slice(512, D))
            scale_rstd(2, slice(0, 512))
            scale_rstd(2, slice(512, D))

        @block.scalar
        def _(act):
            nc.scalar.preload_act_table_set("natural_log_exp_and_others")
            steps = [0]

            def done(ins):
                steps[0] += 1
                ins.then_inc(act_step, 1)
                act.wait_ge(act_step, steps[0])

            for n in range(NX):
                act.wait_ge(unit_full, n + 1)
                nc.scalar.copy(xT_H[:, n // 2, 4 * (n % 2):4 * (n % 2) + 4, :],
                               unit_bank[n % 2][:, :].rearrange("p (c q) -> p c q", c=4)).then_inc(xt_high, 1)
            act.wait_ge(wf_in, 32)
            nc.scalar.copy(wf_parts[:, :, 0:4], w_f).then_inc(wf_high, 1)

            def split_high(k):
                b = BLOCKS.index(PIECES[k][0])
                act.wait_ge(block_in[b % NSLOT], 16 * (b // NSLOT + 1))
                if k >= NPIECE:
                    act.wait_ge(unit_full, last_unit_of(k - NPIECE) + 1)
                nc.scalar.copy(in_H(k), piece_of(in_w[slot_of(k)], k)).then_inc(in_high, 1)

            for k in range(NPIECE):
                split_high(k)
            act.wait_ge(az_ready, 1)
            done(nc.scalar.activation(az_f, az_f, ACT.Exp, scale=-1.0))
            nc.scalar.activation(az_f, az_f, ACT.Ln, bias=1.0).then_inc(sp_ready, 1)

            def empty_unit(u):
                name, half = u
                n = unit_no(u)
                src = unit_bank[n % 2][:, :]
                act.wait_ge(unit_full, n + 1)
                if name in ("fq", "dq"):
                    ins = nc.scalar.mul(qkT[:, 4 * "fd".index(name[0]) + half, :], src, HD ** -0.5)
                elif name in ("fk", "dk"):
                    ins = nc.scalar.copy(qkT[:, 4 * "fd".index(name[0]) + 2 + half, :], src)
                elif name == "cc":
                    if half:
                        unit_emptied(act, unit_no(("cb", 0)))
                    ins = nc.scalar.copy(conv_c, src)
                elif name == "pu":
                    act.wait_ge(pads_ready, 1)
                    ins = nc.scalar.copy(pool_u[half][:, 16:528], src)
                else:
                    act.wait_ge(chan_in, 16 * 8)
                    ins = nc.scalar.mul(mixT[:, 6 + half, :], src, pool_s[:, half:half + 1])
                ins.then_inc(unit_act, 1)

            def empty_sums(k):
                act.wait_ge(cum_full, k + 1)
                if k == 0:
                    ins = nc.scalar.copy(cT, misc_bank[0:4, :])
                elif k == 1:
                    ins = nc.scalar.copy(c_col, head_bank[:, 0:16])
                else:
                    h = k - 2
                    if h >= 2:
                        act.wait_ge(bias_ready, h - 1)
                    ins = nc.scalar.mul(cbc[h % 2], misc_bank[:, :], -1.0)
                ins.then_inc(cum_act, 1)

            for k, u in enumerate(UNITS0):
                if unit_engine(unit_no(u)) == "act":
                    empty_unit(u)
                if k < NPIECE:
                    split_high(NPIECE + k)
                if k == 1:
                    empty_sums(0)
                if k == 2:
                    empty_sums(1)
                if k == 3:
                    empty_sums(2)
                if k == 5:
                    empty_sums(3)
            def split_mix(c):
                if c in (4, 5):
                    unit_emptied(act, unit_no(("cb", c - 4)))
                act.wait_ge(pair_act, 3)
                nc.scalar.copy(mix_H[:, c, :], mixT[:, c, :]).then_inc(mix_high, 1)

            def split_out(half, k):
                for c in (2 * k, 2 * k + 1):
                    ins = nc.scalar.copy(o_H[half][c], o_w[:, c, half * 512:(half + 1) * 512])
                ins.then_inc(o_high, 1)

            for h in range(NH):
                for i in range(NT):
                    s = NT * h + i
                    n = (i + 1) * P
                    p = probs[h % 2][:, OFF[i]:OFF[i] + n]
                    act.wait_ge(npeak_ready, s + 1)
                    nc.scalar.activation(p, p, ACT.Exp, bias=npeak[:, s:s + 1],
                                         accum_out=total[:, s:s + 1]).then_inc(exp_ready, 1)
                if h <= 1:
                    empty_sums(4 + h)
                for k in range(2 * NPIECE + 2 * h, min(2 * NPIECE + 2 * h + 2, len(PIECES))):
                    split_high(k)
                for u in FILL[h]:
                    if unit_engine(unit_no(u)) == "act":
                        empty_unit(u)
                if h == NH - 1:
                    split_mix(0)
                    split_mix(1)
                    act.wait_ge(wo_in, 16)
                    act.wait_ge(unit_full, last_unit_of(len(PIECES) - 1) + 1)
                    split_out(0, 0)
                act.wait_ge(turn_full, NT * (h + 1))
                if h >= 2:
                    act.wait_ge(head_full, h - 1)
                nc.scalar.copy(probsT[h % 2][:, OFF[3]:OFF[3] + NT * P], turn_bank[1][:, :]).then_inc(turn_act, 1)
                if h and h % 2 == 0:
                    m = h // 2 - 1
                    act.wait_ge(pair_full, m + 1)
                    nc.scalar.copy(mixT[:, m, :], misc_bank[:, :]).then_inc(pair_act, 1)
            empty_unit(("pool", 0))
            empty_unit(("pool", 1))
            split_out(0, 1)
            for k, c in enumerate((2, 4, 5, 6, 7)):
                if c == 5:
                    split_out(0, 2)
                if c == 6:
                    act.wait_ge(unit_act, unit_count(unit_no(("pool", 1))))
                    split_out(0, 3)
                split_mix(c)
            act.wait_ge(pair_full, 4)
            nc.scalar.copy(mix_H[:, 3, :], misc_bank[:, :]).then_inc(mix_high, 1)
            for k in range(NT):
                split_out(1, k)

            def rsqrt(t, src, junk, signal):
                done(nc.scalar.activation(junk, src, ACT.Square, bias=nmean[:, t:t + 1],
                                          accum_out=devsq[:, t:t + 1]))
                done(nc.scalar.activation(lnv[:, t:t + 1], devsq[:, t:t + 1], ACT.Ln, bias=eps, scale=1.0 / D))
                nc.scalar.activation(r0[:, t:t + 1], lnv[:, t:t + 1], ACT.Exp, scale=-0.5).then_inc(signal, 1)

            def empty_x1(t):
                for half in range(2):
                    act.wait_ge(x1t_full, 2 * t + half + 1)
                    nc.scalar.copy(x1T[:, 4 * half:4 * half + 4, t * P:(t + 1) * P],
                                   turn_bank[half][:, :].rearrange("p (c q) -> p c q", c=4)).then_inc(x1t_act, 1)

            def split_quarters(e, loaded, count, w, high, high_ready, quarters=range(4)):
                act.wait_ge(loaded, count)
                for k in quarters:
                    c = slice(2 * k, 2 * k + 2)
                    nc.scalar.copy(high[:, c, :], w[:, c, :]).then_inc(high_ready, 1)

            for t in range(NT):
                act.wait_ge(mean_ready, t + 1)
                rsqrt(t, x_sb[:, t, :], squares, rsq_ready)
                if t:
                    empty_x1(t - 1)
                if t == NT - 1:
                    act.wait_ge(wo_full, 2 * NT)
                    split_quarters(0, gate_in[0], 16, gate_w[0], gate_H, gate_high, range(0, 2))
            empty_x1(NT - 1)
            for half in range(2):
                ins = nc.scalar.mul(x_sb[:, NT - 1, :].rearrange("p (q c) -> p c q", c=NC)[:, 4 * half:4 * half + 4, :],
                                    x1p(NT - 1, half), ALPHA)
            ins.then_inc(ax_last, 1)
            act.wait_ge(logit_full, NT)
            nc.scalar.activation(sg, logit_bank[:, 0:64], ACT.Exp, scale=-1.0).then_inc(esig_ready, 1)
            split_quarters(0, gate_in[0], 16, gate_w[0], gate_H, gate_high, range(2, 4))

            def split_rows(e, b):
                act.wait_ge(xg_full, e + 1)
                for k in range(2):
                    ins = nc.scalar.copy(xH[b][:, 4 * k:4 * k + 4, :], xg_bank[k][:, 0:4 * CAP]
                                         .rearrange("p (c s) -> p c s", c=4))
                ins.then_inc(xh_ready, 1)

            def exp_gates(e):
                act.wait_ge(g_full, e + 1)
                nc.scalar.activation(act_g[0:CAP, :], g_bank[0:CAP, :], ACT.Exp, scale=-1.0).then_inc(eg_ready, 1)

            split_quarters(0, up_in[0], 16, up_w[0], up_H, up_high)
            split_rows(0, 0)
            split_rows(1, 1)
            exp_gates(0)

            def expert(e, i, b, ahead):
                if 1 <= ahead <= 3:
                    split_rows(e + 1, 1 - b)
                if ahead >= 1:
                    split_quarters(e + 1, gate_in[1 - b], i * 16 + 16 * (b + 1), gate_w[1 - b], gate_H, gate_high)
                act.wait_ge(down_in[b], i * 16 + 16)
                for c in range(NF):
                    nc.scalar.copy(down_H[c], down_w[b][:, c, :]).then_inc(down_high, 1)
                if ahead == 0:
                    act.wait_ge(hot_turned, 1)
                    nc.scalar.copy(hotT[0:CAP, :], xg_bank[0][0:CAP, :]).then_inc(hot_act, 1)
                act.wait_ge(turned_h, e + 1)
                nc.scalar.copy(hH[:, :], h_bank[:, 0:NF * CAP]).then_inc(hh_ready, 1)
                if ahead >= 1:
                    split_quarters(e + 1, up_in[1 - b], i * 16 + 16 * (b + 1), up_w[1 - b], up_H, up_high)
                    exp_gates(e + 1)
                act.wait_ge(y_full, e + 1)
                act.wait_ge(y_out, e * 16 + 16)
                for half in range(2):
                    ins = nc.scalar.copy((y_sb if ahead else last_yH)[0:CAP, half * 512:(half + 1) * 512],
                                         y_bank[half][0:CAP, :])
                    if ahead == 0:
                        ins.then_inc(last_high, 1)
                if ahead >= 1:
                    ins.then_inc(y_ready, 1)

            experts(act, expert)

            def more(e, j, n):
                act.wait_ge(m_step["g_full"], n)
                nc.scalar.activation(more_g, g_bank[:, 0:NF * CAP], ACT.Exp, scale=-1.0).then_inc(m_step["eg"], 1)
                act.wait_ge(m_step["y_full"], n)
                for k in range(2):
                    ins = nc.scalar.copy(more_yH[0:CAP, 512 * k:512 * k + 512], y_bank[k][0:CAP, :])
                ins.then_inc(m_step["high"], 1)
                act.wait_ge(m_step["turned"], n)
                nc.scalar.copy(more_hotT[0:CAP, :], h_bank[0:CAP, :]).then_inc(m_step["hotT"], 1)

            peak_rows = load_peak(act)
            for t in (2, 3):
                act.wait_ge(y_in[t], 32)
                act.wait_ge(yrow_ready, 1)
                nc.scalar.mul(ya[t], ya[t], gates[:, t:t + 1]).then_inc(first_scaled, 1)

            def spread(t):
                act.wait_ge(mean_ready, NT + t + 1)
                rsqrt(t, x_sb[:, t, :], fin_squares, rsq_ready)

            def scale_second():
                nc.scalar.mul(yb[3], yb[3], gates[:, NT + 3:NT + 4]).then_inc(first_scaled, 1)

            before_spread = steps[0]

            def no_more():
                spread(0)
                scale_second()

            def before_more():
                steps[0] = before_spread
                scale_second()

            more_chunks(act, peak_rows, more, lambda: spread(0), before_more, no_more)

            def normalised(t):
                act.wait_ge(fin_shift, t + 1)
                nc.scalar.activation(x_sb[:, t, :], x_sb[:, t, :], ACT.Identity, scale=rstd[:, t:t + 1],
                                     bias=nmr[:, t:t + 1]).then_inc(fin_norm, 1)

            normalised(0)
            spread(1)
            spread(2)
            normalised(1)
            spread(3)
            act.wait_ge(fin_pool, 2)
            nc.scalar.dma_start(out_v[1], x_sb[:, 1, :]).then_inc(out_done[1], 16)

        @block.gpsimd
        def _(pool):
            steps = [0]

            def done(ins):
                steps[0] += 1
                ins.then_inc(pool_step, 1)
                pool.wait_ge(pool_step, steps[0])

            done(nc.gpsimd.memset(pool_wd, 0.0))
            done(nc.gpsimd.memset(conv_u[:, 0:2], 0.0))
            for c in range(2):
                done(nc.gpsimd.memset(pool_u[c][:, 0:16], 0.0))
            done(nc.gpsimd.memset(pool_a[:, 0:16], 0.0))
            nc.gpsimd.memset(pool_b[:, 0:16], 0.0).then_inc(pads_ready, 1)
            pool.wait_ge(consts_in, 16)
            for h in range(4):
                pool.wait_ge(cum_act, 3 + h)
                if h >= 2:
                    pool.wait_ge(turn_full, NT * (h - 1))
                for i in range(NT):
                    p = probs[h % 2][:, OFF[i]:OFF[i] + (i + 1) * P]
                    done(nc.gpsimd.tensor_scalar(p, cbc[h % 2][:, 0:(i + 1) * P], c_col[:, 4 * i + h:4 * i + h + 1],
                                                 None, ALU.add))
                    ins = nc.gpsimd.tensor_tensor(p[:, i * P:(i + 1) * P], p[:, i * P:(i + 1) * P], tri, ALU.add)
                    if i < NT - 1:
                        done(ins)
                ins.then_inc(bias_ready, 1)

            def doubled(dst, src, w, rows=slice(0, P)):
                done(nc.gpsimd.tensor_tensor(dst[rows, 16:528], src[rows, 16:528], src[rows, 16 - w:528 - w], ALU.add))

            rc = cst[:, C_POOL:C_POOL + 32].rearrange("p (c k) -> p c k", c=2)
            low, high = slice(0, 64), slice(64, P)
            for c in range(2):
                pool.wait_ge(unit_act, unit_count(unit_no(("pu", c))))
                doubled(pool_a, pool_u[c], 1)
                if c == 0:
                    doubled(pool_b, pool_a, 2, high)
                else:
                    doubled(pool_b, pool_a, 2)
                    doubled(pool_a, pool_b, 4)
                    doubled(pool_b, pool_a, 8, high)
                for rows, sums in ((low, pool_a), (high, pool_b)):
                    done(nc.gpsimd.tensor_tensor(sums[rows, 16:32], sums[rows, 16:32], rc[rows, c, :], ALU.mult))
                    done(nc.gpsimd.tensor_scalar(sums[rows, 32:528], sums[rows, 32:528],
                                                 cst[rows, C_POOL + 32 + c:C_POOL + 33 + c], None, ALU.mult))
                    ins = nc.gpsimd.tensor_tensor(pool_u[c][rows, 16:528], sums[rows, 16:528],
                                                  pool_u[c][rows, 16:528], ALU.subtract)
                    if rows is low:
                        done(ins)
                ins.then_inc(pool_ready, 1)
                pool.wait_ge(pool_ready, c + 1)

            def wait_apart(signal, value):
                pool.wait_ge(signal, value)
                pool.sem_inc(gathers_begun, 1)

            def gather(dst, rows, numbers, signal):
                nc.gpsimd.indirect_dma_start(dst, None, rows, bass.IndirectOffsetOnAxis(ap=numbers, axis=0))\
                    .then_inc(signal, 16)

            pool.wait_ge(o_high, 4)
            for c in (6, 7):
                ins = nc.gpsimd.tensor_tensor(o_L[:, c, 0:512], o_w[:, c, 0:512], o_H[0][c].bitcast(F32), ALU.subtract)
            ins.then_inc(o_low_last, 1)
            for t in range(NT - 1):
                pool.wait_ge(x1p_ready, 2 * t + 2)
                for half in range(2):
                    ins = nc.gpsimd.tensor_scalar(x_sb[:, t, :].rearrange("p (q c) -> p c q", c=NC)
                                                  [:, 4 * half:4 * half + 4, :], x1p(t, half), ALPHA, None, ALU.mult)
                ins.then_inc(ax_ready, 1)
            pool.wait_ge(wo_full, 2 * NT)
            for k in range(4):
                pool.wait_ge(gate_high, k + 1)
                c = slice(2 * k, 2 * k + 2)
                nc.gpsimd.tensor_tensor(first_gate_L[k], gate_w[0][:, c, :], gate_H[:, c, :].bitcast(F32),
                                        ALU.subtract).then_inc(gate_low, 1)
            for t in range(NT):
                pool.wait_ge(x1_out[t], 16)
            for b in range(2):
                pool.wait_ge(idx_ready, b + 1)
                gather(xg[b][0:CAP, :], x1_rows, idx[b][0:CAP, :], rows_in[b])
            def split_last_ups(e, b):
                c = slice(NC - 2, NC)
                pool.wait_ge(up_high, e * 4 + 4)
                nc.gpsimd.tensor_tensor(up_L[b][:, c, :], up_w[b][:, c, :], up_H[:, c, :].bitcast(F32),
                                        ALU.subtract).then_inc(up_low_last, 1)

            split_last_ups(0, 0)
            pool.wait_ge(idx_ready, 3)
            pool.wait_ge(xg_full, 1)
            gather(xg[0][0:CAP, :], x1_rows, idx[0][0:CAP, :], rows_in[0])
            pool.wait_ge(idx_ready, 4)
            pool.wait_ge(xg_full, 2)
            gather(xg[1][0:CAP, :], x1_rows, idx[1][0:CAP, :], rows_in[1])
            for k in range(2):
                c = slice(2 * k, 2 * k + 2)
                pool.wait_ge(gate_high, 5 + k)
                nc.gpsimd.tensor_tensor(gate_L[1][:, c, :], gate_w[1][:, c, :], gate_H[:, c, :].bitcast(F32),
                                        ALU.subtract).then_inc(gate_low, 1)

            def expert(e, i, b, ahead):
                if ahead == 0:
                    return
                for c in range(2 if ahead == 4 else NF):
                    if c == 2 and ahead == 3:
                        wait_apart(idx_ready, e + 4)
                        wait_apart(xg_full, e + 2)
                        gather(xg[1 - b][0:CAP, :], x1_rows, idx[1 - b][0:CAP, :], rows_in[1 - b])
                    pool.wait_ge(down_high, e * 4 + c + 1)
                    nc.gpsimd.tensor_tensor(down_L[b][:, c, :], down_w[b][:, c, :], down_H[c].bitcast(F32),
                                            ALU.subtract).then_inc(down_low, 1)
                split_last_ups(e + 1, 1 - b)

            experts(pool, expert)

            pool.wait_ge(y_out, 16 * E)
            pool.wait_ge(yrow_ready, 1)
            for t in range(NT):
                gather(ya[t], y_rows, yrow[:, t:t + 1], y_in[t])
                gather(yb[t], y_rows, yrow[:, NT + t:NT + t + 1], y_in[t])

            def more(e, j, n):
                wait_apart(m_step["idx"], n)
                gather(xg[0][0:CAP, :], x1_rows, idx[0][0:CAP, :], m_step["rows"])

            peak_rows = load_peak(pool)
            for t in (2, 3):
                pool.wait_ge(first_scaled, t - 1)
                nc.gpsimd.tensor_tensor(x_sb[:, t, :], x_sb[:, t, :], ya[t], ALU.add).then_inc(first_added, 1)
            pool.wait_ge(first_scaled, 3)
            pool.wait_ge(first_added, 2)
            nc.gpsimd.tensor_tensor(x_sb[:, 3, :], x_sb[:, 3, :], yb[3], ALU.add).then_inc(first_added, 1)
            more_chunks(pool, peak_rows, more)
            pool.wait_ge(ln2_in, 32)
            for t in range(2):
                pool.wait_ge(fin_norm, t + 1)
                done(nc.gpsimd.tensor_tensor(x_sb[:, t, :], x_sb[:, t, :], ln_gb[:, 0, :], ALU.mult))
                nc.gpsimd.tensor_tensor(x_sb[:, t, :], x_sb[:, t, :], ln_gb[:, 1, :], ALU.add).then_inc(fin_pool, 1)


_INS = ["x", "w_in", "b_f", "conv_w", "pool_w", "pool_scale", "w_o", "ln1_g", "ln1_b", "w_router", "router_bias",
        "w_gate", "w_up", "w_down", "ln2_g", "ln2_b"]


def kernel(**inputs):
    import numpy as _np
    import concourse.bacc as _bacc
    from concourse import mybir as _mybir
    from concourse.bass_utils import run_bass_kernel_spmd as _run

    nc = _bacc.Bacc("TRN2", target_bir_lowering=False, num_devices=1)
    arrays, args = {}, []
    given = [(n, _np.ascontiguousarray(inputs[n])) for n in _INS]
    given += list(zip(["consts", "selectors", "slot_numbers"], constants()))
    for name, a in given:
        arrays[f"in_{name}_dram"] = a
        args.append(nc.dram_tensor(f"in_{name}_dram", a.shape, _mybir.dt.from_np(a.dtype), kind="ExternalInput").ap())
    out = nc.dram_tensor("out_0_dram", (1, S, D), F32, kind="ExternalOutput").ap()
    build(nc, *args, out)
    r = _run(nc, [arrays], core_ids=[0])
    return r.results[0]["out_0_dram"]
```
